# Optimizing a Trainium2 kernel written in Bass

```python
import math
import jax, jax.numpy as jnp
from jax import lax
import numpy as np

D_MODEL = 1024
BATCH = 1
SEQ = 512
DEPTH = 2

DIFF_HEADS = 4
DIFF_DH = 64
DIFF_DV = 2 * DIFF_DH
DIFF_QK = DIFF_HEADS * 2 * DIFF_DH
DIFF_WIDTH = DIFF_HEADS * DIFF_DV
ROPE_THETA = 500000.0
ROPE_DIMS = DIFF_DH // 4
Q_BLOCK = 128
CONV_CH = D_MODEL - DIFF_WIDTH
CONV_WIDTH = 3
RET_HEADS = 4
RET_DK = D_MODEL // RET_HEADS
RET_DV = 2 * RET_DK
RET_QK = RET_HEADS * RET_DK
RET_VW = RET_HEADS * RET_DV
RET_CHUNK = 128
RET_ROPE_THETA = 10000.0
D_FF = ((8 * D_MODEL // 3 + 127) // 128) * 128

EVEN_IN = 2 * DIFF_QK + DIFF_WIDTH + 3 * CONV_CH
ODD_IN = 2 * RET_QK + 2 * RET_VW
N_EVEN = (DEPTH + 1) // 2
N_ODD = DEPTH // 2
DEEPNORM_ALPHA = (2.0 * DEPTH) ** 0.25
DEEPNORM_BETA = (8.0 * DEPTH) ** -0.25
LN_EPS = 1e-5
NEG_INF = -1e30

kernel_name = "hybrid_diffattn_shortconv_retention_macaron"

def layer_norm(x, g, b):
    xf = x.astype(jnp.float32)
    mu = jnp.mean(xf, -1, keepdims=True)
    var = jnp.mean(jnp.square(xf - mu), -1, keepdims=True)
    return ((xf - mu) * lax.rsqrt(var + LN_EPS)).astype(x.dtype) * g + b

def rms_norm(x, g):
    xf = x.astype(jnp.float32)
    y = xf * lax.rsqrt(jnp.mean(jnp.square(xf), -1, keepdims=True) + LN_EPS)
    return y.astype(x.dtype) * g

def rotary(x, n_rot, theta):
    s = x.shape[1]
    half = n_rot // 2
    inv = jnp.exp(-math.log(theta) * jnp.arange(half, dtype=jnp.float32) * (2.0 / n_rot))
    ang = jnp.arange(s, dtype=jnp.float32)[:, None] * inv[None, :]
    cos = jnp.cos(ang)[None, :, None, :].astype(x.dtype)
    sin = jnp.sin(ang)[None, :, None, :].astype(x.dtype)
    x1, x2, xp = x[..., :half], x[..., half:n_rot], x[..., n_rot:]
    return jnp.concatenate([x1 * cos - x2 * sin, x2 * cos + x1 * sin, xp], -1)

def swiglu_ffn(x, w_in, w_out):
    gate, up = jnp.split(x @ w_in, 2, axis=-1)
    return (jax.nn.silu(gate) * up) @ w_out

def diff_attention(q, k, v, lam):
    b, s, h2, d = q.shape
    h = h2 // 2
    nblk = s // Q_BLOCK
    scale = d ** -0.5
    qb = q.reshape(b, nblk, Q_BLOCK, h2, d).transpose(1, 0, 3, 2, 4)
    kt = k.transpose(0, 2, 1, 3)
    vt = v.transpose(0, 2, 1, 3)
    kpos = jnp.arange(s)
    starts = jnp.arange(nblk) * Q_BLOCK

    def one_block(args):
        qblk, start = args
        sc = jnp.einsum('bhqd,bhkd->bhqk', qblk, kt).astype(jnp.float32) * scale
        qpos = start + jnp.arange(Q_BLOCK)
        sc = jnp.where(kpos[None, :] <= qpos[:, None], sc, NEG_INF)
        p = jax.nn.softmax(sc, axis=-1).reshape(b, h, 2, Q_BLOCK, s)
        a = p[:, :, 0] - lam * p[:, :, 1]
        return jnp.einsum('bhqk,bhkv->bhqv', a.astype(vt.dtype), vt)

    out = lax.map(one_block, (qb, starts))
    return out.transpose(1, 0, 3, 2, 4).reshape(b, s, h, v.shape[-1])

def short_gated_conv(gate_b, gate_c, hx, w):
    u = gate_c * hx
    y = lax.conv_general_dilated(
        u, w[:, None, :].astype(u.dtype), window_strides=(1,),
        padding=[(CONV_WIDTH - 1, 0)], dimension_numbers=('NWC', 'WIO', 'NWC'),
        feature_group_count=u.shape[-1])
    return gate_b * y

def even_mixer(x, w_in, w_out, lam_vecs, norm_g, conv_w, layer_idx):
    b, s, _ = x.shape
    hcat = x @ w_in
    o1 = DIFF_QK
    o2 = 2 * DIFF_QK
    o3 = o2 + DIFF_WIDTH
    o4 = o3 + CONV_CH
    o5 = o4 + CONV_CH
    q, k, v, cb, cc, cx = jnp.split(hcat, [o1, o2, o3, o4, o5], axis=-1)
    q = rotary(q.reshape(b, s, 2 * DIFF_HEADS, DIFF_DH), ROPE_DIMS, ROPE_THETA)
    k = rotary(k.reshape(b, s, 2 * DIFF_HEADS, DIFF_DH), ROPE_DIMS, ROPE_THETA)
    v = v.reshape(b, s, DIFF_HEADS, DIFF_DV)
    lambda_init = 0.8 - 0.6 * math.exp(-0.3 * layer_idx)
    lv = lam_vecs.astype(jnp.float32)
    lam = jnp.exp(jnp.sum(lv[0] * lv[1])) - jnp.exp(jnp.sum(lv[2] * lv[3])) + lambda_init
    attn = diff_attention(q, k, v, lam)
    attn = (rms_norm(attn, norm_g) * (1.0 - lambda_init)).reshape(b, s, DIFF_WIDTH)
    conv = short_gated_conv(cb, cc, cx, conv_w)
    return jnp.concatenate([attn, conv], axis=-1) @ w_out

def retention(q, k, v):
    b, s, h, dk = q.shape
    dv = v.shape[-1]
    n = s // RET_CHUNK
    log_g = jnp.log1p(-jnp.exp2(-5.0 - jnp.arange(h, dtype=jnp.float32)))
    idx = jnp.arange(RET_CHUNK, dtype=jnp.float32)
    rel = idx[:, None] - idx[None, :]
    intra_decay = jnp.where(rel >= 0, jnp.exp(log_g[:, None, None] * jnp.maximum(rel, 0.0)), 0.0)
    q_decay = jnp.exp(log_g[:, None] * (idx + 1.0))[None, :, :, None]
    k_decay = jnp.exp(log_g[:, None] * (RET_CHUNK - 1.0 - idx))[None, :, :, None]
    chunk_decay = jnp.exp(log_g * RET_CHUNK)[None, :, None, None]

    def to_chunks(t):
        return t.reshape(b, n, RET_CHUNK, h, t.shape[-1]).transpose(1, 0, 3, 2, 4)

    def step(state, inp):
        qc, kc, vc = inp
        sc = jnp.einsum('bhqd,bhkd->bhqk', qc, kc) * intra_decay[None]
        intra = jnp.einsum('bhqk,bhkv->bhqv', sc, vc)
        cross = jnp.einsum('bhqd,bhdv->bhqv', qc, state) * q_decay
        state = state * chunk_decay + jnp.einsum('bhkd,bhkv->bhdv', kc * k_decay, vc)
        return state, intra + cross

    state0 = jnp.zeros((b, h, dk, dv), jnp.float32)
    _, ys = lax.scan(step, state0, (to_chunks(q), to_chunks(k), to_chunks(v)))
    return ys.transpose(1, 0, 3, 2, 4).reshape(b, s, h, dv).astype(q.dtype)

def odd_mixer(x, w_in, w_out, norm_g):
    b, s, _ = x.shape
    q, k, v, g = jnp.split(x @ w_in, [RET_QK, 2 * RET_QK, 2 * RET_QK + RET_VW], axis=-1)
    q = rotary(q.reshape(b, s, RET_HEADS, RET_DK), RET_DK, RET_ROPE_THETA)
    k = rotary(k.reshape(b, s, RET_HEADS, RET_DK), RET_DK, RET_ROPE_THETA) * (RET_DK ** -0.5)
    v = v.reshape(b, s, RET_HEADS, RET_DV)
    y = retention(q, k, v)
    yf = y.astype(jnp.float32)
    mu = jnp.mean(yf, -1, keepdims=True)
    var = jnp.mean(jnp.square(yf - mu), -1, keepdims=True)
    y = ((yf - mu) * lax.rsqrt(var + LN_EPS)).astype(x.dtype).reshape(b, s, RET_VW) * norm_g
    return (jax.nn.silu(g) * y) @ w_out

def setup_inputs(seed: int = 0) -> dict:
    key = jax.random.key(seed)
    ks = jax.random.split(key, 14)
    beta = DEEPNORM_BETA
    x = jax.random.normal(ks[0], (BATCH, SEQ, D_MODEL), jnp.float32)
    ln_g = 1.0 + 0.02 * jax.random.normal(ks[1], (DEPTH, 3, D_MODEL), jnp.float32)
    ln_b = 0.02 * jax.random.normal(ks[2], (DEPTH, 3, D_MODEL), jnp.float32)
    ffn_w_in = jax.random.normal(ks[3], (DEPTH, 2, D_MODEL, 2 * D_FF), jnp.float32) * (D_MODEL ** -0.5 * beta)
    ffn_w_out = jax.random.normal(ks[4], (DEPTH, 2, D_FF, D_MODEL), jnp.float32) * (D_FF ** -0.5 * beta)
    even_scale = jnp.concatenate([
        jnp.ones((2 * DIFF_QK,), jnp.float32),
        jnp.full((DIFF_WIDTH,), beta, jnp.float32),
        jnp.ones((2 * CONV_CH,), jnp.float32),
        jnp.full((CONV_CH,), beta, jnp.float32)])
    even_w_in = jax.random.normal(ks[5], (N_EVEN, D_MODEL, EVEN_IN), jnp.float32) * (D_MODEL ** -0.5) * even_scale
    even_w_out = jax.random.normal(ks[6], (N_EVEN, DIFF_WIDTH + CONV_CH, D_MODEL), jnp.float32) * ((DIFF_WIDTH + CONV_CH) ** -0.5 * beta)
    diff_lambda = 0.1 * jax.random.normal(ks[7], (N_EVEN, 4, DIFF_DH), jnp.float32)
    diff_norm_g = 1.0 + 0.02 * jax.random.normal(ks[8], (N_EVEN, DIFF_DV), jnp.float32)
    conv_w = jax.random.normal(ks[9], (N_EVEN, CONV_WIDTH, CONV_CH), jnp.float32) * (CONV_WIDTH ** -0.5)
    odd_scale = jnp.concatenate([
        jnp.ones((2 * RET_QK,), jnp.float32),
        jnp.full((RET_VW,), beta, jnp.float32),
        jnp.ones((RET_VW,), jnp.float32)])
    odd_w_in = jax.random.normal(ks[10], (N_ODD, D_MODEL, ODD_IN), jnp.float32) * (D_MODEL ** -0.5) * odd_scale
    odd_w_out = jax.random.normal(ks[11], (N_ODD, RET_VW, D_MODEL), jnp.float32) * (RET_VW ** -0.5 * beta)
    ret_norm_g = 1.0 + 0.02 * jax.random.normal(ks[12], (N_ODD, RET_VW), jnp.float32)
    return {"x": x, "ln_g": ln_g, "ln_b": ln_b, "ffn_w_in": ffn_w_in, "ffn_w_out": ffn_w_out,
            "even_w_in": even_w_in, "even_w_out": even_w_out, "diff_lambda": diff_lambda,
            "diff_norm_g": diff_norm_g, "conv_w": conv_w, "odd_w_in": odd_w_in,
            "odd_w_out": odd_w_out, "ret_norm_g": ret_norm_g}

def reference(x, ln_g, ln_b, ffn_w_in, ffn_w_out, even_w_in, even_w_out, diff_lambda,
              diff_norm_g, conv_w, odd_w_in, odd_w_out, ret_norm_g):
    a = DEEPNORM_ALPHA
    for i in range(DEPTH):
        j = i // 2
        x = layer_norm(a * x + 0.5 * swiglu_ffn(x, ffn_w_in[i, 0], ffn_w_out[i, 0]), ln_g[i, 0], ln_b[i, 0])
        if i % 2 == 0:
            mix = even_mixer(x, even_w_in[j], even_w_out[j], diff_lambda[j], diff_norm_g[j], conv_w[j], i)
        else:
            mix = odd_mixer(x, odd_w_in[j], odd_w_out[j], ret_norm_g[j])
        x = layer_norm(a * x + mix, ln_g[i, 1], ln_b[i, 1])
        x = layer_norm(a * x + 0.5 * swiglu_ffn(x, ffn_w_in[i, 1], ffn_w_out[i, 1]), ln_g[i, 2], ln_b[i, 2])
    return x


_drawn_inputs = setup_inputs


def setup_inputs(seed=0):
    import zlib

    import numpy as np

    out = dict(_drawn_inputs(seed))
    spreads = {}
    factors = {'diff_norm_g': 8.0, 'ret_norm_g': 8.0}
    for name, (base, spread) in spreads.items():
        noise = np.random.default_rng([zlib.crc32(name.encode()), seed]).standard_normal(out[name].shape)
        drawn = base * np.exp(spread * noise) if base else spread * noise
        out[name] = __import__('jax').numpy.asarray(drawn.astype(out[name].dtype))
    for name, factor in factors.items():
        out[name] = (out[name] * factor).astype(out[name].dtype)
    return out
```

```python
from contextlib import ExitStack
import math

import numpy as np
import concourse.bass as bass
from concourse import mybir

F32 = mybir.dt.float32
F32R = mybir.dt.float32r
ALU = mybir.AluOpType
ACT = mybir.ActivationFunctionType
AX_X = mybir.AxisListType.X

P = 128
T = 512
D = 1024
DC = D // P
TB = T // P
FF = 2816
FC = FF // P
UB = 8
RING = 4
OUT_UNITS = -(-FC // UB)
FFN_UNITS = 2 * FC + OUT_UNITS * DC
HEADS = 4
EVEN_UNITS = 24 + DC
ODD_UNITS = 48 + 16
ALPHA = 4.0 ** 0.25
EPS = 1e-5
LAMBDA_INIT = 0.8 - 0.6 * math.exp(0.0)
ATTN_SCALE = 64 ** -0.5
KEY_SCALE = 256 ** -0.5
MASKED = -1e30
SPAN = [(b + 1) * P for b in range(TB)]
SPAN_AT = [sum(SPAN[:b]) for b in range(TB)]
REST = [T - b * P for b in range(TB)]
REST_AT = [sum(REST[:b]) for b in range(TB)]
TRI = sum(REST)

FFN_AT = [0, FFN_UNITS + EVEN_UNITS, 2 * FFN_UNITS + EVEN_UNITS, 3 * FFN_UNITS + EVEN_UNITS + ODD_UNITS]
EVEN_AT = FFN_UNITS
ODD_AT = 3 * FFN_UNITS + EVEN_UNITS
UNITS = 4 * FFN_UNITS + EVEN_UNITS + ODD_UNITS
FFN_LN = [0, 2, 3, 5]
EVEN_LN, ODD_LN, LAST_LN = 1, 4, 5

CONST = {}
_at = 0
for _name, _n in (("ident", P), ("ones", P), ("ones_d", P), ("ones_dv", P), ("ones_rms", 2), ("swap", P),
                  ("mask", P), ("ln_g", 6 * DC), ("ln_b", 6 * DC), ("conv_w", 12), ("norm_g", 1),
                  ("ret_g", 16), ("lam", 256)):
    CONST[_name] = (_at, _n)
    _at += _n
CONST_COLS = _at


def trunk(nc, x_in, stream, const_in, rope_even, rope_odd, decay_in, out):
    with ExitStack() as ctx:
        def sb(name, shape, dt=F32):
            return ctx.enter_context(nc.sbuf_tensor(name, shape, dt))

        def sem(name):
            return ctx.enter_context(nc.semaphore(name))

        bank = [ctx.enter_context(nc.psum_tensor(f"bank{i}", [P, T], F32)) for i in range(8)]

        z = sb("z", [P, DC, T])
        x_hi = sb("x_hi", [P, DC, T], F32R)
        x_lo = sb("x_lo", [P, DC, T], F32R)
        raw = sb("raw", [P, RING, UB * P])
        w_hi = sb("w_hi", [P, RING, UB * P], F32R)
        w_lo = sb("w_lo", [P, RING, UB * P], F32R)
        const = sb("const", [P, CONST_COLS])
        swap = sb("swap", [P, P], F32R)
        acc_sum = sb("acc_sum", [P, T])
        acc_sq = sb("acc_sq", [P, T])
        square = sb("square", [P, 2, T])
        diag = sb("diag", [P, T])
        stat = sb("stat", [P, 24])
        lam = sb("lam", [P, 8])

        def cst(name):
            a, n = CONST[name]
            return const[:, a:a + n]

        ident, ones, ones_d, ones_dv = cst("ident"), cst("ones"), cst("ones_d"), cst("ones_dv")
        mean2, var, rstd = stat[:, 8:12], stat[:, 12:16], stat[:, 16:20]

        class Region:
            def __init__(self, base):
                self.at = base

            def take(self, name, shape, dt=F32):
                t = nc.alloc_sbuf_tensor_at(name, [P] + shape, dt, offset=self.at)
                self.at += -(-4 * math.prod(shape) // 32) * 32
                return t

        arena_cols = (2 * FC + 3) * T
        arena = sb("arena", [P, arena_cols])
        base = nc.lookup_mloc(arena).addr
        ffn = Region(base)
        h_hi = ffn.take("h_hi", [FC, T], F32R)
        h_lo = ffn.take("h_lo", [FC, T], F32R)
        silu_g = ffn.take("silu_g", [2, T])
        h_f = ffn.take("h_f", [T])

        ev = Region(base)
        q_hi = ev.take("q_hi", [HEADS, T], F32R)
        q_lo = ev.take("q_lo", [HEADS, T], F32R)
        k_hi = ev.take("k_hi", [HEADS, T], F32R)
        k_lo = ev.take("k_lo", [HEADS, T], F32R)
        v_hi = ev.take("v_hi", [TB, T], F32R)
        v_lo = ev.take("v_lo", [TB, T], F32R)
        rope_e = ev.take("rope_e", [2, T])
        at_hi = ev.take("at_hi", [TRI], F32R)
        at_lo = ev.take("at_lo", [TRI], F32R)
        cc_sb = ev.take("cc_sb", [T])
        u_sb = ev.take("u_sb", [T + 2])
        y_sb = ev.take("y_sb", [T])
        ao_sb = ev.take("ao_sb", [T])
        e_sum = ev.take("e_sum", [2, 8])
        e_rec = ev.take("e_rec", [8])
        e_max = ev.take("e_max", [2, 2])
        rot_at = ev.at
        prob = ev.take("prob", [2, TRI])
        a_sb = ev.take("a_sb", [TRI])
        ev2 = Region(rot_at)
        qr_hi = ev2.take("qr_hi", [2, T], F32R)
        qr_lo = ev2.take("qr_lo", [2, T], F32R)
        qr_cos = ev2.take("qr_cos", [2, T])
        qr_sin = ev2.take("qr_sin", [T])

        od = Region(base)
        rq_hi = od.take("rq_hi", [2, T], F32R)
        rq_lo = od.take("rq_lo", [2, T], F32R)
        rk_hi = od.take("rk_hi", [2, T], F32R)
        rk_lo = od.take("rk_lo", [2, T], F32R)
        rv_hi = od.take("rv_hi", [TB, T], F32R)
        rv_lo = od.take("rv_lo", [TB, T], F32R)
        m_hi = od.take("m_hi", [TRI], F32R)
        m_lo = od.take("m_lo", [TRI], F32R)
        m_f = od.take("m_f", [T])
        r_t = od.take("r_t", [2, T])
        sg = od.take("sg", [4, T])
        y_f = od.take("y_f", [4, T])
        y_hi = od.take("y_hi", [4, T], F32R)
        y_lo = od.take("y_lo", [4, T], F32R)
        decay = od.take("decay", [HEADS, T])
        rope_o = od.take("rope_o", [2, T])
        for r in (ffn, ev, ev2, od):
            assert r.at <= base + 4 * arena_cols, (r.at - base, 4 * arena_cols)

        const_loaded = sem("const_loaded")
        x_loaded = sem("x_loaded")
        swap_ready = sem("swap_ready")
        raw_loaded = [sem(f"raw_loaded{i}") for i in range(RING)]
        w_hi_ready, w_ready, w_used = sem("w_hi_ready"), sem("w_ready"), sem("w_used")
        chain_sem = sem("dve_chain")
        x_hi_ready, x_ready = sem("x_hi_ready"), sem("x_ready")
        silu_done, h_full, h_hi_ready, h_ready = (sem(n) for n in (
            "silu_done", "h_full", "h_hi_ready", "h_ready"))
        z_full, square_full, sum_full, sumsq_full = (sem(n) for n in (
            "z_full", "square_full", "sum_full", "sumsq_full"))
        small_full, mean_full, rvar_ready, rstd_ready, diag_ready, rstd_full = (sem(n) for n in (
            "small_full", "mean_full", "rvar_ready", "rstd_ready", "diag_ready", "rstd_full"))
        centred, scaled, affine_done = sem("centred"), sem("scaled"), sem("affine_done")
        rope_e_loaded = sem("rope_e_loaded")
        lam_sum, lam_exp = sem("lam_sum"), sem("lam_exp")
        raw_hi, raw_lo, swap_full, rot_ready = (sem(n) for n in (
            "raw_hi", "raw_lo", "swap_full", "rot_ready"))
        e_v_hi, e_v_ready = sem("e_v_hi"), sem("e_v_ready")
        cc_copied, u_full, conv_ready = (sem(n) for n in (
            "cc_copied", "u_full", "conv_ready"))
        score_full, bias_ready, exp_done, mixed = (sem(n) for n in (
            "score_full", "bias_ready", "exp_done", "mixed"))
        at_full, at_hi_ready, at_ready, pv_full = (sem(n) for n in (
            "at_full", "at_hi_ready", "at_ready", "pv_full"))
        ao_copied, ao_squared, rms_small, rms_rvar, rms_rstd, rms_diag, rms_full, attn_ready = (sem(n) for n in (
            "ao_copied", "ao_squared", "rms_small", "rms_rvar", "rms_rstd", "rms_diag", "rms_full", "attn_ready"))
        table_o_loaded = sem("table_o_loaded")
        o_rot_ready, o_v_hi, o_v_ready, o_out_half = (sem(n) for n in (
            "o_rot_ready", "o_v_hi", "o_v_ready", "o_out_half"))
        ret_full, m_ready, sg_done, y_full, y_copied, y_squared = (sem(n) for n in (
            "ret_full", "m_ready", "sg_done", "y_full", "y_copied", "y_squared"))
        gn_sum, gn_sumsq, gn_small, gn_mean, gn_rvar, gn_rstd, gn_diag, gn_full, y_ready, z_scaled = (sem(n) for n in (
            "gn_sum", "gn_sumsq", "gn_small", "gn_mean", "gn_rvar", "gn_rstd", "gn_diag", "gn_full", "y_ready",
            "z_scaled"))
        stored = sem("stored")

        Z_AT = {0: 0, 1: 10, 2: 20, 3: 30, 4: 40 + 24, 5: 50 + 24}
        X_AT = {"ffn0": 0, "even": DC, "ffn1": 2 * DC, "ffn2": 3 * DC, "odd": 4 * DC, "ffn3": 5 * DC}
        block = ctx.enter_context(nc.Block())

        @block.sync
        def _(sp):
            def load(u, slot):
                sp.dma_start(raw[:, slot, :], stream[bass.ds(u, 1), :, :].rearrange("a p n -> (a p) n")).then_inc(raw_loaded[slot], 16)

            load(0, 0)
            for c in range(DC):
                sp.dma_start(z[:, c, :], x_in[c]).then_inc(x_loaded, 16)
                if c == 3:
                    load(1, 1)
            load(2, 2)
            load(3, 3)
            with sp.Fori(1, UNITS // RING) as i:
                for s in range(RING):
                    sp.wait_ge(w_ready, RING * i + (s + 1 - RING))
                    load(RING * i + s, s)
            for c in range(DC):
                sp.wait_ge(affine_done, DC * LAST_LN + c + 1)
                sp.dma_start(out[c], z[:, c, :]).then_inc(stored, 16)
            sp.wait_ge(stored, 16 * DC)

        @block.gpsimd
        def _(pool):
            def low_part(u, slot):
                pool.wait_ge(w_hi_ready, u + 1)
                nc.gpsimd.tensor_tensor(w_lo[:, slot, :], raw[:, slot, :], w_hi[:, slot, :].bitcast(F32),
                                        ALU.subtract).then_inc(w_ready, 1)

            with pool.Fori(0, UNITS // RING) as i:
                for s in range(RING):
                    low_part(RING * i + s, s)

        @block.scalar
        def _(act):
            def cast(u, loads, slot, free=True):
                act.wait_ge(raw_loaded[slot], 16 * (loads + 1))
                if free:
                    act.wait_ge(w_used, u + (1 - RING))
                nc.scalar.copy(w_hi[:, slot, :], raw[:, slot, :]).then_inc(w_hi_ready, 1)

            def cast_after(u):
                if u + RING < UNITS:
                    cast(u + RING, u // RING + 1, u % RING)

            act.dma_start(const[:, :], const_in).then_inc(const_loaded, 16)
            for u in range(RING):
                if u == 1:
                    for c in range(DC):
                        act.wait_ge(x_loaded, 16 * DC)
                        nc.scalar.copy(x_hi[:, c, :], z[:, c, :]).then_inc(x_hi_ready, 1)
                cast(u, 0, u, free=False)
            act.wait_ge(lam_sum, 2)
            nc.scalar.activation(lam[:, 2:4], lam[:, 0:2], ACT.Exp).then_inc(lam_exp, 1)

            def square_z(ln, oc, slot):
                act.wait_ge(z_full, oc + (Z_AT[ln] + 3))
                zo = z[:, bass.ds(oc, 1), :].rearrange("p a t -> p (a t)")
                nc.scalar.activation(square[:, slot, :], zo, ACT.Square).then_inc(square_full, 1)

            def ffn_in(n):
                b = FFN_AT[n]

                def pair(j, u_loads, s):
                    act.wait_ge(w_used, 2 * j + (b + 1))
                    nc.scalar.activation(silu_g[:, s // 2, :], bank[s][:], ACT.Silu).then_inc(silu_done, 1)
                    for k in range(2):
                        cast(2 * j + (b + k + RING), u_loads + 1, s + k)

                for p in range(2):
                    pair(p, b // RING, 2 * p)
                with act.Fori(1, FC // 2) as i:
                    for p in range(2):
                        pair(2 * i + p, b // RING + i, 2 * p)

            def ffn_out(n):
                b = FFN_AT[n] + 2 * FC
                ln = FFN_LN[n]
                if n < 3:
                    with act.Fori(0, 2) as i:
                        for q in range(4):
                            for k in range(OUT_UNITS):
                                r = OUT_UNITS * q + k
                                cast(12 * i + (b + r + RING), 3 * i + ((b + r) // RING + 1), r % RING)
                            square_z(ln, 4 * i + q, q % 2)
                else:
                    for oc in range(DC):
                        for k in range(OUT_UNITS):
                            cast_after(b + OUT_UNITS * oc + k)
                        square_z(ln, oc, oc % 2)

            def layer_norm(ln):
                act.wait_ge(rvar_ready, ln + 1)
                nc.scalar.activation(rstd, var, ACT.Sqrt).then_inc(rstd_ready, 1)
                g, b = CONST["ln_g"][0] + DC * ln, CONST["ln_b"][0] + DC * ln
                for c in range(DC):
                    act.wait_ge(scaled, DC * ln + c + 1)
                    nc.scalar.activation(z[:, c, :], z[:, c, :], ACT.Identity, bias=const[:, b + c:b + c + 1],
                                         scale=const[:, g + c:g + c + 1]).then_inc(affine_done, 1)
                    if ln != LAST_LN:
                        act.wait_ge(affine_done, DC * ln + c + 1)
                        nc.scalar.copy(x_hi[:, c, :], z[:, c, :]).then_inc(x_hi_ready, 1)

            def even():
                b = EVEN_AT
                for t in range(8):
                    act.wait_ge(w_used, b + t + 1)
                    if t >= 2:
                        act.wait_ge(swap_full, t - 1)
                    nc.scalar.copy(qr_hi[:, t % 2, :], bank[t][:]).then_inc(raw_hi, 1)
                    cast_after(b + t)
                for k in range(4):
                    cast_after(b + 8 + k)
                for t in range(TB):
                    act.wait_ge(w_used, b + 12)
                    nc.scalar.copy(v_hi[:, t, :], bank[t][:]).then_inc(e_v_hi, 1)
                for i in range(6):
                    for s in range(8 if i < 5 else 4):
                        if 1 <= i <= 4 and s == 0:
                            cast_after(b + 12 + 3 * i - 1)
                        if i < 4 and s in (3, 6):
                            cast_after(b + 12 + 3 * i + s // 3 - 1)
                        if i < 4 and s == 3:
                            act.wait_ge(w_used, b + 12 + 3 * i + 1)
                            if i:
                                act.wait_ge(u_full, i)
                            nc.scalar.copy(cc_sb[:], bank[0][:]).then_inc(cc_copied, 1)
                        if i < 4:
                            j, q = s // TB, s % TB
                            act.wait_ge(bias_ready, 8 * i + s + 1)
                            if i:
                                act.wait_ge(mixed, TB * (i - 1) + q + 1)
                            nc.scalar.activation(prob[:, j, SPAN_AT[q]:SPAN_AT[q] + SPAN[q]],
                                                 bank[4 + s % 2][:, 0:SPAN[q]], ACT.Exp,
                                                 bias=e_max[:, s % 2, 1:2], scale=ATTN_SCALE,
                                                 accum_out=e_sum[:, i % 2, s:s + 1]).then_inc(exp_done, 1)
                        if 1 <= i <= 4 and 4 <= s <= 6:
                            g = s - 4
                            a, n = REST_AT[g], REST[g] if g < 2 else TRI - REST_AT[2]
                            act.wait_ge(at_full, 3 * (i - 1) + g + 1)
                            nc.scalar.copy(at_hi[:, a:a + n], bank[6][:, 0:n]).then_inc(at_hi_ready, 1)
                        if i >= 2 and s == 0:
                            act.wait_ge(pv_full, i - 1)
                            if i >= 3:
                                act.wait_ge(attn_ready, i - 2)
                            nc.scalar.copy(ao_sb[:], bank[7][:]).then_inc(ao_copied, 1)
                            nc.scalar.activation(square[:, 0, :], bank[7][:], ACT.Square).then_inc(ao_squared, 1)
                        if i >= 2 and s == 1:
                            act.wait_ge(rms_rvar, i - 1)
                            nc.scalar.activation(rstd, var, ACT.Sqrt).then_inc(rms_rstd, 1)
                for oc in range(DC):
                    cast_after(b + 24 + oc)
                    square_z(EVEN_LN, oc, oc % 2)

            def odd():
                b = ODD_AT

                def head(h, u0, loads):
                    first = isinstance(h, int)
                    w, k0 = (0, 4) if first else (4, 8)
                    for k in range(4 + w + 4):
                        cast(u0 + (k + RING), loads + (k // RING + 1), k % RING)
                    for t in range(TB):
                        act.wait_ge(w_used, u0 + (4 + w + 4))
                        nc.scalar.copy(rv_hi[:, t, :], bank[4 + t][:]).then_inc(o_v_hi, 1)
                    for c, gb in enumerate((4, 1, 4, 1)):
                        act.wait_ge(w_used, u0 + (k0 + 4 + c + 1))
                        nc.scalar.activation(sg[:, c, :], bank[gb][:], ACT.Silu).then_inc(sg_done, 1)
                        k = k0 + 4 + c
                        cast(u0 + (k + RING), loads + (k // RING + 1), k % RING)
                        if c == 0:
                            for y, yb in enumerate((5, 6, 7, 0)):
                                act.wait_ge(y_full, 4 * h + y + 1)
                                nc.scalar.copy(y_f[:, y, :], bank[yb][:]).then_inc(y_copied, 1)
                                if y >= 2:
                                    act.wait_ge(gn_sumsq, 3 * h + y - 1)
                                nc.scalar.activation(square[:, y % 2, :], bank[yb][:],
                                                     ACT.Square).then_inc(y_squared, 1)
                        if c == 1:
                            act.wait_ge(gn_rvar, h + 1)
                            nc.scalar.activation(rstd, var, ACT.Sqrt).then_inc(gn_rstd, 1)

                head(0, b, b // RING)
                with act.Fori(1, HEADS) as h:
                    head(h, 16 * h + (b - 4), 4 * h + (b - 4) // RING)
                for oc in range(DC):
                    square_z(ODD_LN, oc, oc % 2)
                    if oc % 2:
                        cast_after(b + 60 + oc // 2)

            ffn_in(0)
            ffn_out(0)
            act.dma_start(rope_e[:, :, :], rope_even).then_inc(rope_e_loaded, 16)
            layer_norm(0)
            even()
            layer_norm(1)
            ffn_in(1)
            ffn_out(1)
            layer_norm(2)
            ffn_in(2)
            ffn_out(2)
            act.dma_start(rope_o[:, :, :], rope_odd).then_inc(table_o_loaded, 16)
            act.dma_start(decay[:, :, :], decay_in).then_inc(table_o_loaded, 16)
            layer_norm(3)
            odd()
            layer_norm(4)
            ffn_in(3)
            ffn_out(3)
            layer_norm(5)

        @block.vector
        def _(dve):
            class Chain:
                n = 0

                def link(self, ins):
                    ins.then_inc(chain_sem, 1)
                    self.n = self.n + 1
                    dve.wait_ge(chain_sem, self.n)

            chain = Chain()
            link = chain.link

            def loop(lo, hi, per, body):
                start = chain.n
                with dve.Fori(lo, hi) as i:
                    chain.n = (i - lo) * per + start
                    body(i)
                    last = chain.n
                chain.n = start + (hi - lo) * per
                return last

            dve.wait_ge(const_loaded, 16)
            nc.vector.tensor_copy(swap[:], cst("swap")).then_inc(swap_ready, 1)
            la = CONST["lam"][0]
            for k in range(2):
                link(nc.vector.tensor_tensor(diag[:, 64 * k:64 * k + 64], const[:, la + 128 * k:la + 128 * k + 64],
                                             const[:, la + 128 * k + 64:la + 128 * k + 128], ALU.mult))
                nc.vector.reduce_sum(lam[:, k:k + 1], diag[:, 64 * k:64 * k + 64], AX_X).then_inc(lam_sum, 1)
            dve.wait_ge(lam_exp, 1)
            link(nc.vector.tensor_tensor(lam[:, 4:5], lam[:, 3:4], lam[:, 2:3], ALU.subtract))
            link(nc.vector.tensor_scalar(lam[:, 5:6], lam[:, 4:5], -LAMBDA_INIT, None, ALU.add))
            link(nc.vector.tensor_scalar(lam[:, 6:7], cst("norm_g"), 1.0 - LAMBDA_INIT, None, ALU.mult))
            for c in range(DC):
                dve.wait_ge(x_hi_ready, c + 1)
                nc.vector.tensor_tensor(x_lo[:, c, :], z[:, c, :], x_hi[:, c, :].bitcast(F32),
                                        ALU.subtract).then_inc(x_ready, 1)

            def ffn_in(n):
                def pair(j, p):
                    g = FC * n + j
                    dve.wait_ge(silu_done, g + 1)
                    dve.wait_ge(w_used, 2 * j + (FFN_AT[n] + 2))
                    dve.wait_ge(h_ready, g)
                    nc.vector.scalar_tensor_tensor(out=h_f[:], in0=silu_g[:, p, :], scalar=0.5,
                                                   in1=bank[2 * p + 1][:], op0=ALU.mult,
                                                   op1=ALU.mult).then_inc(h_full, 1)
                    dve.wait_ge(h_full, g + 1)
                    hj = h_hi[:, bass.ds(j, 1), :].rearrange("p a t -> p (a t)")
                    nc.vector.tensor_copy(hj, h_f[:]).then_inc(h_hi_ready, 1)
                    dve.wait_ge(h_hi_ready, g + 1)
                    nc.vector.tensor_tensor(h_lo[:, bass.ds(j, 1), :].rearrange("p a t -> p (a t)"), h_f[:],
                                            hj.bitcast(F32), ALU.subtract).then_inc(h_ready, 1)

                for p in range(2):
                    pair(p, p)
                with dve.Fori(1, FC // 2) as i:
                    for p in range(2):
                        pair(2 * i + p, p)

            def clear_sums(ln):
                if ln:
                    dve.wait_ge(small_full, ln)
                    dve.wait_ge(mean_full, ln)
                dve.wait_ge(x_ready, DC * (ln + 1))
                dve.wait_ge(sumsq_full, DC * ln)
                nc.vector.memset(acc_sum[:], 0.0).then_inc(z_full, 1)
                nc.vector.memset(acc_sq[:], 0.0).then_inc(z_full, 1)
                dve.wait_ge(z_full, Z_AT[ln] + 2)

            def out_chunk(ln, oc, slot, b, scale=ALPHA):
                zo = z[:, bass.ds(oc, 1), :].rearrange("p a t -> p (a t)")
                nc.vector.scalar_tensor_tensor(out=zo, in0=zo, scalar=scale, in1=bank[b][:], op0=ALU.mult,
                                               op1=ALU.add).then_inc(z_full, 1)
                dve.wait_ge(z_full, oc + (Z_AT[ln] + 3))
                nc.vector.tensor_tensor(acc_sum[:], acc_sum[:], zo, ALU.add).then_inc(sum_full, 1)
                dve.wait_ge(square_full, oc + (DC * ln + 1))
                nc.vector.tensor_tensor(acc_sq[:], acc_sq[:], square[:, slot, :], ALU.add).then_inc(sumsq_full, 1)

            def ffn_out(n):
                ln = FFN_LN[n]
                clear_sums(ln)
                with dve.Fori(0, 2) as i:
                    for q in range(4):
                        dve.wait_ge(w_used, 12 * i + (FFN_AT[n] + 2 * FC + OUT_UNITS * (q + 1)))
                        out_chunk(ln, 4 * i + q, q % 2, 4 + q % 2)

            def variance(b, ready, index):
                dve.wait_ge(ready, index)
                link(nc.vector.tensor_copy(stat[:, 0:8].rearrange("p (s k) -> p s k", s=2),
                                           bank[b][:, 0:16:2].rearrange("p (s k) -> p s k", s=2)))
                link(nc.vector.tensor_tensor(mean2, stat[:, 0:4], stat[:, 0:4], ALU.mult))
                link(nc.vector.tensor_tensor(mean2, stat[:, 4:8], mean2, ALU.subtract))
                link(nc.vector.tensor_scalar(mean2, mean2, 0.0, EPS, ALU.max, ALU.add))
                nc.vector.reciprocal(var, mean2).then_inc(ready, 1)

            def diagonals(ready):
                for k in range(TB):
                    nc.vector.tensor_scalar(diag[:, k * P:(k + 1) * P], ident, rstd[:, k:k + 1], None,
                                            ALU.mult).then_inc(ready, 1)

            def layer_norm(ln):
                dve.wait_ge(small_full, ln + 1)
                variance(6, rvar_ready, ln)
                dve.wait_ge(rstd_ready, ln + 1)
                diagonals(diag_ready)

                def centre(c):
                    nc.vector.tensor_tensor(z[:, c, :], z[:, c, :], bank[7][:], ALU.subtract).then_inc(centred, 1)

                def low(c):
                    dve.wait_ge(x_hi_ready, DC * (ln + 1) + c + 1)
                    nc.vector.tensor_tensor(x_lo[:, c, :], z[:, c, :], x_hi[:, c, :].bitcast(F32),
                                            ALU.subtract).then_inc(x_ready, 1)

                dve.wait_ge(mean_full, ln + 1)
                for c in range(2):
                    centre(c)
                dve.wait_ge(rstd_full, ln + 1)
                for c in range(DC):
                    dve.wait_ge(centred, DC * ln + c + 1)
                    nc.vector.tensor_tensor(z[:, c, :], z[:, c, :], bank[6][:], ALU.mult).then_inc(scaled, 1)
                    if c + 2 < DC:
                        centre(c + 2)
                    if c and ln != LAST_LN:
                        low(c - 1)
                if ln != LAST_LN:
                    low(DC - 1)

            def even():
                dve.wait_ge(rope_e_loaded, 16)

                def unrotated(t):
                    dve.wait_ge(raw_hi, t + 1)
                    nc.vector.tensor_tensor(qr_lo[:, t % 2, :], bank[t][:], qr_hi[:, t % 2, :].bitcast(F32),
                                            ALU.subtract).then_inc(raw_lo, 1)
                    nc.vector.tensor_tensor(qr_cos[:, t % 2, :], bank[t][:], rope_e[:, 0, :],
                                            ALU.mult).then_inc(raw_lo, 1)

                def rotated(t):
                    hi, lo = (q_hi, q_lo) if t % 2 == 0 else (k_hi, k_lo)
                    dve.wait_ge(swap_full, t + 1)
                    dve.wait_ge(rot_ready, t)
                    link(nc.vector.tensor_tensor(qr_sin[:], bank[t][:], rope_e[:, 1, :], ALU.mult))
                    dve.wait_ge(raw_lo, 2 * t + 2)
                    link(nc.vector.tensor_tensor(qr_sin[:], qr_sin[:], qr_cos[:, t % 2, :], ALU.add))
                    link(nc.vector.tensor_copy(hi[:, t // 2, :], qr_sin[:]))
                    nc.vector.tensor_tensor(lo[:, t // 2, :], qr_sin[:], hi[:, t // 2, :].bitcast(F32),
                                            ALU.subtract).then_inc(rot_ready, 1)

                unrotated(0)
                unrotated(1)
                for t in range(6):
                    rotated(t)
                    unrotated(t + 2)
                rotated(6)
                rotated(7)
                link(nc.vector.memset(u_sb[:, 0:2], 0.0))
                for t in range(TB):
                    dve.wait_ge(e_v_hi, t + 1)
                    nc.vector.tensor_tensor(v_lo[:, t, :], bank[t][:], v_hi[:, t, :].bitcast(F32),
                                            ALU.subtract).then_inc(e_v_ready, 1)
                cw = CONST["conv_w"][0]

                def conv_w(k, i):
                    return const[:, cw + 4 * k + i:cw + 4 * k + i + 1]

                def conv_product(i):
                    dve.wait_ge(cc_copied, i + 1)
                    dve.wait_ge(w_used, EVEN_AT + 12 + 3 * i + 2)
                    nc.vector.tensor_tensor(u_sb[:, 2:T + 2], cc_sb[:], bank[1][:], ALU.mult).then_inc(u_full, 1)
                    dve.wait_ge(u_full, i + 1)
                    dve.wait_ge(conv_ready, i)
                    link(nc.vector.tensor_scalar(y_sb[:], u_sb[:, 2:T + 2], conv_w(2, i), None, ALU.mult))
                    for k in (1, 0):
                        link(nc.vector.scalar_tensor_tensor(out=y_sb[:], in0=u_sb[:, k:T + k], scalar=conv_w(k, i),
                                                            in1=y_sb[:], op0=ALU.mult, op1=ALU.add))

                def conv_gate(i):
                    dve.wait_ge(w_used, EVEN_AT + 12 + 3 * i + 3)
                    dve.wait_ge(score_full, 8 * i + 8)
                    link(nc.vector.tensor_tensor(y_sb[:], y_sb[:], bank[2][:], ALU.mult))
                    link(nc.vector.tensor_copy(q_hi[:, i, :], y_sb[:]))
                    nc.vector.tensor_tensor(q_lo[:, i, :], y_sb[:], q_hi[:, i, :].bitcast(F32),
                                            ALU.subtract).then_inc(conv_ready, 1)

                def score(i, s):
                    q, b, m = s % TB, bank[4 + s % 2], e_max[:, s % 2, :]
                    dve.wait_ge(score_full, 8 * i + s + 1)
                    own = b[:, SPAN[q] - P:SPAN[q]]
                    link(nc.vector.tensor_tensor(own, own, cst("mask"), ALU.add))
                    if 8 * i + s >= 2:
                        dve.wait_ge(exp_done, 8 * i + s - 1)
                        dve.wait_ge(bias_ready, 8 * i + s - 1)
                    link(nc.vector.reduce_max(m[:, 0:1], b[:, 0:SPAN[q]], AX_X))
                    nc.vector.tensor_scalar(m[:, 1:2], m[:, 0:1], -ATTN_SCALE, None, ALU.mult).then_inc(bias_ready, 1)

                def mix(h, q):
                    if q == 0:
                        dve.wait_ge(exp_done, 8 * h + 8)
                        dve.wait_ge(mixed, TB * h)
                        link(nc.vector.reciprocal(e_rec[:], e_sum[:, h % 2, :]))
                        link(nc.vector.tensor_scalar(e_rec[:, 4:8], e_rec[:, 4:8], lam[:, 5:6], None, ALU.mult))
                        if h:
                            dve.wait_ge(at_full, 3 * h)
                    a, n = SPAN_AT[q], SPAN[q]
                    link(nc.vector.tensor_scalar(prob[:, 1, a:a + n], prob[:, 1, a:a + n], e_rec[:, 4 + q:5 + q], None,
                                                 ALU.mult))
                    nc.vector.scalar_tensor_tensor(out=a_sb[:, a:a + n], in0=prob[:, 0, a:a + n],
                                                   scalar=e_rec[:, q:q + 1], in1=prob[:, 1, a:a + n],
                                                   op0=ALU.mult, op1=ALU.add).then_inc(mixed, 1)

                for i in range(6):
                    for s in range(8 if i < 5 else 4):
                        if 1 <= i <= 4 and s < 4:
                            mix(i - 1, s)
                        if i < 4:
                            score(i, s)
                        if 1 <= i <= 4 and s == 0:
                            conv_gate(i - 1)
                        if i < 4 and s == 6:
                            conv_product(i)
                        if 1 <= i <= 4 and 4 <= s <= 6:
                            g = s - 4
                            a, n = REST_AT[g], REST[g] if g < 2 else TRI - REST_AT[2]
                            dve.wait_ge(at_hi_ready, 3 * (i - 1) + g + 1)
                            nc.vector.tensor_tensor(at_lo[:, a:a + n], bank[6][:, 0:n], at_hi[:, a:a + n].bitcast(F32),
                                                    ALU.subtract).then_inc(at_ready, 1)
                        if i >= 2 and s == 1:
                            dve.wait_ge(rms_small, i - 1)
                            dve.wait_ge(rms_rvar, i - 2)
                            link(nc.vector.tensor_scalar(mean2, bank[3][:, 0:8:2], EPS, None, ALU.add))
                            nc.vector.reciprocal(var, mean2).then_inc(rms_rvar, 1)
                        if i >= 2 and s == 2:
                            dve.wait_ge(rms_rstd, i - 1)
                            diagonals(rms_diag)
                        if i >= 2 and s == 3:
                            h = i - 2
                            dve.wait_ge(rms_full, h + 1)
                            dve.wait_ge(ao_copied, h + 1)
                            link(nc.vector.tensor_tensor(ao_sb[:], ao_sb[:], bank[3][:], ALU.mult))
                            link(nc.vector.tensor_scalar(k_hi[:, h, :], ao_sb[:], lam[:, 6:7], None, ALU.mult))
                            nc.vector.scalar_tensor_tensor(out=k_lo[:, h, :], in0=ao_sb[:], scalar=lam[:, 6:7],
                                                           in1=k_hi[:, h, :].bitcast(F32), op0=ALU.mult,
                                                           op1=ALU.subtract).then_inc(attn_ready, 1)
                clear_sums(EVEN_LN)
                for oc in range(DC):
                    dve.wait_ge(w_used, EVEN_AT + 24 + oc + 1)
                    out_chunk(EVEN_LN, oc, oc % 2, (0, 1, 4, 5)[oc % 4])

            def odd():
                dve.wait_ge(table_o_loaded, 32)
                dve.wait_ge(x_ready, DC * (ODD_LN))
                for c in range(DC):
                    nc.vector.tensor_scalar(z[:, c, :], z[:, c, :], ALPHA, None, ALU.mult).then_inc(z_scaled, 1)
                rg = CONST["ret_g"][0]

                def head(h):
                    first = isinstance(h, int)
                    u0 = ODD_AT if first else 16 * h + (ODD_AT - 4)
                    cos, sin = rope_o[:, 0, :], rope_o[:, 1, :]
                    for b0, hi, lo in ((0, rq_hi, rq_lo), (2, rk_hi, rk_lo)):
                        dve.wait_ge(w_used, u0 + (b0 + 2))
                        for k, op in ((0, ALU.subtract), (1, ALU.add)):
                            dve.wait_ge(o_rot_ready, 4 * h + (b0 + k))
                            link(nc.vector.tensor_tensor(r_t[:, 0, :], bank[b0 + k][:], cos, ALU.mult))
                            link(nc.vector.tensor_tensor(r_t[:, 1, :], bank[b0 + 1 - k][:], sin, ALU.mult))
                            link(nc.vector.tensor_tensor(r_t[:, 0, :], r_t[:, 0, :], r_t[:, 1, :], op))
                            link(nc.vector.tensor_copy(hi[:, k, :], r_t[:, 0, :]))
                            nc.vector.tensor_tensor(lo[:, k, :], r_t[:, 0, :], hi[:, k, :].bitcast(F32),
                                                    ALU.subtract).then_inc(o_rot_ready, 1)
                    if not first:
                        for oc in range(DC):
                            if oc % 2 == 0:
                                dve.wait_ge(o_out_half, 4 * h + (oc // 2 - 3))
                            else:
                                dve.wait_ge(w_used, u0 + (4 + oc // 2 + 1))
                            dve.wait_ge(z_scaled, oc + 1)
                            nc.vector.tensor_tensor(z[:, oc, :], z[:, oc, :], bank[5 + oc % 2][:],
                                                    ALU.add).then_inc(z_full, 1)
                    for t in range(TB):
                        dve.wait_ge(o_v_hi, TB * h + t + 1)
                        nc.vector.tensor_tensor(rv_lo[:, t, :], bank[4 + t][:], rv_hi[:, t, :].bitcast(F32),
                                                ALU.subtract).then_inc(o_v_ready, 1)
                    for k in range(TB):
                        n, a = REST[k], REST_AT[k]
                        dve.wait_ge(ret_full, TB * h + k + 1)
                        dve.wait_ge(m_ready, TB * h + k)
                        link(nc.vector.tensor_tensor(m_f[:, 0:n], bank[k][:, 0:n],
                                                     decay[:, bass.ds(h, 1), 0:n].rearrange("p a t -> p (a t)"),
                                                     ALU.mult))
                        link(nc.vector.tensor_copy(m_hi[:, a:a + n], m_f[:, 0:n]))
                        nc.vector.tensor_tensor(m_lo[:, a:a + n], m_f[:, 0:n], m_hi[:, a:a + n].bitcast(F32),
                                                ALU.subtract).then_inc(m_ready, 1)
                    for c in range(1, 4):
                        dve.wait_ge(y_copied, 4 * h + c + 1)
                        dve.wait_ge(gn_sum, 3 * h + (c - 1))
                        nc.vector.tensor_tensor(acc_sum[:], y_f[:, 0, :] if c == 1 else acc_sum[:], y_f[:, c, :],
                                                ALU.add).then_inc(gn_sum, 1)
                        dve.wait_ge(y_squared, 4 * h + c + 1)
                        dve.wait_ge(gn_sumsq, 3 * h + (c - 1))
                        nc.vector.tensor_tensor(acc_sq[:], square[:, 0, :] if c == 1 else acc_sq[:],
                                                square[:, c % 2, :], ALU.add).then_inc(gn_sumsq, 1)
                    dve.wait_ge(gn_small, h + 1)
                    variance(2, gn_rvar, h)
                    dve.wait_ge(gn_rstd, h + 1)
                    diagonals(gn_diag)
                    dve.wait_ge(gn_mean, h + 1)
                    link(nc.vector.tensor_tensor(y_f[:, 0, :], y_f[:, 0, :], bank[3][:], ALU.subtract))
                    dve.wait_ge(gn_full, h + 1)
                    for c in range(4):
                        if c:
                            link(nc.vector.tensor_tensor(y_f[:, c, :], y_f[:, c, :], bank[3][:], ALU.subtract))
                        link(nc.vector.tensor_tensor(y_f[:, c, :], y_f[:, c, :], bank[2][:], ALU.mult))
                        dve.wait_ge(sg_done, 4 * h + c + 1)
                        link(nc.vector.scalar_tensor_tensor(out=y_f[:, c, :], in0=y_f[:, c, :],
                                                            scalar=const[:, bass.ds(4 * h + (rg + c), 1)],
                                                            in1=sg[:, c, :], op0=ALU.mult, op1=ALU.mult))
                        link(nc.vector.tensor_copy(y_hi[:, c, :], y_f[:, c, :]))
                        nc.vector.tensor_tensor(y_lo[:, c, :], y_f[:, c, :], y_hi[:, c, :].bitcast(F32),
                                                ALU.subtract).then_inc(y_ready, 1)

                before = chain.n
                head(0)
                loop(1, HEADS, chain.n - before, head)
                clear_sums(ODD_LN)
                for oc in range(DC):
                    if oc % 2 == 0:
                        dve.wait_ge(o_out_half, 4 * 3 + oc // 2 + 1)
                    else:
                        dve.wait_ge(w_used, ODD_AT + 60 + oc // 2 + 1)
                    out_chunk(ODD_LN, oc, oc % 2, 5 + oc % 2, scale=1.0)

            ffn_in(0)
            ffn_out(0)
            layer_norm(0)
            even()
            layer_norm(1)
            ffn_in(1)
            ffn_out(1)
            layer_norm(2)
            ffn_in(2)
            ffn_out(2)
            layer_norm(3)
            odd()
            layer_norm(4)
            ffn_in(3)
            ffn_out(3)
            layer_norm(5)

        @block.tensor
        def _(pe):
            def mm3(o, a, b, start, stop):
                nc.tensor.matmul(o, a[0], b[0], start=start, stop=False)
                nc.tensor.matmul(o, a[0], b[1], start=False, stop=False)
                return nc.tensor.matmul(o, a[1], b[0], start=False, stop=stop)

            def w(slot, blk):
                c = slice(blk * P, (blk + 1) * P)
                return w_hi[:, slot, c], w_lo[:, slot, c]

            def x(c):
                return x_hi[:, c, :], x_lo[:, c, :]

            def part(hi, lo, *at):
                return hi[:, *at], lo[:, *at]

            def unit(u):
                pe.wait_ge(w_ready, u + 1)

            def first_four(u0, x_at):
                for c in range(DC):
                    pe.wait_ge(x_ready, x_at + c + 1)
                    for s in range(RING):
                        if c == 0:
                            unit(u0 + s)
                        last = mm3(bank[s][:], w(s, c), x(c), c == 0, c == DC - 1)
                        if c == DC - 1:
                            last.then_inc(w_used, 1)

            def project(u, slot, o):
                unit(u)
                for c in range(DC):
                    last = mm3(o, w(slot, c), x(c), c == 0, c == DC - 1)
                last.then_inc(w_used, 1)

            def project_v(u0, o, each=None):
                for k in range(RING):
                    unit(u0 + k)
                    for half in range(2):
                        c = 2 * k + half
                        n = slice(half * T, (half + 1) * T)
                        for t in range(TB):
                            if c == 0 and each:
                                each(t)
                            last = mm3(o[t][:], part(x_hi, x_lo, c, slice(t * P, (t + 1) * P)),
                                       part(w_hi, w_lo, k, n), c == 0, c == DC - 1)
                    last.then_inc(w_used, 1)
                    yield k

            def ffn_in(n):
                b = FFN_AT[n]
                first_four(b, X_AT[f"ffn{n}"])
                with pe.Fori(1, FC // 2) as i:
                    for s in range(4):
                        if s % 2 == 0:
                            pe.wait_ge(h_full, 2 * i + (FC * n + s // 2 - 1))
                        project(4 * i + (b + s), s, bank[s][:])

            def ffn_out(n):
                b, ln = FFN_AT[n] + 2 * FC, FFN_LN[n]
                with pe.Fori(0, 2) as i:
                    for q in range(4):
                        o = bank[4 + q % 2][:]
                        pe.wait_ge(z_full, 4 * i + (Z_AT[ln] + q + 1))
                        for kc in range(FC):
                            r = OUT_UNITS * q + kc // UB
                            if kc % UB == 0:
                                unit(12 * i + (b + r))
                            if q == 0:
                                pe.wait_ge(h_ready, FC * n + kc + 1)
                            last = mm3(o, w(r % RING, kc % UB), part(h_hi, h_lo, kc), kc == 0, kc == FC - 1)
                            if kc % UB == UB - 1 or kc == FC - 1:
                                last.then_inc(w_used, 1)

            def small_sums(o, col, acc, one):
                for k in range(TB):
                    last = nc.tensor.matmul(o[:, col + 2 * k:col + 2 * k + 2], acc[:, k * P:(k + 1) * P],
                                            one[:, 0:2], start=True, stop=True)
                return last

            def layer_norm(ln):
                pe.wait_ge(sum_full, DC * (ln + 1))
                small_sums(bank[6], 0, acc_sum, ones_d)
                nc.tensor.matmul(bank[7][:], ones_d, acc_sum[:], start=True, stop=True).then_inc(mean_full, 1)
                pe.wait_ge(sumsq_full, DC * (ln + 1))
                small_sums(bank[6], 8, acc_sq, ones_d).then_inc(small_full, 1)
                pe.wait_ge(diag_ready, TB * (ln + 1))
                nc.tensor.matmul(bank[6][:], ones, diag[:], start=True, stop=True).then_inc(rstd_full, 1)

            def even():
                b = EVEN_AT

                def swap_halves(t):
                    pe.wait_ge(raw_lo, 2 * t + 2)
                    nc.tensor.matmul(bank[t][:], swap[:], qr_hi[:, t % 2, :], start=True, stop=False)
                    nc.tensor.matmul(bank[t][:], swap[:], qr_lo[:, t % 2, :], start=False,
                                     stop=True).then_inc(swap_full, 1)

                pe.wait_ge(swap_ready, 1)
                first_four(b, X_AT["even"])
                for t in range(4):
                    project(b + 4 + t, t, bank[4 + t][:])
                    swap_halves(t)
                for k in project_v(b + 8, bank[0:4], lambda t: pe.wait_ge(rot_ready, t + 1)):
                    swap_halves(4 + k)

                def conv_part(i, m):
                    f, c = m // DC, m % DC
                    if c == 0:
                        unit(b + 12 + 3 * i + f)
                        if i == 0:
                            pe.wait_ge(e_v_ready, f + 1)
                        else:
                            pe.wait_ge((cc_copied, u_full, conv_ready)[f], i)
                    last = mm3(bank[f][:], w((3 * i + f) % RING, c), x(c), c == 0, c == DC - 1)
                    if c == DC - 1:
                        last.then_inc(w_used, 1)

                def score(i, s):
                    j, q = s // TB, s % TB
                    if 8 * i + s < 2:
                        pe.wait_ge(rot_ready, 8)
                    else:
                        pe.wait_ge(exp_done, 8 * i + s - 1)
                    r = slice(64 * j, 64 * j + 64)
                    qs, ks = slice(q * P, (q + 1) * P), slice(0, SPAN[q])
                    mm3(bank[4 + s % 2][:, ks], (q_hi[r, i, qs], q_lo[r, i, qs]), (k_hi[r, i, ks], k_lo[r, i, ks]),
                        True, True).then_inc(score_full, 1)

                def turn(h, g):
                    pe.wait_ge(mixed, TB * (h + 1))
                    if 3 * h + g:
                        pe.wait_ge(at_ready, 3 * h + g)
                    if h:
                        pe.wait_ge(pv_full, h)
                    for kb in ((0,), (1,), (2, 3))[g]:
                        for q in range(kb, TB):
                            c = REST_AT[kb] - REST_AT[g] + (q - kb) * P
                            last = nc.tensor.transpose(bank[6][:, c:c + P],
                                                       a_sb[:, SPAN_AT[q] + kb * P:SPAN_AT[q] + kb * P + P], ident)
                    last.then_inc(at_full, 1)

                def values(h):
                    pe.wait_ge(at_ready, 3 * h + 3)
                    if h == 0:
                        pe.wait_ge(e_v_ready, TB)
                    else:
                        pe.wait_ge(ao_squared, h)
                    for kb in range(TB):
                        last = mm3(bank[7][:, kb * P:T], part(v_hi, v_lo, kb, slice(h * P, (h + 1) * P)),
                                   part(at_hi, at_lo, slice(REST_AT[kb], REST_AT[kb] + REST[kb])),
                                   kb == 0, kb == TB - 1)
                    last.then_inc(pv_full, 1)

                O = (0, 1, 4, 5)

                def out_part(oc, blk):
                    if blk == 0:
                        unit(b + 24 + oc)
                        if oc >= 4:
                            pe.wait_ge(z_full, Z_AT[EVEN_LN] + 2 + oc - 3)
                        else:
                            pe.wait_ge(*((cc_copied, 4), (u_full, 4), (exp_done, 31), (exp_done, 32))[oc])
                    if blk < 4:
                        pe.wait_ge(conv_ready, blk + 1)
                        src = part(q_hi, q_lo, blk)
                    else:
                        pe.wait_ge(attn_ready, blk - 3)
                        src = part(k_hi, k_lo, blk - 4)
                    last = mm3(bank[O[oc % 4]][:], w(oc % RING, blk), src, blk == 0, blk == UB - 1)
                    if blk == UB - 1:
                        last.then_inc(w_used, 1)

                for i in range(6):
                    for s in range(8 if i < 5 else 4):
                        if i < 4:
                            for m in range(3 * s, 3 * s + 3):
                                conv_part(i, m)
                            score(i, s)
                        elif i == 4:
                            for m in (2 * s, 2 * s + 1):
                                out_part(m // 4, m % 4)
                        else:
                            for blk in (4, 5, 6):
                                out_part(s, blk)
                        if 1 <= i <= 4 and 4 <= s <= 6:
                            turn(i - 1, s - 4)
                        if 1 <= i <= 4 and s == 7:
                            values(i - 1)
                        if i >= 2 and s == 0:
                            pe.wait_ge(ao_squared, i - 1)
                            small_sums(bank[3], 0, square[:, 0, :], cst("ones_rms")).then_inc(rms_small, 1)
                        if i >= 2 and s == 3:
                            pe.wait_ge(rms_diag, TB * (i - 1))
                            nc.tensor.matmul(bank[3][:], ones, diag[:], start=True, stop=True).then_inc(rms_full, 1)
                for oc in range(4):
                    out_part(oc, 7)
                for oc in range(4, DC):
                    for blk in range(UB):
                        out_part(oc, blk)

            def odd():
                b = ODD_AT

                def out_of_head(u0, z_free):
                    for wu in range(4):
                        unit(u0 + wu)
                        for o in range(2):
                            oc = 2 * wu + o
                            if oc >= 2:
                                pe.wait_ge(z_full, z_free + (oc - 1))
                            for c in range(4):
                                last = mm3(bank[5 + o][:], w(wu, 4 * o + c), part(y_hi, y_lo, c), c == 0, c == 3)
                            last.then_inc(w_used if o else o_out_half, 1)

                def head(h, u0):
                    first = isinstance(h, int)
                    if first:
                        first_four(u0, X_AT["odd"])
                        v0 = u0 + 4
                    else:
                        for s, (free, n) in enumerate(((y_squared, 4), (sg_done, 4), (y_ready, 4), (y_ready, 4))):
                            pe.wait_ge(free, n * h)
                            project(u0 + s, s, bank[s][:])
                        z_at = Z_AT[3] + 10
                        out_of_head(u0 + 4, 8 * h + (z_at - 8))
                        pe.wait_ge(z_full, 8 * h + z_at)
                        v0 = u0 + 8
                    for _ in project_v(v0, bank[4:8]):
                        pass
                    for kb in range(TB):
                        pe.wait_ge(o_rot_ready, 4 * h + 4)
                        for c in range(2):
                            last = mm3(bank[kb][:, 0:REST[kb]], part(rk_hi, rk_lo, c, slice(kb * P, (kb + 1) * P)),
                                       part(rq_hi, rq_lo, c, slice(kb * P, T)), c == 0, c == 1)
                        last.then_inc(ret_full, 1)
                    g0 = v0 + 4
                    pe.wait_ge(o_v_ready, 4 * h + 1)
                    project(g0, 0, bank[4][:])
                    pe.wait_ge(o_v_ready, 4 * h + 4)
                    pe.wait_ge(m_ready, 4 * h + 4)
                    for c, yb in enumerate((5, 6, 7, 0)):
                        for kb in range(TB):
                            last = mm3(bank[yb][:, kb * P:T], part(rv_hi, rv_lo, kb, slice(c * P, (c + 1) * P)),
                                       part(m_hi, m_lo, slice(REST_AT[kb], REST_AT[kb] + REST[kb])),
                                       kb == 0, kb == TB - 1)
                        last.then_inc(y_full, 1)
                    project(g0 + 1, 1, bank[1][:])
                    pe.wait_ge(gn_sum, 3 * h + 3)
                    small_sums(bank[2], 0, acc_sum, ones_dv)
                    nc.tensor.matmul(bank[3][:], ones_dv, acc_sum[:], start=True, stop=True).then_inc(gn_mean, 1)
                    pe.wait_ge(gn_sumsq, 3 * h + 3)
                    small_sums(bank[2], 8, acc_sq, ones_dv).then_inc(gn_small, 1)
                    pe.wait_ge(sg_done, 4 * h + 1)
                    project(g0 + 2, 2, bank[4][:])
                    pe.wait_ge(gn_diag, 4 * h + 4)
                    nc.tensor.matmul(bank[2][:], ones, diag[:], start=True, stop=True).then_inc(gn_full, 1)
                    pe.wait_ge(sg_done, 4 * h + 2)
                    project(g0 + 3, 3, bank[1][:])

                head(0, b)
                with pe.Fori(1, HEADS) as h:
                    head(h, 16 * h + (b - 4))
                pe.wait_ge(y_ready, 4 * HEADS)
                pe.wait_ge(y_squared, 4 * HEADS)
                out_of_head(b + 60, Z_AT[ODD_LN] + 2)

            ffn_in(0)
            ffn_out(0)
            layer_norm(0)
            even()
            layer_norm(1)
            ffn_in(1)
            ffn_out(1)
            layer_norm(2)
            ffn_in(2)
            ffn_out(2)
            layer_norm(3)
            odd()
            layer_norm(4)
            ffn_in(3)
            ffn_out(3)
            layer_norm(5)


def _weight_stream(ffn_w_in, ffn_w_out, even_w_in, even_w_out, odd_w_in, odd_w_out):
    out = np.zeros((UNITS, P, UB, P), np.float32)
    at = [0]

    def put(blocks):
        out[at[0], :, :len(blocks)] = blocks.transpose(1, 0, 2)
        at[0] += 1

    def columns(wt, c):
        put(wt[:, c:c + P].reshape(DC, P, P))

    def values(wt, c):
        for k in range(RING):
            put(wt[2 * k * P:(2 * k + 2) * P, c:c + T].reshape(2, P, 4, P).transpose(0, 2, 1, 3).reshape(8, P, P))

    def ffn(w_in, w_out):
        for j in range(FC):
            columns(w_in, j * P)
            columns(w_in, FF + j * P)
        for oc in range(DC):
            rows = w_out[:, oc * P:(oc + 1) * P].reshape(FC, P, P)
            for k in range(OUT_UNITS):
                put(rows[UB * k:UB * (k + 1)])

    def even(w_in, w_out):
        for t in range(4):
            columns(w_in, t * P)
            columns(w_in, 512 + t * P)
        values(w_in, 1024)
        for i in range(4):
            for f in (2048, 2560, 1536):
                columns(w_in, f + i * P)
        for oc in range(DC):
            rows = w_out[:, oc * P:(oc + 1) * P].reshape(DC, P, P)
            put(np.concatenate([rows[4:], rows[:4]]))

    def odd(w_in, w_out):
        def share(h):
            rows = w_out[h * T:(h + 1) * T].reshape(4, P, DC, P)
            for wu in range(4):
                put(rows[:, :, 2 * wu:2 * wu + 2].transpose(2, 0, 1, 3).reshape(8, P, P))

        for h in range(HEADS):
            for c in (0, P, D, D + P):
                columns(w_in, c + 256 * h)
            if h:
                share(h - 1)
            values(w_in, 2 * D + T * h)
            for c in range(4):
                columns(w_in, 4 * D + T * h + c * P)
        share(HEADS - 1)

    ffn(ffn_w_in[0, 0], ffn_w_out[0, 0])
    even(even_w_in[0], even_w_out[0])
    ffn(ffn_w_in[0, 1], ffn_w_out[0, 1])
    ffn(ffn_w_in[1, 0], ffn_w_out[1, 0])
    odd(odd_w_in[0], odd_w_out[0])
    ffn(ffn_w_in[1, 1], ffn_w_out[1, 1])
    return out.reshape(UNITS, P, UB * P)


def _rope(half, theta, n_rot):
    inv = np.exp(np.float32(-math.log(theta)) * np.arange(half, dtype=np.float32) * np.float32(2.0 / n_rot))
    ang = inv[:, None].astype(np.float32) * np.arange(T, dtype=np.float32)[None, :]
    return np.cos(ang).astype(np.float32), np.sin(ang).astype(np.float32)


def _tables():
    c, s = _rope(8, 500000.0, 16)
    even = np.zeros((P, 2, T), np.float32)
    even[:, 0] = 1.0
    swap = np.zeros((P, P), np.float32)
    for head in (0, 64):
        even[head:head + 8, 0], even[head + 8:head + 16, 0] = c, c
        even[head:head + 8, 1], even[head + 8:head + 16, 1] = -s, s
        for m in range(8):
            swap[head + m, head + 8 + m] = swap[head + 8 + m, head + m] = 1.0
    c, s = _rope(128, 10000.0, 256)
    odd = np.stack([c, s], 1)
    rel = np.arange(T)[None, :] - np.arange(P)[:, None]
    decay = np.zeros((P, HEADS, T), np.float32)
    for h in range(HEADS):
        decay[:, h] = np.where(rel >= 0, np.exp(np.log1p(-2.0 ** (-5 - h)) * np.maximum(rel, 0)), 0.0) * KEY_SCALE
    mask = np.where(np.arange(P)[None, :] <= np.arange(P)[:, None], 0.0, MASKED).astype(np.float32)
    return even, odd, decay, swap, mask


def kernel(x, ln_g, ln_b, ffn_w_in, ffn_w_out, even_w_in, even_w_out, diff_lambda, diff_norm_g, conv_w,
           odd_w_in, odd_w_out, ret_norm_g):
    import concourse.bacc as bacc
    from concourse.bass_utils import run_bass_kernel_spmd

    even, odd, decay, swap, mask = _tables()
    packed = {
        "ident": np.eye(P), "ones": np.ones((P, P)), "ones_d": np.full((P, P), 1.0 / D),
        "ones_dv": np.full((P, P), 1.0 / T), "ones_rms": np.full((P, 2), 1.0 / P), "swap": swap, "mask": mask,
        "ln_g": np.asarray(ln_g).reshape(6 * DC, P).T, "ln_b": np.asarray(ln_b).reshape(6 * DC, P).T,
        "conv_w": np.asarray(conv_w).reshape(12, P).T, "norm_g": np.asarray(diff_norm_g).reshape(P, 1),
        "ret_g": np.asarray(ret_norm_g).reshape(16, P).T,
        "lam": np.broadcast_to(np.asarray(diff_lambda).reshape(1, 256), (P, 256)),
    }
    const = np.concatenate([np.asarray(packed[name], np.float32) for name in CONST], 1)
    arrays = {
        "x_t": np.ascontiguousarray(np.asarray(x)[0].T.reshape(DC, P, T)),
        "stream": _weight_stream(*(np.asarray(a) for a in (ffn_w_in, ffn_w_out, even_w_in, even_w_out,
                                                           odd_w_in, odd_w_out))),
        "const": np.ascontiguousarray(const), "rope_even": even, "rope_odd": odd, "decay": decay,
    }
    nc = bacc.Bacc("TRN2", target_bir_lowering=False, num_devices=1)
    args = [nc.dram_tensor(f"in_{n}", a.shape, mybir.dt.from_np(a.dtype), kind="ExternalInput").ap()
            for n, a in arrays.items()]
    out = nc.dram_tensor("out_t", (DC, P, T), F32, kind="ExternalOutput").ap()
    trunk(nc, *args, out)
    r = run_bass_kernel_spmd(nc, [{f"in_{n}": a for n, a in arrays.items()}], core_ids=[0])
    got = np.asarray(r.results[0]["out_t"])
    return np.ascontiguousarray(got.reshape(D, T).T).reshape(1, T, D)
```

```python
from contextlib import ExitStack
import math

import numpy as np
import concourse.bass as bass
from concourse import mybir

F32 = mybir.dt.float32
F32R = mybir.dt.float32r
ALU = mybir.AluOpType
ACT = mybir.ActivationFunctionType
AX_X = mybir.AxisListType.X

P = 128
T = 512
D = 1024
DC = D // P
TB = T // P
FF = 2816
FC = FF // P
UB = 8
RING = 4
OUT_UNITS = -(-FC // UB)
FFN_UNITS = 2 * FC + OUT_UNITS * DC
HEADS = 4
EVEN_UNITS = 24 + DC
ODD_UNITS = 48 + 16
ALPHA = 4.0 ** 0.25
EPS = 1e-5
LAMBDA_INIT = 0.8 - 0.6 * math.exp(0.0)
ATTN_SCALE = 64 ** -0.5
KEY_SCALE = 256 ** -0.5
MASKED = -1e30
SPAN = [(b + 1) * P for b in range(TB)]
SPAN_AT = [sum(SPAN[:b]) for b in range(TB)]
REST = [T - b * P for b in range(TB)]
REST_AT = [sum(REST[:b]) for b in range(TB)]
TRI = sum(REST)

FFN_AT = [0, FFN_UNITS + EVEN_UNITS, 2 * FFN_UNITS + EVEN_UNITS, 3 * FFN_UNITS + EVEN_UNITS + ODD_UNITS]
EVEN_AT = FFN_UNITS
ODD_AT = 3 * FFN_UNITS + EVEN_UNITS
UNITS = 4 * FFN_UNITS + EVEN_UNITS + ODD_UNITS
FFN_LN = [0, 2, 3, 5]
EVEN_LN, ODD_LN, LAST_LN = 1, 4, 5

OUT_BANKS = (5, 6, 7, 4)

CONST = {}
_at = 0
for _name, _n in (("ident", P), ("mean_d", 2), ("mean_dv", 2), ("mean_rms", 2), ("swap", P), ("mask", P),
                  ("rows", T), ("ln_g", 6 * DC), ("ln_b", 6 * DC), ("conv_w", 12), ("norm_g", 1),
                  ("ret_g", 16), ("lam", 256)):
    CONST[_name] = (_at, _n)
    _at += _n
CONST_COLS = _at


def trunk(nc, x_in, stream, const_in, rope_even, rope_odd, decay_in, out):
    with ExitStack() as ctx:
        def sb(name, shape, dt=F32):
            return ctx.enter_context(nc.sbuf_tensor(name, shape, dt))

        def sem(name):
            return ctx.enter_context(nc.semaphore(name))

        bank = [ctx.enter_context(nc.psum_tensor(f"bank{i}", [P, T], F32)) for i in range(8)]

        z = sb("z", [P, DC, T])
        x_hi = sb("x_hi", [P, DC, T], F32R)
        x_lo = sb("x_lo", [P, DC, T], F32R)
        raw = sb("raw", [P, RING, UB * P])
        w_hi = sb("w_hi", [P, RING, UB * P], F32R)
        w_lo = sb("w_lo", [P, RING, UB * P], F32R)
        const = sb("const", [P, CONST_COLS])
        swap = sb("swap", [P, P], F32R)
        ident_r = sb("ident_r", [P, P], F32R)
        mask = sb("mask", [P, P], F32R)
        rows = sb("rows", [8, T], F32R)
        acc_sum = sb("acc_sum", [P, T])
        acc_sq = sb("acc_sq", [P, T])
        square = sb("square", [P, 2, T])
        stat = sb("stat", [P, 40])
        row_mean = sb("row_mean", [8, P], F32R)
        row_rstd = sb("row_rstd", [8, P], F32R)
        lam = sb("lam", [P, 8])

        def cst(name):
            a, n = CONST[name]
            return const[:, a:a + n]

        ident = cst("ident")
        mean, mean2, inv_var, rstd = (stat[:, 4 * k:4 * k + 4] for k in range(4))
        parts_mean, parts_rstd = stat[:, 16:24], stat[:, 24:32]

        class Region:
            def __init__(self, base):
                self.at = base

            def take(self, name, shape, dt=F32):
                t = nc.alloc_sbuf_tensor_at(name, [P] + shape, dt, offset=self.at)
                self.at += -(-4 * math.prod(shape) // 32) * 32
                return t

        arena_cols = (2 * FC + 3) * T
        arena = sb("arena", [P, arena_cols])
        base = nc.lookup_mloc(arena).addr
        ffn = Region(base)
        h_hi = ffn.take("h_hi", [FC, T], F32R)
        h_lo = ffn.take("h_lo", [FC, T], F32R)
        silu_g = ffn.take("silu_g", [2, T])
        h_f = ffn.take("h_f", [T])

        ev = Region(base)
        q_hi = ev.take("q_hi", [HEADS, T], F32R)
        q_lo = ev.take("q_lo", [HEADS, T], F32R)
        k_hi = ev.take("k_hi", [HEADS, T], F32R)
        k_lo = ev.take("k_lo", [HEADS, T], F32R)
        v_hi = ev.take("v_hi", [TB, T], F32R)
        v_lo = ev.take("v_lo", [TB, T], F32R)
        rope_e = ev.take("rope_e", [4, T])
        at_hi = ev.take("at_hi", [TRI], F32R)
        at_lo = ev.take("at_lo", [TRI], F32R)
        cc_sb = ev.take("cc_sb", [T])
        u_sb = ev.take("u_sb", [T + 2])
        y_sb = ev.take("y_sb", [T])
        ao_sb = ev.take("ao_sb", [T])
        e_sum = ev.take("e_sum", [2, 8])
        e_rec = ev.take("e_rec", [8])
        e_max = ev.take("e_max", [2])
        rot_at = ev.at
        prob = ev.take("prob", [2, TRI])
        a_sb = ev.take("a_sb", [TRI])
        ev2 = Region(rot_at)
        qr_hi = ev2.take("qr_hi", [2, T], F32R)
        qr_lo = ev2.take("qr_lo", [2, T], F32R)
        qr_cos = ev2.take("qr_cos", [2, T])
        qr_sin = ev2.take("qr_sin", [T])

        od = Region(base)
        rq_hi = od.take("rq_hi", [2, T], F32R)
        rq_lo = od.take("rq_lo", [2, T], F32R)
        rk_hi = od.take("rk_hi", [2, T], F32R)
        rk_lo = od.take("rk_lo", [2, T], F32R)
        rv_hi = od.take("rv_hi", [TB, T], F32R)
        rv_lo = od.take("rv_lo", [TB, T], F32R)
        m_hi = od.take("m_hi", [TRI], F32R)
        m_lo = od.take("m_lo", [TRI], F32R)
        m_f = od.take("m_f", [T])
        r_t = od.take("r_t", [2, T])
        sg = od.take("sg", [4, T])
        y_f = od.take("y_f", [4, T])
        y_hi = od.take("y_hi", [4, T], F32R)
        y_lo = od.take("y_lo", [4, T], F32R)
        decay = od.take("decay", [HEADS, T])
        rope_o = od.take("rope_o", [2, T])
        for r in (ffn, ev, ev2, od):
            assert r.at <= base + 4 * arena_cols, (r.at - base, 4 * arena_cols)

        const_loaded = sem("const_loaded")
        x_loaded = [sem(f"x_loaded{c}") for c in range(DC)]
        const_ready = sem("const_ready")
        raw_loaded = [sem(f"raw_loaded{i}") for i in range(RING)]
        w_hi_ready, w_ready, w_used = sem("w_hi_ready"), sem("w_ready"), sem("w_used")
        chain_sem = sem("dve_chain")
        x_hi_ready, x_ready = sem("x_hi_ready"), sem("x_ready")
        silu_done, h_full, h_hi_ready, h_ready = (sem(n) for n in (
            "silu_done", "h_full", "h_hi_ready", "h_ready"))
        z_full, square_full, sum_full, sumsq_full = (sem(n) for n in (
            "z_full", "square_full", "sum_full", "sumsq_full"))

        class Stats:

            def __init__(self, kind):
                self.sums = sem(kind + "_sums")
                self.squares = sem(kind + "_squares")
                self.mean_parts = sem(kind + "_mean_parts")
                self.mean_turned = sem(kind + "_mean_turned")
                self.mean_row = sem(kind + "_mean_row")
                self.mean_full = sem(kind + "_mean_full")
                self.inv_var = sem(kind + "_inv_var")
                self.rstd = sem(kind + "_rstd")
                self.rstd_parts = sem(kind + "_rstd_parts")
                self.rstd_turned = sem(kind + "_rstd_turned")
                self.rstd_row = sem(kind + "_rstd_row")
                self.rstd_full = sem(kind + "_rstd_full")

        ln_stats, rms_stats, gn_stats = Stats("ln"), Stats("rms"), Stats("gn")
        centred, scaled, affine_done = sem("centred"), sem("scaled"), sem("affine_done")
        rope_e_loaded = sem("rope_e_loaded")
        lam_sum, lam_exp = sem("lam_sum"), sem("lam_exp")
        raw_hi, raw_lo, swap_full, rot_ready = (sem(n) for n in (
            "raw_hi", "raw_lo", "swap_full", "rot_ready"))
        e_v_hi, e_v_ready = sem("e_v_hi"), sem("e_v_ready")
        cc_copied, u_full, conv_ready = (sem(n) for n in (
            "cc_copied", "u_full", "conv_ready"))
        score_full, bias_ready, exp_done, mixed = (sem(n) for n in (
            "score_full", "bias_ready", "exp_done", "mixed"))
        at_full, at_hi_ready, at_ready, pv_full = (sem(n) for n in (
            "at_full", "at_hi_ready", "at_ready", "pv_full"))
        ao_copied, ao_squared, attn_ready = (sem(n) for n in ("ao_copied", "ao_squared", "attn_ready"))
        table_o_loaded = sem("table_o_loaded")
        o_rot_ready, o_v_hi, o_v_ready, o_out_half = (sem(n) for n in (
            "o_rot_ready", "o_v_hi", "o_v_ready", "o_out_half"))
        ret_full, m_ready, sg_done, y_full, y_copied, y_squared = (sem(n) for n in (
            "ret_full", "m_ready", "sg_done", "y_full", "y_copied", "y_squared"))
        gn_sum, gn_sumsq, y_ready, z_scaled = (sem(n) for n in ("gn_sum", "gn_sumsq", "y_ready", "z_scaled"))
        stored = sem("stored")

        Z_AT = {0: 0, 1: 10, 2: 20, 3: 30, 4: 40 + 24, 5: 50 + 24}
        X_AT = {"ffn0": 0, "even": DC, "ffn1": 2 * DC, "ffn2": 3 * DC, "odd": 4 * DC, "ffn3": 5 * DC}
        block = ctx.enter_context(nc.Block())

        @block.sync
        def _(sp):
            def load(u, slot):
                sp.dma_start(raw[:, slot, :], stream[bass.ds(u, 1), :, :].rearrange("a p n -> (a p) n")).then_inc(raw_loaded[slot], 16)

            load(0, 0)
            for c in range(DC):
                sp.dma_start(z[:, c, :], x_in[c]).then_inc(x_loaded[c], 16)
            load(1, 1)
            load(2, 2)
            sp.dma_start(const[:, :], const_in).then_inc(const_loaded, 16)
            load(3, 3)
            with sp.Fori(1, UNITS // RING) as i:
                for s in range(RING):
                    sp.wait_ge(w_ready, RING * i + (s + 1 - RING))
                    load(RING * i + s, s)
            for c in range(DC):
                sp.wait_ge(affine_done, DC * LAST_LN + c + 1)
                sp.dma_start(out[c], z[:, c, :]).then_inc(stored, 16)
            sp.wait_ge(stored, 16 * DC)

        @block.gpsimd
        def _(pool):
            def low_part(u, slot):
                pool.wait_ge(w_hi_ready, u + 1)
                nc.gpsimd.tensor_tensor(w_lo[:, slot, :], raw[:, slot, :], w_hi[:, slot, :].bitcast(F32),
                                        ALU.subtract).then_inc(w_ready, 1)

            with pool.Fori(0, UNITS // RING) as i:
                for s in range(RING):
                    low_part(RING * i + s, s)

        @block.scalar
        def _(act):
            def cast(u, loads, slot, free=True):
                act.wait_ge(raw_loaded[slot], 16 * (loads + 1))
                if free:
                    act.wait_ge(w_used, u + (1 - RING))
                nc.scalar.copy(w_hi[:, slot, :], raw[:, slot, :]).then_inc(w_hi_ready, 1)

            def cast_after(u):
                if u + RING < UNITS:
                    cast(u + RING, u // RING + 1, u % RING)

            for u in range(RING):
                cast(u, 0, u, free=False)
                if u == 0:
                    for c in range(DC):
                        act.wait_ge(x_loaded[c], 16)
                        nc.scalar.copy(x_hi[:, c, :], z[:, c, :]).then_inc(x_hi_ready, 1)
            act.wait_ge(lam_sum, 2)
            nc.scalar.activation(lam[:, 2:4], lam[:, 0:2], ACT.Exp).then_inc(lam_exp, 1)

            def square_z(ln, oc, slot):
                act.wait_ge(z_full, oc + (Z_AT[ln] + 3))
                zo = z[:, bass.ds(oc, 1), :].rearrange("p a t -> p (a t)")
                nc.scalar.activation(square[:, slot, :], zo, ACT.Square).then_inc(square_full, 1)

            def ffn_in(n):
                b = FFN_AT[n]

                def pair(j, u_loads, s):
                    act.wait_ge(w_used, 2 * j + (b + 1))
                    nc.scalar.activation(silu_g[:, s // 2, :], bank[s][:], ACT.Silu).then_inc(silu_done, 1)
                    for k in range(2):
                        cast(2 * j + (b + k + RING), u_loads + 1, s + k)

                for p in range(2):
                    pair(p, b // RING, 2 * p)
                with act.Fori(1, FC // 2) as i:
                    for p in range(2):
                        pair(2 * i + p, b // RING + i, 2 * p)

            def ffn_out(n):
                b = FFN_AT[n] + 2 * FC
                ln = FFN_LN[n]
                if n < 3:
                    with act.Fori(0, 2) as i:
                        for q in range(4):
                            for k in range(OUT_UNITS):
                                r = OUT_UNITS * q + k
                                if k == OUT_UNITS - 1:
                                    square_z(ln, 4 * i + q, q % 2)
                                cast(12 * i + (b + r + RING), 3 * i + ((b + r) // RING + 1), r % RING)
                else:
                    for oc in range(DC):
                        for k in range(OUT_UNITS):
                            if k == OUT_UNITS - 1:
                                square_z(ln, oc, oc % 2)
                            cast_after(b + OUT_UNITS * oc + k)

            def copy_row(ready, done, n, row, b):
                act.wait_ge(ready, n)
                nc.scalar.copy(row[:], bank[b][0:8, 0:P]).then_inc(done, 1)

            def root(st, n):
                act.wait_ge(st.inv_var, n)
                nc.scalar.activation(rstd, inv_var, ACT.Sqrt).then_inc(st.rstd, 1)

            def layer_norm(ln):
                st = ln_stats
                copy_row(st.mean_turned, st.mean_row, ln + 1, row_mean, 7)
                root(st, ln + 1)
                copy_row(st.rstd_turned, st.rstd_row, ln + 1, row_rstd, 6)
                g, b = CONST["ln_g"][0] + DC * ln, CONST["ln_b"][0] + DC * ln
                for c in range(DC):
                    act.wait_ge(scaled, DC * ln + c + 1)
                    gain = {"bias": const[:, b + c:b + c + 1], "scale": const[:, g + c:g + c + 1]}
                    if ln != LAST_LN:
                        nc.scalar.activation(x_hi[:, c, :], z[:, c, :], ACT.Identity, **gain).then_inc(x_hi_ready, 1)
                        act.wait_ge(x_hi_ready, DC * (ln + 1) + c + 1)
                    nc.scalar.activation(z[:, c, :], z[:, c, :], ACT.Identity, **gain).then_inc(affine_done, 1)

            def even():
                b = EVEN_AT
                for t in range(8):
                    act.wait_ge(w_used, b + t + 1)
                    if t >= 2:
                        act.wait_ge(swap_full, t - 1)
                    nc.scalar.copy(qr_hi[:, t % 2, :], bank[t][:]).then_inc(raw_hi, 1)
                    cast_after(b + t)
                for k in range(4):
                    cast_after(b + 8 + k)
                for t in range(TB):
                    act.wait_ge(w_used, b + 12)
                    nc.scalar.copy(v_hi[:, t, :], bank[t][:]).then_inc(e_v_hi, 1)
                for i in range(6):
                    for s in range(8 if i < 5 else 5):
                        if 1 <= i <= 4 and s == 0:
                            cast_after(b + 12 + 3 * i - 1)
                        if i < 4 and s in (3, 6):
                            cast_after(b + 12 + 3 * i + s // 3 - 1)
                        if i < 4 and s == 3:
                            act.wait_ge(w_used, b + 12 + 3 * i + 1)
                            if i:
                                act.wait_ge(u_full, i)
                            nc.scalar.copy(cc_sb[:], bank[0][:]).then_inc(cc_copied, 1)
                        if i < 4:
                            j, q = s // TB, s % TB
                            act.wait_ge(bias_ready, 8 * i + s + 1)
                            if i:
                                act.wait_ge(mixed, TB * (i - 1) + q + 1)
                            nc.scalar.activation(prob[:, j, SPAN_AT[q]:SPAN_AT[q] + SPAN[q]],
                                                 bank[4 + s % 2][:, 0:SPAN[q]], ACT.Exp,
                                                 bias=e_max[:, s % 2:s % 2 + 1],
                                                 accum_out=e_sum[:, i % 2, s:s + 1]).then_inc(exp_done, 1)
                        if 1 <= i <= 4 and 4 <= s <= 6:
                            g = s - 4
                            a, n = REST_AT[g], REST[g] if g < 2 else TRI - REST_AT[2]
                            act.wait_ge(at_full, 3 * (i - 1) + g + 1)
                            nc.scalar.copy(at_hi[:, a:a + n], bank[6][:, 0:n]).then_inc(at_hi_ready, 1)
                        if i >= 2 and s == 0:
                            act.wait_ge(pv_full, i - 1)
                            if i >= 3:
                                act.wait_ge(attn_ready, i - 2)
                            nc.scalar.copy(ao_sb[:], bank[7][:]).then_inc(ao_copied, 1)
                            nc.scalar.activation(square[:, 0, :], bank[7][:], ACT.Square).then_inc(ao_squared, 1)
                        if i >= 2 and s == 1:
                            root(rms_stats, i - 1)
                        if i >= 2 and s == 3:
                            copy_row(rms_stats.rstd_turned, rms_stats.rstd_row, i - 1, row_rstd, 3)
                for oc in range(DC):
                    square_z(EVEN_LN, oc, oc % 2)
                    cast_after(b + 24 + oc)

            def odd():
                b = ODD_AT

                def head(h, u0, loads):
                    first = isinstance(h, int)
                    w, k0 = (0, 4) if first else (4, 8)
                    for k in range(4 + w + 4):
                        cast(u0 + (k + RING), loads + (k // RING + 1), k % RING)
                    for t in range(TB):
                        act.wait_ge(w_used, u0 + (4 + w + 4))
                        nc.scalar.copy(rv_hi[:, t, :], bank[4 + t][:]).then_inc(o_v_hi, 1)
                    for c, gb in enumerate((4, 1, 4, 1)):
                        act.wait_ge(w_used, u0 + (k0 + 4 + c + 1))
                        nc.scalar.activation(sg[:, c, :], bank[gb][:], ACT.Silu).then_inc(sg_done, 1)
                        k = k0 + 4 + c
                        cast(u0 + (k + RING), loads + (k // RING + 1), k % RING)
                        if c == 0:
                            for y, yb in enumerate((5, 6, 7, 0)):
                                act.wait_ge(y_full, 4 * h + y + 1)
                                nc.scalar.copy(y_f[:, y, :], bank[yb][:]).then_inc(y_copied, 1)
                                if y >= 2:
                                    act.wait_ge(gn_sumsq, 3 * h + y - 1)
                                nc.scalar.activation(square[:, y % 2, :], bank[yb][:],
                                                     ACT.Square).then_inc(y_squared, 1)
                        if c == 1:
                            copy_row(gn_stats.mean_turned, gn_stats.mean_row, h + 1, row_mean, 3)
                            root(gn_stats, h + 1)
                            copy_row(gn_stats.rstd_turned, gn_stats.rstd_row, h + 1, row_rstd, 2)

                head(0, b, b // RING)
                with act.Fori(1, HEADS) as h:
                    head(h, 16 * h + (b - 4), 4 * h + (b - 4) // RING)
                for oc in range(DC):
                    square_z(ODD_LN, oc, oc % 2)
                    if oc % 2:
                        cast_after(b + 60 + oc // 2)

            ffn_in(0)
            ffn_out(0)
            act.dma_start(rope_e[:, :, :], rope_even).then_inc(rope_e_loaded, 16)
            layer_norm(0)
            even()
            layer_norm(1)
            ffn_in(1)
            ffn_out(1)
            layer_norm(2)
            ffn_in(2)
            ffn_out(2)
            act.dma_start(rope_o[:, :, :], rope_odd).then_inc(table_o_loaded, 16)
            act.dma_start(decay[:, :, :], decay_in).then_inc(table_o_loaded, 16)
            layer_norm(3)
            odd()
            layer_norm(4)
            ffn_in(3)
            ffn_out(3)
            layer_norm(5)

        @block.vector
        def _(dve):
            class Chain:
                n = 0

                def link(self, ins):
                    ins.then_inc(chain_sem, 1)
                    self.n = self.n + 1
                    dve.wait_ge(chain_sem, self.n)

            chain = Chain()
            link = chain.link

            def loop(lo, hi, per, body):
                start = chain.n
                with dve.Fori(lo, hi) as i:
                    chain.n = (i - lo) * per + start
                    body(i)
                    last = chain.n
                chain.n = start + (hi - lo) * per
                return last

            for c in range(DC):
                dve.wait_ge(x_hi_ready, c + 1)
                nc.vector.tensor_tensor(x_lo[:, c, :], z[:, c, :], x_hi[:, c, :].bitcast(F32),
                                        ALU.subtract).then_inc(x_ready, 1)
            dve.wait_ge(const_loaded, 16)
            nc.vector.tensor_copy(swap[:], cst("swap")).then_inc(const_ready, 1)
            nc.vector.tensor_copy(ident_r[:], ident).then_inc(const_ready, 1)
            nc.vector.tensor_copy(mask[:], cst("mask")).then_inc(const_ready, 1)
            nc.vector.tensor_copy(rows[:], cst("rows")[0:8, :]).then_inc(const_ready, 1)
            la = CONST["lam"][0]
            for k in range(2):
                link(nc.vector.tensor_tensor(square[:, k, 0:64], const[:, la + 128 * k:la + 128 * k + 64],
                                             const[:, la + 128 * k + 64:la + 128 * k + 128], ALU.mult))
                nc.vector.reduce_sum(lam[:, k:k + 1], square[:, k, 0:64], AX_X).then_inc(lam_sum, 1)
            dve.wait_ge(lam_exp, 1)
            link(nc.vector.tensor_tensor(lam[:, 4:5], lam[:, 3:4], lam[:, 2:3], ALU.subtract))
            link(nc.vector.tensor_scalar(lam[:, 5:6], lam[:, 4:5], -LAMBDA_INIT, None, ALU.add))
            link(nc.vector.tensor_scalar(lam[:, 6:7], cst("norm_g"), 1.0 - LAMBDA_INIT, None, ALU.mult))

            def ffn_in(n):
                clear_sums(FFN_LN[n])

                def pair(j, p):
                    g = FC * n + j
                    dve.wait_ge(silu_done, g + 1)
                    dve.wait_ge(w_used, 2 * j + (FFN_AT[n] + 2))
                    dve.wait_ge(h_ready, g)
                    nc.vector.scalar_tensor_tensor(out=h_f[:], in0=silu_g[:, p, :], scalar=0.5,
                                                   in1=bank[2 * p + 1][:], op0=ALU.mult,
                                                   op1=ALU.mult).then_inc(h_full, 1)
                    dve.wait_ge(h_full, g + 1)
                    hj = h_hi[:, bass.ds(j, 1), :].rearrange("p a t -> p (a t)")
                    nc.vector.tensor_copy(hj, h_f[:]).then_inc(h_hi_ready, 1)
                    dve.wait_ge(h_hi_ready, g + 1)
                    nc.vector.tensor_tensor(h_lo[:, bass.ds(j, 1), :].rearrange("p a t -> p (a t)"), h_f[:],
                                            hj.bitcast(F32), ALU.subtract).then_inc(h_ready, 1)

                for p in range(2):
                    pair(p, p)
                with dve.Fori(1, FC // 2) as i:
                    for p in range(2):
                        pair(2 * i + p, p)

            def clear_sums(ln):
                if ln:
                    dve.wait_ge(ln_stats.squares, ln)
                dve.wait_ge(x_ready, DC * (ln + 1))
                dve.wait_ge(sumsq_full, (DC - 1) * ln)
                nc.vector.memset(acc_sum[:], 0.0).then_inc(z_full, 1)
                nc.vector.memset(acc_sq[:], 0.0).then_inc(z_full, 1)
                dve.wait_ge(z_full, Z_AT[ln] + 2)

            def out_chunk(ln, oc, slot, b, scale=ALPHA):
                zo = z[:, bass.ds(oc, 1), :].rearrange("p a t -> p (a t)")
                nc.vector.scalar_tensor_tensor(out=zo, in0=zo, scalar=scale, in1=bank[b][:], op0=ALU.mult,
                                               op1=ALU.add).then_inc(z_full, 1)
                if isinstance(oc, int) and oc == DC - 1:
                    return
                dve.wait_ge(z_full, oc + (Z_AT[ln] + 3))
                nc.vector.tensor_tensor(acc_sum[:], acc_sum[:], zo, ALU.add).then_inc(sum_full, 1)
                dve.wait_ge(square_full, oc + (DC * ln + 1))
                nc.vector.tensor_tensor(acc_sq[:], acc_sq[:], square[:, slot, :], ALU.add).then_inc(sumsq_full, 1)

            def ffn_out(n):
                ln = FFN_LN[n]

                def chunk(oc, q):
                    dve.wait_ge(w_used, OUT_UNITS * oc + (FFN_AT[n] + 2 * FC + OUT_UNITS))
                    out_chunk(ln, oc, q, 4 + q)

                with dve.Fori(0, DC // 2 - 1) as i:
                    for q in range(2):
                        chunk(2 * i + q, q)
                for q in range(2):
                    chunk(DC - 2 + q, q)

            def hi_lo(values, parts, done):
                link(nc.vector.tensor_copy(parts[:, 0:4].bitcast(F32R), values))
                nc.vector.tensor_tensor(parts[:, 4:8], values, parts[:, 0:4], ALU.subtract).then_inc(done, 1)

            def mean_of(st, n, b):
                dve.wait_ge(st.sums, n)
                link(nc.vector.tensor_copy(mean, bank[b][:, 0:8:2]))
                hi_lo(mean, parts_mean, st.mean_parts)
                link(nc.vector.tensor_tensor(mean2, mean, mean, ALU.mult))

            def variance_of(st, n, b):
                dve.wait_ge(st.squares, n)
                link(nc.vector.scalar_tensor_tensor(out=mean2, in0=bank[b][:, 0:8:2], scalar=EPS, in1=mean2,
                                                    op0=ALU.add, op1=ALU.subtract))
                link(nc.vector.tensor_scalar(mean2, mean2, EPS, None, ALU.max))
                link_inv(st, n)

            def link_inv(st, n):
                nc.vector.reciprocal(inv_var, mean2).then_inc(st.inv_var, 1)
                dve.wait_ge(st.inv_var, n)
                dve.wait_ge(st.rstd, n)
                hi_lo(rstd, parts_rstd, st.rstd_parts)

            def layer_norm(ln):
                mean_of(ln_stats, ln + 1, 7)
                variance_of(ln_stats, ln + 1, 6)

                def centre(c):
                    nc.vector.tensor_tensor(z[:, c, :], z[:, c, :], bank[7][:], ALU.subtract).then_inc(centred, 1)

                def low(c):
                    dve.wait_ge(affine_done, DC * ln + c + 1)
                    nc.vector.tensor_tensor(x_lo[:, c, :], z[:, c, :], x_hi[:, c, :].bitcast(F32),
                                            ALU.subtract).then_inc(x_ready, 1)

                dve.wait_ge(ln_stats.mean_full, ln + 1)
                centre(0)
                dve.wait_ge(ln_stats.rstd_full, ln + 1)
                for c in range(DC):
                    dve.wait_ge(centred, DC * ln + c + 1)
                    nc.vector.tensor_tensor(z[:, c, :], z[:, c, :], bank[6][:], ALU.mult).then_inc(scaled, 1)
                    if c + 1 < DC:
                        centre(c + 1)
                    if c and ln != LAST_LN:
                        low(c - 1)
                if ln != LAST_LN:
                    low(DC - 1)

            def even():
                dve.wait_ge(rope_e_loaded, 16)

                def unrotated(t):
                    dve.wait_ge(raw_hi, t + 1)
                    nc.vector.tensor_tensor(qr_lo[:, t % 2, :], bank[t][:], qr_hi[:, t % 2, :].bitcast(F32),
                                            ALU.subtract).then_inc(raw_lo, 1)
                    nc.vector.tensor_tensor(qr_cos[:, t % 2, :], bank[t][:], rope_e[:, 2 * (t % 2), :],
                                            ALU.mult).then_inc(raw_lo, 1)

                def rotated(t):
                    hi, lo = (q_hi, q_lo) if t % 2 == 0 else (k_hi, k_lo)
                    dve.wait_ge(swap_full, t + 1)
                    dve.wait_ge(rot_ready, t)
                    link(nc.vector.tensor_tensor(qr_sin[:], bank[t][:], rope_e[:, 2 * (t % 2) + 1, :], ALU.mult))
                    dve.wait_ge(raw_lo, 2 * t + 2)
                    link(nc.vector.tensor_tensor(qr_sin[:], qr_sin[:], qr_cos[:, t % 2, :], ALU.add))
                    link(nc.vector.tensor_copy(hi[:, t // 2, :], qr_sin[:]))
                    nc.vector.tensor_tensor(lo[:, t // 2, :], qr_sin[:], hi[:, t // 2, :].bitcast(F32),
                                            ALU.subtract).then_inc(rot_ready, 1)

                unrotated(0)
                unrotated(1)
                for t in range(6):
                    rotated(t)
                    unrotated(t + 2)
                rotated(6)
                rotated(7)
                link(nc.vector.memset(u_sb[:, 0:2], 0.0))
                for t in range(TB):
                    dve.wait_ge(e_v_hi, t + 1)
                    nc.vector.tensor_tensor(v_lo[:, t, :], bank[t][:], v_hi[:, t, :].bitcast(F32),
                                            ALU.subtract).then_inc(e_v_ready, 1)
                cw = CONST["conv_w"][0]

                def conv_w(k, i):
                    return const[:, cw + 4 * k + i:cw + 4 * k + i + 1]

                def conv_product(i):
                    dve.wait_ge(cc_copied, i + 1)
                    dve.wait_ge(w_used, EVEN_AT + 12 + 3 * i + 2)
                    nc.vector.tensor_tensor(u_sb[:, 2:T + 2], cc_sb[:], bank[1][:], ALU.mult).then_inc(u_full, 1)
                    dve.wait_ge(u_full, i + 1)
                    dve.wait_ge(conv_ready, i)
                    link(nc.vector.tensor_scalar(y_sb[:], u_sb[:, 2:T + 2], conv_w(2, i), None, ALU.mult))
                    for k in (1, 0):
                        link(nc.vector.scalar_tensor_tensor(out=y_sb[:], in0=u_sb[:, k:T + k], scalar=conv_w(k, i),
                                                            in1=y_sb[:], op0=ALU.mult, op1=ALU.add))

                def conv_gate(i):
                    dve.wait_ge(w_used, EVEN_AT + 12 + 3 * i + 3)
                    dve.wait_ge(score_full, 8 * i + 8)
                    link(nc.vector.tensor_tensor(y_sb[:], y_sb[:], bank[2][:], ALU.mult))
                    link(nc.vector.tensor_copy(q_hi[:, i, :], y_sb[:]))
                    nc.vector.tensor_tensor(q_lo[:, i, :], y_sb[:], q_hi[:, i, :].bitcast(F32),
                                            ALU.subtract).then_inc(conv_ready, 1)

                def score(i, s):
                    dve.wait_ge(score_full, 8 * i + s + 1)
                    if 8 * i + s >= 2:
                        dve.wait_ge(exp_done, 8 * i + s - 1)
                        dve.wait_ge(bias_ready, 8 * i + s - 1)
                    nc.vector.reduce_max(e_max[:, s % 2:s % 2 + 1], bank[4 + s % 2][:, 0:SPAN[s % TB]], AX_X,
                                         negate=True).then_inc(bias_ready, 1)

                def mix(h, q):
                    if q == 0:
                        dve.wait_ge(exp_done, 8 * h + 8)
                        dve.wait_ge(mixed, TB * h)
                        link(nc.vector.reciprocal(e_rec[:], e_sum[:, h % 2, :]))
                        link(nc.vector.tensor_scalar(e_rec[:, 4:8], e_rec[:, 4:8], lam[:, 5:6], None, ALU.mult))
                        if h:
                            dve.wait_ge(at_full, 3 * h)
                    a, n = SPAN_AT[q], SPAN[q]
                    link(nc.vector.tensor_scalar(prob[:, 1, a:a + n], prob[:, 1, a:a + n], e_rec[:, 4 + q:5 + q], None,
                                                 ALU.mult))
                    nc.vector.scalar_tensor_tensor(out=a_sb[:, a:a + n], in0=prob[:, 0, a:a + n],
                                                   scalar=e_rec[:, q:q + 1], in1=prob[:, 1, a:a + n],
                                                   op0=ALU.mult, op1=ALU.add).then_inc(mixed, 1)

                for i in range(6):
                    for s in range(8 if i < 5 else 5):
                        if i < 4:
                            score(i, s)
                        if 1 <= i <= 4 and s < 4:
                            mix(i - 1, s)
                        if 1 <= i <= 4 and s == 0:
                            conv_gate(i - 1)
                        if i < 4 and s == 6:
                            conv_product(i)
                        if 1 <= i <= 4 and 4 <= s <= 6:
                            g = s - 4
                            a, n = REST_AT[g], REST[g] if g < 2 else TRI - REST_AT[2]
                            dve.wait_ge(at_hi_ready, 3 * (i - 1) + g + 1)
                            nc.vector.tensor_tensor(at_lo[:, a:a + n], bank[6][:, 0:n], at_hi[:, a:a + n].bitcast(F32),
                                                    ALU.subtract).then_inc(at_ready, 1)
                        if i >= 2 and s == 1:
                            dve.wait_ge(rms_stats.squares, i - 1)
                            link(nc.vector.tensor_scalar(mean2, bank[3][:, 0:8:2], EPS, None, ALU.add))
                            link_inv(rms_stats, i - 1)
                        if i >= 2 and s == 4:
                            h = i - 2
                            dve.wait_ge(rms_stats.rstd_full, h + 1)
                            dve.wait_ge(ao_copied, h + 1)
                            link(nc.vector.tensor_tensor(ao_sb[:], ao_sb[:], bank[3][:], ALU.mult))
                            link(nc.vector.tensor_scalar(k_hi[:, h, :], ao_sb[:], lam[:, 6:7], None, ALU.mult))
                            nc.vector.scalar_tensor_tensor(out=k_lo[:, h, :], in0=ao_sb[:], scalar=lam[:, 6:7],
                                                           in1=k_hi[:, h, :].bitcast(F32), op0=ALU.mult,
                                                           op1=ALU.subtract).then_inc(attn_ready, 1)
                clear_sums(EVEN_LN)
                for oc in range(DC):
                    dve.wait_ge(w_used, EVEN_AT + 24 + oc + 1)
                    out_chunk(EVEN_LN, oc, oc % 2, (0, 1, 4, 5)[oc % 4])

            def odd():
                dve.wait_ge(table_o_loaded, 32)
                dve.wait_ge(x_ready, DC * (ODD_LN))
                for c in range(DC):
                    nc.vector.tensor_scalar(z[:, c, :], z[:, c, :], ALPHA, None, ALU.mult).then_inc(z_scaled, 1)
                rg = CONST["ret_g"][0]

                def head(h):
                    first = isinstance(h, int)
                    u0 = ODD_AT if first else 16 * h + (ODD_AT - 4)
                    cos, sin = rope_o[:, 0, :], rope_o[:, 1, :]
                    for b0, hi, lo in ((0, rq_hi, rq_lo), (2, rk_hi, rk_lo)):
                        dve.wait_ge(w_used, u0 + (b0 + 2))
                        for k, op in ((0, ALU.subtract), (1, ALU.add)):
                            dve.wait_ge(o_rot_ready, 4 * h + (b0 + k))
                            link(nc.vector.tensor_tensor(r_t[:, 0, :], bank[b0 + k][:], cos, ALU.mult))
                            link(nc.vector.tensor_tensor(r_t[:, 1, :], bank[b0 + 1 - k][:], sin, ALU.mult))
                            link(nc.vector.tensor_tensor(r_t[:, 0, :], r_t[:, 0, :], r_t[:, 1, :], op))
                            link(nc.vector.tensor_copy(hi[:, k, :], r_t[:, 0, :]))
                            nc.vector.tensor_tensor(lo[:, k, :], r_t[:, 0, :], hi[:, k, :].bitcast(F32),
                                                    ALU.subtract).then_inc(o_rot_ready, 1)
                    if not first:
                        for oc in range(DC):
                            if oc % 2 == 0:
                                dve.wait_ge(o_out_half, 4 * h + (oc // 2 - 3))
                            else:
                                dve.wait_ge(w_used, u0 + (4 + oc // 2 + 1))
                            dve.wait_ge(z_scaled, oc + 1)
                            nc.vector.tensor_tensor(z[:, oc, :], z[:, oc, :], bank[OUT_BANKS[oc % 4]][:],
                                                    ALU.add).then_inc(z_full, 1)

                    def value_parts():
                        for t in range(TB):
                            dve.wait_ge(o_v_hi, TB * h + t + 1)
                            nc.vector.tensor_tensor(rv_lo[:, t, :], bank[4 + t][:], rv_hi[:, t, :].bitcast(F32),
                                                    ALU.subtract).then_inc(o_v_ready, 1)

                    if first:
                        value_parts()
                    for k in range(TB):
                        n, a = REST[k], REST_AT[k]
                        dve.wait_ge(ret_full, TB * h + k + 1)
                        dve.wait_ge(m_ready, TB * h + k)
                        link(nc.vector.tensor_tensor(m_f[:, 0:n], bank[k][:, 0:n],
                                                     decay[:, bass.ds(h, 1), 0:n].rearrange("p a t -> p (a t)"),
                                                     ALU.mult))
                        link(nc.vector.tensor_copy(m_hi[:, a:a + n], m_f[:, 0:n]))
                        nc.vector.tensor_tensor(m_lo[:, a:a + n], m_f[:, 0:n], m_hi[:, a:a + n].bitcast(F32),
                                                ALU.subtract).then_inc(m_ready, 1)
                    if not first:
                        value_parts()
                    for c in range(1, 4):
                        dve.wait_ge(y_copied, 4 * h + c + 1)
                        dve.wait_ge(gn_sum, 3 * h + (c - 1))
                        nc.vector.tensor_tensor(acc_sum[:], y_f[:, 0, :] if c == 1 else acc_sum[:], y_f[:, c, :],
                                                ALU.add).then_inc(gn_sum, 1)
                        dve.wait_ge(y_squared, 4 * h + c + 1)
                        dve.wait_ge(gn_sumsq, 3 * h + (c - 1))
                        nc.vector.tensor_tensor(acc_sq[:], square[:, 0, :] if c == 1 else acc_sq[:],
                                                square[:, c % 2, :], ALU.add).then_inc(gn_sumsq, 1)
                    mean_of(gn_stats, h + 1, 3)
                    variance_of(gn_stats, h + 1, 2)
                    dve.wait_ge(gn_stats.mean_full, h + 1)
                    link(nc.vector.tensor_tensor(y_f[:, 0, :], y_f[:, 0, :], bank[3][:], ALU.subtract))
                    dve.wait_ge(gn_stats.rstd_full, h + 1)
                    for c in range(4):
                        if c:
                            link(nc.vector.tensor_tensor(y_f[:, c, :], y_f[:, c, :], bank[3][:], ALU.subtract))
                        link(nc.vector.tensor_tensor(y_f[:, c, :], y_f[:, c, :], bank[2][:], ALU.mult))
                        dve.wait_ge(sg_done, 4 * h + c + 1)
                        link(nc.vector.scalar_tensor_tensor(out=y_f[:, c, :], in0=y_f[:, c, :],
                                                            scalar=const[:, bass.ds(4 * h + (rg + c), 1)],
                                                            in1=sg[:, c, :], op0=ALU.mult, op1=ALU.mult))
                        link(nc.vector.tensor_copy(y_hi[:, c, :], y_f[:, c, :]))
                        nc.vector.tensor_tensor(y_lo[:, c, :], y_f[:, c, :], y_hi[:, c, :].bitcast(F32),
                                                ALU.subtract).then_inc(y_ready, 1)

                before = chain.n
                head(0)
                loop(1, HEADS, chain.n - before, head)
                clear_sums(ODD_LN)
                for oc in range(DC):
                    if oc % 2 == 0:
                        dve.wait_ge(o_out_half, 4 * 3 + oc // 2 + 1)
                    else:
                        dve.wait_ge(w_used, ODD_AT + 60 + oc // 2 + 1)
                    out_chunk(ODD_LN, oc, oc % 2, OUT_BANKS[oc % 4], scale=1.0)

            ffn_in(0)
            ffn_out(0)
            layer_norm(0)
            even()
            layer_norm(1)
            ffn_in(1)
            ffn_out(1)
            layer_norm(2)
            ffn_in(2)
            ffn_out(2)
            layer_norm(3)
            odd()
            layer_norm(4)
            ffn_in(3)
            ffn_out(3)
            layer_norm(5)

        @block.tensor
        def _(pe):
            def mm3(o, a, b, start, stop):
                nc.tensor.matmul(o, a[0], b[0], start=start, stop=False)
                nc.tensor.matmul(o, a[0], b[1], start=False, stop=False)
                return nc.tensor.matmul(o, a[1], b[0], start=False, stop=stop)

            def w(slot, blk):
                c = slice(blk * P, (blk + 1) * P)
                return w_hi[:, slot, c], w_lo[:, slot, c]

            def x(c):
                return x_hi[:, c, :], x_lo[:, c, :]

            def part(hi, lo, *at):
                return hi[:, *at], lo[:, *at]

            def unit(u):
                pe.wait_ge(w_ready, u + 1)

            def first_four(u0, x_at):
                for c in range(DC):
                    pe.wait_ge(x_hi_ready, x_at + c + 1)
                    for s in range(RING):
                        if c == 0:
                            unit(u0 + s)
                        hi, lo = w(s, c)
                        nc.tensor.matmul(bank[s][:], hi, x_hi[:, c, :], start=c == 0, stop=False)
                        nc.tensor.matmul(bank[s][:], lo, x_hi[:, c, :], start=False, stop=False)
                    pe.wait_ge(x_ready, x_at + c + 1)
                    for s in range(RING):
                        last = nc.tensor.matmul(bank[s][:], w(s, c)[0], x_lo[:, c, :], start=False, stop=c == DC - 1)
                        if c == DC - 1:
                            last.then_inc(w_used, 1)

            def project(u, slot, o, x_at=None, between=None):
                unit(u)
                for c in range(DC):
                    if between:
                        between(c)
                    if x_at is not None:
                        pe.wait_ge(x_ready, x_at + c + 1)
                    last = mm3(o, w(slot, c), x(c), c == 0, c == DC - 1)
                last.then_inc(w_used, 1)

            def project_v(u0, o, each=None):
                for k in range(RING):
                    unit(u0 + k)
                    for half in range(2):
                        c = 2 * k + half
                        n = slice(half * T, (half + 1) * T)
                        for t in range(TB):
                            if c == 0 and each:
                                each(t)
                            last = mm3(o[t][:], part(x_hi, x_lo, c, slice(t * P, (t + 1) * P)),
                                       part(w_hi, w_lo, k, n), c == 0, c == DC - 1)
                    last.then_inc(w_used, 1)
                    yield k

            def ffn_in(n):
                b = FFN_AT[n]
                if n == 0:
                    for s in range(RING):
                        project(s, s, bank[s][:], 0)
                else:
                    first_four(b, X_AT[f"ffn{n}"])
                with pe.Fori(1, FC // 2) as i:
                    for s in range(4):
                        if s % 2 == 0:
                            pe.wait_ge(h_full, 2 * i + (FC * n + s // 2 - 1))
                        project(4 * i + (b + s), s, bank[s][:])

            def ffn_out(n):
                b, ln = FFN_AT[n] + 2 * FC, FFN_LN[n]
                with pe.Fori(0, 2) as i:
                    for q in range(4):
                        o = bank[4 + q % 2][:]
                        pe.wait_ge(z_full, 4 * i + (Z_AT[ln] + q + 1))
                        for kc in range(FC):
                            r = OUT_UNITS * q + kc // UB
                            if kc % UB == 0:
                                unit(12 * i + (b + r))
                            if q == 0:
                                pe.wait_ge(h_ready, FC * n + kc + 1)
                            last = mm3(o, w(r % RING, kc % UB), part(h_hi, h_lo, kc), kc == 0, kc == FC - 1)
                            if kc % UB == UB - 1 or kc == FC - 1:
                                last.then_inc(w_used, 1)

            def token_means(o, src, one, first):
                for k in range(TB):
                    last = nc.tensor.matmul(o[:, 2 * k:2 * k + 2], src[:, k * P:(k + 1) * P],
                                            one, start=first and k == 0, stop=False, skip_group_check=True)
                return last

            def turn_parts(parts, done, n, turned, o):
                pe.wait_ge(done, n)
                nc.tensor.transpose(o[0:8, 0:P], parts, ident).then_inc(turned, 1)

            def spread(row_done, n, row, full, o):
                pe.wait_ge(row_done, n)
                for k in range(TB):
                    last = nc.tensor.matmul(o[:, k * P:(k + 1) * P], rows[0:8, k * P:(k + 1) * P], row[0:8, :],
                                            start=True, stop=True)
                last.then_inc(full, 1)

            def mean_turn_and_spread(st, n, b):
                turn_parts(parts_mean, st.mean_parts, n, st.mean_turned, bank[b])
                spread(st.mean_row, n, row_mean, st.mean_full, bank[b])

            def rstd_turn(st, n, b):
                turn_parts(parts_rstd, st.rstd_parts, n, st.rstd_turned, bank[b])

            def rstd_spread(st, n, b):
                spread(st.rstd_row, n, row_rstd, st.rstd_full, bank[b])

            def layer_norm(ln):
                one, st = cst("mean_d"), ln_stats
                pe.wait_ge(sum_full, (DC - 1) * (ln + 1))
                token_means(bank[7], acc_sum, one, True)
                pe.wait_ge(sumsq_full, (DC - 1) * (ln + 1))
                token_means(bank[6], acc_sq, one, True)
                pe.wait_ge(z_full, Z_AT[ln] + 2 + DC)
                token_means(bank[7], z[:, DC - 1, :], one, False).then_inc(st.sums, 1)
                pe.wait_ge(square_full, DC * (ln + 1))
                token_means(bank[6], square[:, 1, :], one, False).then_inc(st.squares, 1)
                mean_turn_and_spread(st, ln + 1, 7)
                rstd_turn(st, ln + 1, 6)
                rstd_spread(st, ln + 1, 6)

            def even():
                b = EVEN_AT

                def swap_halves(t):
                    pe.wait_ge(raw_lo, 2 * t + 2)
                    nc.tensor.matmul(bank[t][:], swap[:], qr_hi[:, t % 2, :], start=True, stop=False)
                    nc.tensor.matmul(bank[t][:], swap[:], qr_lo[:, t % 2, :], start=False,
                                     stop=True).then_inc(swap_full, 1)

                pe.wait_ge(const_ready, 4)
                first_four(b, X_AT["even"])
                for t in range(4):
                    project(b + 4 + t, t, bank[4 + t][:])
                    swap_halves(t)
                for k in project_v(b + 8, bank[0:4], lambda t: pe.wait_ge(rot_ready, t + 1)):
                    swap_halves(4 + k)

                def conv_part(i, m):
                    f, c = m // DC, m % DC
                    if c == 0:
                        unit(b + 12 + 3 * i + f)
                        if i == 0:
                            pe.wait_ge(e_v_ready, f + 1)
                        else:
                            pe.wait_ge((cc_copied, u_full, conv_ready)[f], i)
                    last = mm3(bank[f][:], w((3 * i + f) % RING, c), x(c), c == 0, c == DC - 1)
                    if c == DC - 1:
                        last.then_inc(w_used, 1)

                def score(i, s):
                    j, q = s // TB, s % TB
                    if 8 * i + s < 2:
                        pe.wait_ge(rot_ready, 8)
                    else:
                        pe.wait_ge(exp_done, 8 * i + s - 1)
                    r = slice(64 * j, 64 * j + 64)
                    qs, ks = slice(q * P, (q + 1) * P), slice(0, SPAN[q])
                    o = bank[4 + s % 2]
                    mm3(o[:, ks], (q_hi[r, i, qs], q_lo[r, i, qs]), (k_hi[r, i, ks], k_lo[r, i, ks]), True, False)
                    nc.tensor.matmul(o[:, SPAN[q] - P:SPAN[q]], ident_r[:], mask[:], start=False,
                                     stop=True).then_inc(score_full, 1)

                def turn(h, g):
                    pe.wait_ge(mixed, TB * (h + 1))
                    if 3 * h + g:
                        pe.wait_ge(at_ready, 3 * h + g)
                    if h:
                        pe.wait_ge(pv_full, h)
                    for kb in ((0,), (1,), (2, 3))[g]:
                        for q in range(kb, TB):
                            c = REST_AT[kb] - REST_AT[g] + (q - kb) * P
                            last = nc.tensor.transpose(bank[6][:, c:c + P],
                                                       a_sb[:, SPAN_AT[q] + kb * P:SPAN_AT[q] + kb * P + P], ident)
                    last.then_inc(at_full, 1)

                def values(h):
                    pe.wait_ge(at_ready, 3 * h + 3)
                    if h == 0:
                        pe.wait_ge(e_v_ready, TB)
                    else:
                        pe.wait_ge(ao_squared, h)
                    for kb in range(TB):
                        last = mm3(bank[7][:, kb * P:T], part(v_hi, v_lo, kb, slice(h * P, (h + 1) * P)),
                                   part(at_hi, at_lo, slice(REST_AT[kb], REST_AT[kb] + REST[kb])),
                                   kb == 0, kb == TB - 1)
                    last.then_inc(pv_full, 1)

                O = (0, 1, 4, 5)

                def out_part(oc, blk):
                    if blk == 0:
                        unit(b + 24 + oc)
                        if oc >= 4:
                            pe.wait_ge(z_full, Z_AT[EVEN_LN] + 2 + oc - 3)
                        else:
                            pe.wait_ge(*((cc_copied, 4), (u_full, 4), (exp_done, 31), (exp_done, 32))[oc])
                    if blk < 4:
                        pe.wait_ge(conv_ready, blk + 1)
                        src = part(q_hi, q_lo, blk)
                    else:
                        pe.wait_ge(attn_ready, blk - 3)
                        src = part(k_hi, k_lo, blk - 4)
                    last = mm3(bank[O[oc % 4]][:], w(oc % RING, blk), src, blk == 0, blk == UB - 1)
                    if blk == UB - 1:
                        last.then_inc(w_used, 1)

                for i in range(6):
                    for s in range(8 if i < 5 else 5):
                        if i < 4:
                            for m in range(3 * s, 3 * s + 3):
                                conv_part(i, m)
                            score(i, s)
                        elif i == 4:
                            for m in (2 * s, 2 * s + 1):
                                out_part(m // 4, m % 4)
                        else:
                            for m in range(12 * s // 5, 12 * (s + 1) // 5):
                                out_part(m // 3, 4 + m % 3)
                        if 1 <= i <= 4 and 4 <= s <= 6:
                            turn(i - 1, s - 4)
                        if 1 <= i <= 4 and s == 7:
                            values(i - 1)
                        if i >= 2 and s == 1:
                            pe.wait_ge(ao_squared, i - 1)
                            token_means(bank[3], square[:, 0, :], cst("mean_rms"),
                                        True).then_inc(rms_stats.squares, 1)
                        if i >= 2 and s == 3:
                            rstd_turn(rms_stats, i - 1, 3)
                        if i >= 2 and s == 4:
                            rstd_spread(rms_stats, i - 1, 3)
                for oc in range(4):
                    out_part(oc, 7)
                for oc in range(4, DC):
                    for blk in range(UB):
                        out_part(oc, blk)

            def odd():
                b = ODD_AT

                def share(wu, o, c, last_c):
                    last = mm3(bank[OUT_BANKS[(2 * wu + o) % 4]][:], w(wu, 4 * o + c), part(y_hi, y_lo, c),
                               c == 0, c == last_c)
                    if c == last_c:
                        last.then_inc(w_used if o else o_out_half, 1)

                def out_of_head(u0, z_free, units):
                    for wu in units:
                        unit(u0 + wu)
                        for o in range(2):
                            oc = 2 * wu + o
                            if oc >= 4:
                                pe.wait_ge(z_full, z_free + (oc - 3))
                            for c in range(4):
                                share(wu, o, c, 3)

                def head(h, u0):
                    first = isinstance(h, int)
                    if first:
                        first_four(u0, X_AT["odd"])
                        v0 = u0 + 4
                    else:
                        for s, (free, n) in enumerate(((y_squared, 4), (sg_done, 4), (y_ready, 4), (y_ready, 4))):
                            pe.wait_ge(free, n * h)
                            project(u0 + s, s, bank[s][:])
                        z_at = Z_AT[3] + 10
                        out_of_head(u0 + 4, 8 * h + (z_at - 8), range(4))
                        v0 = u0 + 8
                    if first:
                        for _ in project_v(v0, bank[4:8]):
                            pass
                    for kb in range(TB):
                        pe.wait_ge(o_rot_ready, 4 * h + 4)
                        for c in range(2):
                            last = mm3(bank[kb][:, 0:REST[kb]], part(rk_hi, rk_lo, c, slice(kb * P, (kb + 1) * P)),
                                       part(rq_hi, rq_lo, c, slice(kb * P, T)), c == 0, c == 1)
                        last.then_inc(ret_full, 1)
                    if not first:
                        pe.wait_ge(z_full, 8 * h + z_at)
                        for _ in project_v(v0, bank[4:8]):
                            pass
                    g0 = v0 + 4
                    pe.wait_ge(o_v_ready, 4 * h + 1)
                    project(g0, 0, bank[4][:])
                    pe.wait_ge(o_v_ready, 4 * h + 4)
                    pe.wait_ge(m_ready, 4 * h + 4)
                    for c, yb in enumerate((5, 6, 7, 0)):
                        for kb in range(TB):
                            last = mm3(bank[yb][:, kb * P:T], part(rv_hi, rv_lo, kb, slice(c * P, (c + 1) * P)),
                                       part(m_hi, m_lo, slice(REST_AT[kb], REST_AT[kb] + REST[kb])),
                                       kb == 0, kb == TB - 1)
                        last.then_inc(y_full, 1)
                    project(g0 + 1, 1, bank[1][:])
                    pe.wait_ge(gn_sum, 3 * h + 3)
                    token_means(bank[3], acc_sum, cst("mean_dv"), True).then_inc(gn_stats.sums, 1)
                    pe.wait_ge(gn_sumsq, 3 * h + 3)
                    token_means(bank[2], acc_sq, cst("mean_dv"), True).then_inc(gn_stats.squares, 1)
                    mean_turn_and_spread(gn_stats, h + 1, 3)
                    pe.wait_ge(sg_done, 4 * h + 1)
                    project(g0 + 2, 2, bank[4][:], between=lambda c: c == 2 and rstd_turn(gn_stats, h + 1, 2))
                    rstd_spread(gn_stats, h + 1, 2)
                    pe.wait_ge(sg_done, 4 * h + 2)
                    project(g0 + 3, 3, bank[1][:])

                head(0, b)
                with pe.Fori(1, HEADS) as h:
                    head(h, 16 * h + (b - 4))
                pe.wait_ge(y_squared, 4 * HEADS)
                pe.wait_ge(sg_done, 4 * HEADS)
                for wu in range(2):
                    unit(b + 60 + wu)
                for c in range(4):
                    pe.wait_ge(y_ready, 4 * (HEADS - 1) + c + 1)
                    for wu in range(2):
                        for o in range(2):
                            share(wu, o, c, 3)
                out_of_head(b + 60, Z_AT[ODD_LN] + 2, (2, 3))

            ffn_in(0)
            ffn_out(0)
            layer_norm(0)
            even()
            layer_norm(1)
            ffn_in(1)
            ffn_out(1)
            layer_norm(2)
            ffn_in(2)
            ffn_out(2)
            layer_norm(3)
            odd()
            layer_norm(4)
            ffn_in(3)
            ffn_out(3)
            layer_norm(5)


def _weight_stream(ffn_w_in, ffn_w_out, even_w_in, even_w_out, odd_w_in, odd_w_out):
    out = np.zeros((UNITS, P, UB, P), np.float32)
    at = [0]

    def put(blocks):
        out[at[0], :, :len(blocks)] = blocks.transpose(1, 0, 2)
        at[0] += 1

    def columns(wt, c):
        put(wt[:, c:c + P].reshape(DC, P, P))

    def values(wt, c):
        for k in range(RING):
            put(wt[2 * k * P:(2 * k + 2) * P, c:c + T].reshape(2, P, 4, P).transpose(0, 2, 1, 3).reshape(8, P, P))

    def ffn(w_in, w_out):
        for j in range(FC):
            columns(w_in, j * P)
            columns(w_in, FF + j * P)
        for oc in range(DC):
            rows = w_out[:, oc * P:(oc + 1) * P].reshape(FC, P, P)
            for k in range(OUT_UNITS):
                put(rows[UB * k:UB * (k + 1)])

    def even(w_in, w_out):
        for t in range(4):
            columns(w_in, t * P)
            columns(w_in, 512 + t * P)
        values(w_in, 1024)
        for i in range(4):
            for f in (2048, 2560, 1536):
                columns(w_in, f + i * P)
        for oc in range(DC):
            rows = w_out[:, oc * P:(oc + 1) * P].reshape(DC, P, P)
            put(np.concatenate([rows[4:], rows[:4]]))

    def odd(w_in, w_out):
        def share(h):
            rows = w_out[h * T:(h + 1) * T].reshape(4, P, DC, P)
            for wu in range(4):
                put(rows[:, :, 2 * wu:2 * wu + 2].transpose(2, 0, 1, 3).reshape(8, P, P))

        for h in range(HEADS):
            for c in (0, P, D, D + P):
                columns(w_in, c + 256 * h)
            if h:
                share(h - 1)
            values(w_in, 2 * D + T * h)
            for c in range(4):
                columns(w_in, 4 * D + T * h + c * P)
        share(HEADS - 1)

    ffn(ffn_w_in[0, 0], ffn_w_out[0, 0])
    even(even_w_in[0], even_w_out[0])
    ffn(ffn_w_in[0, 1], ffn_w_out[0, 1])
    ffn(ffn_w_in[1, 0], ffn_w_out[1, 0])
    odd(odd_w_in[0], odd_w_out[0])
    ffn(ffn_w_in[1, 1], ffn_w_out[1, 1])
    return out.reshape(UNITS, P, UB * P)


def _rope(half, theta, n_rot):
    inv = np.exp(np.float32(-math.log(theta)) * np.arange(half, dtype=np.float32) * np.float32(2.0 / n_rot))
    ang = inv[:, None].astype(np.float32) * np.arange(T, dtype=np.float32)[None, :]
    return np.cos(ang).astype(np.float32), np.sin(ang).astype(np.float32)


def _tables():
    c, s = _rope(8, 500000.0, 16)
    even = np.zeros((P, 4, T), np.float32)
    even[:, 2] = 1.0
    swap = np.zeros((P, P), np.float32)
    for head in (0, 64):
        even[head:head + 8, 2], even[head + 8:head + 16, 2] = c, c
        even[head:head + 8, 3], even[head + 8:head + 16, 3] = -s, s
        for m in range(8):
            swap[head + m, head + 8 + m] = swap[head + 8 + m, head + m] = 1.0
    even[:, 0:2] = even[:, 2:4] * np.float32(ATTN_SCALE)
    rows = np.zeros((P, TB, P), np.float32)
    for b in range(TB):
        rows[[b, b + 4], b] = 1.0
    c, s = _rope(128, 10000.0, 256)
    odd = np.stack([c, s], 1)
    rel = np.arange(T)[None, :] - np.arange(P)[:, None]
    decay = np.zeros((P, HEADS, T), np.float32)
    for h in range(HEADS):
        decay[:, h] = np.where(rel >= 0, np.exp(np.log1p(-2.0 ** (-5 - h)) * np.maximum(rel, 0)), 0.0) * KEY_SCALE
    mask = np.where(np.arange(P)[None, :] <= np.arange(P)[:, None], 0.0, MASKED).astype(np.float32)
    return even, odd, decay, swap, mask, rows.reshape(P, T)


def kernel(x, ln_g, ln_b, ffn_w_in, ffn_w_out, even_w_in, even_w_out, diff_lambda, diff_norm_g, conv_w,
           odd_w_in, odd_w_out, ret_norm_g):
    import concourse.bacc as bacc
    from concourse.bass_utils import run_bass_kernel_spmd

    even, odd, decay, swap, mask, rows = _tables()
    packed = {
        "ident": np.eye(P), "mean_d": np.full((P, 2), 1.0 / D), "mean_dv": np.full((P, 2), 1.0 / T),
        "mean_rms": np.full((P, 2), 1.0 / P), "swap": swap, "mask": mask, "rows": rows,
        "ln_g": np.asarray(ln_g).reshape(6 * DC, P).T, "ln_b": np.asarray(ln_b).reshape(6 * DC, P).T,
        "conv_w": np.asarray(conv_w).reshape(12, P).T, "norm_g": np.asarray(diff_norm_g).reshape(P, 1),
        "ret_g": np.asarray(ret_norm_g).reshape(16, P).T,
        "lam": np.broadcast_to(np.asarray(diff_lambda).reshape(1, 256), (P, 256)),
    }
    const = np.concatenate([np.asarray(packed[name], np.float32) for name in CONST], 1)
    arrays = {
        "x_t": np.ascontiguousarray(np.asarray(x)[0].T.reshape(DC, P, T)),
        "stream": _weight_stream(*(np.asarray(a) for a in (ffn_w_in, ffn_w_out, even_w_in, even_w_out,
                                                           odd_w_in, odd_w_out))),
        "const": np.ascontiguousarray(const), "rope_even": even, "rope_odd": odd, "decay": decay,
    }
    nc = bacc.Bacc("TRN2", target_bir_lowering=False, num_devices=1)
    args = [nc.dram_tensor(f"in_{n}", a.shape, mybir.dt.from_np(a.dtype), kind="ExternalInput").ap()
            for n, a in arrays.items()]
    out = nc.dram_tensor("out_t", (DC, P, T), F32, kind="ExternalOutput").ap()
    trunk(nc, *args, out)
    r = run_bass_kernel_spmd(nc, [{f"in_{n}": a for n, a in arrays.items()}], core_ids=[0])
    got = np.asarray(r.results[0]["out_t"])
    return np.ascontiguousarray(got.reshape(D, T).T).reshape(1, T, D)
```

```python
from contextlib import ExitStack
import math

import numpy as np
import concourse.bass as bass
from concourse import mybir

F32 = mybir.dt.float32
F32R = mybir.dt.float32r
ALU = mybir.AluOpType
ACT = mybir.ActivationFunctionType
AX_X = mybir.AxisListType.X

P = 128
T = 512
D = 1024
DC = D // P
TB = T // P
FF = 2816
FC = FF // P
UB = 8
RING = 4
OUT_UNITS = -(-FC // UB)
FFN_UNITS = 2 * FC + OUT_UNITS * DC
HEADS = 4
EVEN_UNITS = 24 + DC
ODD_UNITS = 48 + 16
ALPHA = 4.0 ** 0.25
EPS = 1e-5
LAMBDA_INIT = 0.8 - 0.6 * math.exp(0.0)
ATTN_SCALE = 64 ** -0.5
KEY_SCALE = 256 ** -0.5
MASKED = -1e30
SPAN = [(b + 1) * P for b in range(TB)]
SPAN_AT = [sum(SPAN[:b]) for b in range(TB)]
REST = [T - b * P for b in range(TB)]
REST_AT = [sum(REST[:b]) for b in range(TB)]
TRI = sum(REST)
HALF = T // 2
HALVES = (slice(0, HALF), slice(HALF, T))
HALF_BLOCKS = ((0, 1), (2, 3))

FFN_AT = [0, FFN_UNITS + EVEN_UNITS, 2 * FFN_UNITS + EVEN_UNITS, 3 * FFN_UNITS + EVEN_UNITS + ODD_UNITS]
EVEN_AT = FFN_UNITS
ODD_AT = 3 * FFN_UNITS + EVEN_UNITS
UNITS = 4 * FFN_UNITS + EVEN_UNITS + ODD_UNITS
FFN_LN = [0, 2, 3, 5]
EVEN_LN, ODD_LN, LAST_LN = 1, 4, 5

SPLIT_AT = [DC - 1, 6, DC - 1, DC - 1, 4, DC - 1]
SPLIT = [DC - c for c in SPLIT_AT]
UPDATES = [DC + n for n in SPLIT]
UP_AT = [sum(UPDATES[:ln]) for ln in range(6)]
CLEARS = [2, 0, 2, 2, 0, 2]
Z_AT = [UP_AT[ln] + sum(CLEARS[:ln + 1]) + (24 if ln >= ODD_LN else 0) for ln in range(6)]
HALF_AT = [sum(SPLIT[:ln]) + (2 if ln > ODD_LN else 0) for ln in range(6)]
B_SLOTS = [(4,), (1, 3), (4,), (4,), (0, 1, 2, 3), (5,)]
END_SLOT = [slots[-1] + 1 for slots in B_SLOTS]
LAST_UNIT = [FFN_AT[0] + FFN_UNITS, EVEN_AT + EVEN_UNITS, FFN_AT[1] + FFN_UNITS, FFN_AT[2] + FFN_UNITS,
             ODD_AT + ODD_UNITS, FFN_AT[3] + FFN_UNITS]
HELD = [OUT_UNITS, 2, OUT_UNITS, OUT_UNITS, 2, OUT_UNITS]

A_BANKS = [(5,), (4, 5), (5,), (5,), (6, 7, 4, 5), (5,)]
CONV_BANKS = ((6, 7, 2), (0, 1, 2))
NORM_BANKS = ((7, 6), (5, 4))
OUT_BANKS = (5, 6, 7, 4)

RMS_SLOTS = {2: (2, 4, 5), 3: (2, 4, 5), 4: (2, 4, 5), 5: (0, 1, 2)}

CONST = {}
_at = 0
for _name, _n in (("ident", P), ("mean_d", 2), ("mean_dv", 2), ("mean_rms", 2), ("swap", P), ("mask", P),
                  ("rows", T), ("ln_g", 6 * DC), ("ln_b", 6 * DC), ("conv_w", 12), ("norm_g", 1),
                  ("ret_g", 16), ("lam", 256)):
    CONST[_name] = (_at, _n)
    _at += _n
CONST_COLS = _at


def trunk(nc, x_in, stream, const_in, rope_even, rope_odd, decay_in, out):
    with ExitStack() as ctx:
        def sb(name, shape, dt=F32):
            return ctx.enter_context(nc.sbuf_tensor(name, shape, dt))

        def sem(name):
            return ctx.enter_context(nc.semaphore(name))

        bank = [ctx.enter_context(nc.psum_tensor(f"bank{i}", [P, T], F32)) for i in range(8)]

        z = sb("z", [P, DC, T])
        x_hi = sb("x_hi", [P, DC, T], F32R)
        x_lo = sb("x_lo", [P, DC, T], F32R)
        raw = sb("raw", [P, RING, UB * P])
        w_hi = sb("w_hi", [P, RING, UB * P], F32R)
        w_lo = sb("w_lo", [P, RING, UB * P], F32R)
        const = sb("const", [P, CONST_COLS])
        swap = sb("swap", [P, P], F32R)
        ident_r = sb("ident_r", [P, P], F32R)
        mask = sb("mask", [P, P], F32R)
        rows = sb("rows", [8, T], F32R)
        acc_sum = sb("acc_sum", [P, T])
        acc_sq = sb("acc_sq", [P, T])
        square = sb("square", [P, 2, T])
        stat = sb("stat", [P, 40])
        row_mean = sb("row_mean", [8, P], F32R)
        row_rstd = sb("row_rstd", [8, P], F32R)
        lam = sb("lam", [P, 8])

        def cst(name):
            a, n = CONST[name]
            return const[:, a:a + n]

        ident = cst("ident")
        mean, mean2, inv_var, rstd = (stat[:, 4 * k:4 * k + 4] for k in range(4))
        parts_mean, parts_rstd = stat[:, 16:24], stat[:, 24:32]

        class Region:
            def __init__(self, base):
                self.at = base

            def take(self, name, shape, dt=F32):
                t = nc.alloc_sbuf_tensor_at(name, [P] + shape, dt, offset=self.at)
                self.at += -(-4 * math.prod(shape) // 32) * 32
                return t

        arena_cols = (2 * FC + 3) * T
        arena = sb("arena", [P, arena_cols])
        base = nc.lookup_mloc(arena).addr
        ffn = Region(base)
        h_hi = ffn.take("h_hi", [FC, T], F32R)
        h_lo = ffn.take("h_lo", [FC, T], F32R)
        silu_g = ffn.take("silu_g", [2, T])
        h_f = ffn.take("h_f", [T])

        ev = Region(base)
        q_hi = ev.take("q_hi", [HEADS, T], F32R)
        q_lo = ev.take("q_lo", [HEADS, T], F32R)
        k_hi = ev.take("k_hi", [HEADS, T], F32R)
        k_lo = ev.take("k_lo", [HEADS, T], F32R)
        v_hi = ev.take("v_hi", [TB, T], F32R)
        v_lo = ev.take("v_lo", [TB, T], F32R)
        rope_e = ev.take("rope_e", [4, T])
        at_hi = ev.take("at_hi", [TRI], F32R)
        at_lo = ev.take("at_lo", [TRI], F32R)
        cc_sb = ev.take("cc_sb", [T])
        u_sb = ev.take("u_sb", [T + 2])
        y_sb = ev.take("y_sb", [T])
        ao_sb = ev.take("ao_sb", [T])
        e_sum = ev.take("e_sum", [2, 8])
        e_rec = ev.take("e_rec", [8])
        e_max = ev.take("e_max", [2])
        rot_at = ev.at
        prob = ev.take("prob", [2, TRI])
        a_sb = ev.take("a_sb", [TRI])
        ev2 = Region(rot_at)
        qr_hi = ev2.take("qr_hi", [2, T], F32R)
        qr_lo = ev2.take("qr_lo", [2, T], F32R)
        qr_cos = ev2.take("qr_cos", [2, T])
        qr_sin = ev2.take("qr_sin", [T])

        od = Region(base)
        rq_hi = od.take("rq_hi", [2, T], F32R)
        rq_lo = od.take("rq_lo", [2, T], F32R)
        rk_hi = od.take("rk_hi", [2, T], F32R)
        rk_lo = od.take("rk_lo", [2, T], F32R)
        rv_hi = od.take("rv_hi", [TB, T], F32R)
        rv_lo = od.take("rv_lo", [TB, T], F32R)
        m_hi = od.take("m_hi", [TRI], F32R)
        m_lo = od.take("m_lo", [TRI], F32R)
        m_f = od.take("m_f", [T])
        r_t = od.take("r_t", [2, T])
        sg = od.take("sg", [4, T])
        y_f = od.take("y_f", [4, T])
        y_hi = od.take("y_hi", [4, T], F32R)
        y_lo = od.take("y_lo", [4, T], F32R)
        decay = od.take("decay", [HEADS, T])
        rope_o = od.take("rope_o", [2, T])
        for r in (ffn, ev, ev2, od):
            assert r.at <= base + 4 * arena_cols, (r.at - base, 4 * arena_cols)

        const_loaded = sem("const_loaded")
        x_loaded = [sem(f"x_loaded{c}") for c in range(DC)]
        const_ready = sem("const_ready")
        raw_loaded = [sem(f"raw_loaded{i}") for i in range(RING)]
        w_hi_ready, w_ready, w_used = sem("w_hi_ready"), sem("w_ready"), sem("w_used")
        chain_sem = sem("dve_chain")
        x_hi_ready, x_ready = sem("x_hi_ready"), sem("x_ready")
        silu_done, h_full, h_hi_ready, h_ready = (sem(n) for n in (
            "silu_done", "h_full", "h_hi_ready", "h_ready"))
        z_full, square_full, sum_full, sumsq_full = (sem(n) for n in (
            "z_full", "square_full", "sum_full", "sumsq_full"))

        class Stats:

            def __init__(self, kind):
                self.sums = sem(kind + "_sums")
                self.squares = sem(kind + "_squares")
                self.mean_parts = sem(kind + "_mean_parts")
                self.mean_turned = sem(kind + "_mean_turned")
                self.mean_row = sem(kind + "_mean_row")
                self.mean_full = sem(kind + "_mean_full")
                self.inv_var = sem(kind + "_inv_var")
                self.rstd = sem(kind + "_rstd")
                self.rstd_parts = sem(kind + "_rstd_parts")
                self.rstd_turned = sem(kind + "_rstd_turned")
                self.rstd_row = sem(kind + "_rstd_row")
                self.rstd_full = sem(kind + "_rstd_full")

        ln_stats, rms_stats, gn_stats = Stats("ln"), Stats("rms"), Stats("gn")
        half_full = sem("half_full")
        centred, scaled, affine_done = sem("centred"), sem("scaled"), sem("affine_done")
        rope_e_loaded = sem("rope_e_loaded")
        lam_sum, lam_exp = sem("lam_sum"), sem("lam_exp")
        raw_hi, raw_lo, swap_full, rot_ready = (sem(n) for n in (
            "raw_hi", "raw_lo", "swap_full", "rot_ready"))
        e_v_hi, e_v_ready = sem("e_v_hi"), sem("e_v_ready")
        cc_copied, u_full, conv_ready = (sem(n) for n in (
            "cc_copied", "u_full", "conv_ready"))
        score_full, bias_ready, exp_done, mixed = (sem(n) for n in (
            "score_full", "bias_ready", "exp_done", "mixed"))
        at_full, at_hi_ready, at_ready, pv_full = (sem(n) for n in (
            "at_full", "at_hi_ready", "at_ready", "pv_full"))
        ao_copied, ao_squared, attn_ready = (sem(n) for n in ("ao_copied", "ao_squared", "attn_ready"))
        table_o_loaded = sem("table_o_loaded")
        o_rot_ready, o_v_hi, o_v_ready, o_out_half = (sem(n) for n in (
            "o_rot_ready", "o_v_hi", "o_v_ready", "o_out_half"))
        ret_full, m_ready, sg_done, y_full, y_copied, y_squared = (sem(n) for n in (
            "ret_full", "m_ready", "sg_done", "y_full", "y_copied", "y_squared"))
        y_centred, y_scaled, y_gated, y_hi_ready = (sem(n) for n in (
            "y_centred", "y_scaled", "y_gated", "y_hi_ready"))
        gn_sum, gn_sumsq, y_ready, z_scaled = (sem(n) for n in ("gn_sum", "gn_sumsq", "y_ready", "z_scaled"))
        stored = sem("stored")

        NORM_X_AT = [DC + 2 * DC * ln for ln in range(6)]
        block = ctx.enter_context(nc.Block())

        @block.sync
        def _(sp):
            def load(u, slot):
                sp.dma_start(raw[:, slot, :],
                             stream[bass.ds(u, 1), :, :].rearrange("a p n -> (a p) n")).then_inc(raw_loaded[slot], 16)

            load(0, 0)
            for c in range(DC):
                sp.dma_start(z[:, c, :], x_in[c]).then_inc(x_loaded[c], 16)
            load(1, 1)
            load(2, 2)
            sp.dma_start(const[:, :], const_in).then_inc(const_loaded, 16)
            load(3, 3)
            with sp.Fori(1, UNITS // RING) as i:
                for s in range(RING):
                    sp.wait_ge(w_ready, RING * i + (s + 1 - RING))
                    load(RING * i + s, s)
            for a, tokens in enumerate(HALVES):
                for c in range(DC):
                    sp.wait_ge(affine_done, DC * (2 * LAST_LN + a) + c + 1)
                    sp.dma_start(out[c, :, tokens], z[:, c, tokens]).then_inc(stored, 16)
            sp.wait_ge(stored, 2 * 16 * DC)

        @block.gpsimd
        def _(pool):
            def low_part(u, slot):
                pool.wait_ge(w_hi_ready, u + 1)
                nc.gpsimd.tensor_tensor(w_lo[:, slot, :], raw[:, slot, :], w_hi[:, slot, :].bitcast(F32),
                                        ALU.subtract).then_inc(w_ready, 1)

            with pool.Fori(0, UNITS // RING) as i:
                for s in range(RING):
                    low_part(RING * i + s, s)

        @block.scalar
        def _(act):
            def cast(u, loads, slot, free=True):
                act.wait_ge(raw_loaded[slot], 16 * (loads + 1))
                if free:
                    act.wait_ge(w_used, u + (1 - RING))
                nc.scalar.copy(w_hi[:, slot, :], raw[:, slot, :]).then_inc(w_hi_ready, 1)

            def cast_after(u):
                if u + RING < UNITS:
                    cast(u + RING, u // RING + 1, u % RING)

            for u in range(RING):
                cast(u, 0, u, free=False)
                if u == 0:
                    for c in range(DC):
                        act.wait_ge(x_loaded[c], 16)
                        nc.scalar.copy(x_hi[:, c, :], z[:, c, :]).then_inc(x_hi_ready, 1)
            act.wait_ge(lam_sum, 2)
            nc.scalar.activation(lam[:, 2:4], lam[:, 0:2], ACT.Exp).then_inc(lam_exp, 1)

            def square_z(ln, j, oc, tokens=slice(0, T)):
                act.wait_ge(z_full, Z_AT[ln] + 1 + j)
                nc.scalar.activation(square[:, j % 2, tokens], z[:, oc, tokens], ACT.Square).then_inc(square_full, 1)

            def load_table(func):
                nc.scalar.activation(lam[:, 7:8], cst("mean_d")[:, 0:1], func)

            def ffn_in(n):
                b = FFN_AT[n]

                def pair(j, u_loads, s):
                    act.wait_ge(w_used, 2 * j + (b + 1))
                    nc.scalar.activation(silu_g[:, s // 2, :], bank[s][:], ACT.Silu).then_inc(silu_done, 1)
                    for k in range(2):
                        cast(2 * j + (b + k + RING), u_loads + 1, s + k)

                load_table(ACT.Silu)
                for p in range(2):
                    pair(p, b // RING, 2 * p)
                with act.Fori(1, FC // 2) as i:
                    for p in range(2):
                        pair(2 * i + p, b // RING + i, 2 * p)

            def ffn_out(n):
                b = FFN_AT[n] + 2 * FC
                ln = FFN_LN[n]
                for oc in range(DC - 1):
                    for k in range(OUT_UNITS):
                        if k == OUT_UNITS - 1:
                            square_z(ln, oc, oc)
                        cast_after(b + OUT_UNITS * oc + k)
                load_table(ACT.Sqrt)

            def copy_row(ready, done, n, row, b):
                act.wait_ge(ready, n)
                nc.scalar.copy(row[:], bank[b][0:8, 0:P]).then_inc(done, 1)

            def root(st, n, blocks=slice(0, TB)):
                act.wait_ge(st.inv_var, n)
                nc.scalar.activation(rstd[:, blocks], inv_var[:, blocks], ACT.Sqrt).then_inc(st.rstd, 1)

            def layer_norm(ln, load_rope=None):
                st, n = ln_stats, 2 * ln + 1
                end = END_SLOT[ln]
                for k in range(SPLIT[ln]):
                    square_z(ln, SPLIT_AT[ln] + k, SPLIT_AT[ln] + k, HALVES[0])

                def b_square(k):
                    if k in B_SLOTS[ln]:
                        j = B_SLOTS[ln].index(k)
                        square_z(ln, DC + j, SPLIT_AT[ln] + j, HALVES[1])
                        if j == SPLIT[ln] - 1 and load_rope:
                            load_rope()

                def slot(k):
                    if 1 <= k <= HELD[ln]:
                        cast_after(LAST_UNIT[ln] - HELD[ln] + k - 1)
                    if k == end + 2:
                        root(st, n + 1, slice(2, 4))
                        copy_row(st.mean_turned, st.mean_row, n + 1, row_mean, 5)
                    if k == min(end + 4, DC + 1):
                        copy_row(st.rstd_turned, st.rstd_row, n + 1, row_rstd, 4)

                copy_row(st.mean_turned, st.mean_row, n, row_mean, 7)
                root(st, n, slice(0, 2))
                b_square(0)
                copy_row(st.rstd_turned, st.rstd_row, n, row_rstd, 6)
                b_square(1)
                slot(1)
                g, b = CONST["ln_g"][0] + DC * ln, CONST["ln_b"][0] + DC * ln
                for a, tokens in enumerate(HALVES):
                    for c in range(DC + 1):
                        at = DC * (2 * ln + a) + c
                        if a == 0 and c:
                            b_square(c + 1)
                        if c < DC and ln != LAST_LN:
                            act.wait_ge(scaled, at + 1)
                            nc.scalar.activation(x_hi[:, c, tokens], z[:, c, tokens], ACT.Identity,
                                                 bias=const[:, b + c:b + c + 1],
                                                 scale=const[:, g + c:g + c + 1]).then_inc(x_hi_ready, 1)
                        if c:
                            if ln != LAST_LN:
                                act.wait_ge(x_hi_ready, DC + at)
                            else:
                                act.wait_ge(scaled, at)
                            zc = z[:, c - 1, tokens]
                            nc.scalar.activation(zc, zc, ACT.Identity, bias=const[:, b + c - 1:b + c],
                                                 scale=const[:, g + c - 1:g + c]).then_inc(affine_done, 1)
                        if a == 0 and c:
                            slot(c + 1)

            def even():
                b = EVEN_AT
                for t in range(8):
                    act.wait_ge(w_used, b + t + 1)
                    if t >= 2:
                        act.wait_ge(swap_full, t - 1)
                    if t == 0:
                        cast_after(b)
                    nc.scalar.copy(qr_hi[:, t % 2, :], bank[t][:]).then_inc(raw_hi, 1)
                    if t:
                        cast_after(b + t)
                for k in range(3):
                    cast_after(b + 8 + k)
                for t in range(TB):
                    act.wait_ge(w_used, b + 12)
                    nc.scalar.copy(v_hi[:, t, :], bank[t][:]).then_inc(e_v_hi, 1)
                cast_after(b + 11)
                for i in range(6):
                    for s in range(8 if i < 5 else 5):
                        if 1 <= i <= 4 and s == 0:
                            cast_after(b + 12 + 3 * i - 1)
                        if i < 4 and s in (3, 6):
                            cast_after(b + 12 + 3 * i + s // 3 - 1)
                        if i < 4 and s == 3:
                            act.wait_ge(w_used, b + 12 + 3 * i + 1)
                            if i:
                                act.wait_ge(u_full, i)
                            nc.scalar.copy(cc_sb[:], bank[CONV_BANKS[min(i, 1)][0]][:]).then_inc(cc_copied, 1)
                        if i < 4:
                            j, q = s // TB, s % TB
                            act.wait_ge(bias_ready, 8 * i + s + 1)
                            if i:
                                act.wait_ge(mixed, TB * (i - 1) + q + 1)
                            nc.scalar.activation(prob[:, j, SPAN_AT[q]:SPAN_AT[q] + SPAN[q]],
                                                 bank[4 + s % 2][:, 0:SPAN[q]], ACT.Exp,
                                                 bias=e_max[:, s % 2:s % 2 + 1],
                                                 accum_out=e_sum[:, i % 2, s:s + 1]).then_inc(exp_done, 1)
                        if 1 <= i <= 4 and 4 <= s <= 6:
                            g = s - 4
                            a, n = REST_AT[g], REST[g] if g < 2 else TRI - REST_AT[2]
                            act.wait_ge(at_full, 3 * (i - 1) + g + 1)
                            nc.scalar.copy(at_hi[:, a:a + n], bank[6][:, 0:n]).then_inc(at_hi_ready, 1)
                        if i >= 2 and s == 0:
                            act.wait_ge(pv_full, i - 1)
                            if i >= 3:
                                act.wait_ge(attn_ready, i - 2)
                            nc.scalar.copy(ao_sb[:], bank[7][:]).then_inc(ao_copied, 1)
                            nc.scalar.activation(square[:, 0, :], bank[7][:], ACT.Square).then_inc(ao_squared, 1)
                        if i >= 2 and s == RMS_SLOTS[i][0]:
                            root(rms_stats, i - 1)
                        if i >= 2 and s == RMS_SLOTS[i][1]:
                            copy_row(rms_stats.rstd_turned, rms_stats.rstd_row, i - 1, row_rstd, 3)
                load_table(ACT.Sqrt)
                for oc in range(SPLIT_AT[EVEN_LN]):
                    square_z(EVEN_LN, oc, oc)
                    cast_after(b + 24 + oc)

            def odd():
                b = ODD_AT

                def head(h, u0, loads):
                    first = isinstance(h, int)
                    w, k0 = (0, 4) if first else (4, 8)
                    for k in range(4 + w + 4):
                        cast(u0 + (k + RING), loads + (k // RING + 1), k % RING)
                    for t in range(TB):
                        act.wait_ge(w_used, u0 + (4 + w + 4))
                        nc.scalar.copy(rv_hi[:, t, :], bank[4 + t][:]).then_inc(o_v_hi, 1)
                    for c, gb in enumerate((4, 1, 4, 1) if first else (1, 4, 1, 4)):
                        act.wait_ge(w_used, u0 + (k0 + 4 + c + 1))
                        nc.scalar.activation(sg[:, c, :], bank[gb][:], ACT.Silu).then_inc(sg_done, 1)
                        k = k0 + 4 + c
                        cast(u0 + (k + RING), loads + (k // RING + 1), k % RING)
                        if c == 0:
                            load_table(ACT.Sqrt)
                            for y, yb in enumerate((5, 6, 7, 0)):
                                act.wait_ge(y_full, 4 * h + y + 1)
                                nc.scalar.copy(y_f[:, y, :], bank[yb][:]).then_inc(y_copied, 1)
                                if y >= 2:
                                    act.wait_ge(gn_sumsq, 3 * h + y - 1)
                                nc.scalar.activation(square[:, y % 2, :], bank[yb][:],
                                                     ACT.Square).then_inc(y_squared, 1)
                        if c >= 2:
                            for y in (2 * c - 4, 2 * c - 3):
                                act.wait_ge(y_gated, 4 * h + y + 1)
                                nc.scalar.copy(y_hi[:, y, :], y_f[:, y, :]).then_inc(y_hi_ready, 1)
                        if c == 1:
                            copy_row(gn_stats.mean_turned, gn_stats.mean_row, h + 1, row_mean, 3)
                            root(gn_stats, h + 1)
                            copy_row(gn_stats.rstd_turned, gn_stats.rstd_row, h + 1, row_rstd, 2)

                head(0, b, b // RING)
                with act.Fori(1, HEADS) as h:
                    head(h, 16 * h + (b - 4), 4 * h + (b - 4) // RING)
                load_table(ACT.Sqrt)
                for oc in range(SPLIT_AT[ODD_LN]):
                    square_z(ODD_LN, oc, oc)
                    if oc % 2:
                        cast_after(b + 60 + oc // 2)

            def load_even():
                act.dma_start(rope_e[:, :, :], rope_even).then_inc(rope_e_loaded, 16)

            def load_odd():
                act.dma_start(rope_o[:, :, :], rope_odd).then_inc(table_o_loaded, 16)
                act.dma_start(decay[:, :, :], decay_in).then_inc(table_o_loaded, 16)

            ffn_in(0)
            ffn_out(0)
            layer_norm(0, load_even)
            even()
            layer_norm(1)
            ffn_in(1)
            ffn_out(1)
            layer_norm(2)
            ffn_in(2)
            ffn_out(2)
            layer_norm(3, load_odd)
            odd()
            layer_norm(4)
            ffn_in(3)
            ffn_out(3)
            layer_norm(5)

        @block.vector
        def _(dve):
            class Chain:
                n = 0

                def link(self, ins):
                    ins.then_inc(chain_sem, 1)
                    self.n = self.n + 1
                    dve.wait_ge(chain_sem, self.n)

            chain = Chain()
            link = chain.link

            def loop(lo, hi, per, body):
                start = chain.n
                with dve.Fori(lo, hi) as i:
                    chain.n = (i - lo) * per + start
                    body(i)
                    last = chain.n
                chain.n = start + (hi - lo) * per
                return last

            for c in range(DC):
                dve.wait_ge(x_hi_ready, c + 1)
                nc.vector.tensor_tensor(x_lo[:, c, :], z[:, c, :], x_hi[:, c, :].bitcast(F32),
                                        ALU.subtract).then_inc(x_ready, 1)
            dve.wait_ge(const_loaded, 16)
            nc.vector.tensor_copy(swap[:], cst("swap")).then_inc(const_ready, 1)
            nc.vector.tensor_copy(ident_r[:], ident).then_inc(const_ready, 1)
            nc.vector.tensor_copy(mask[:], cst("mask")).then_inc(const_ready, 1)
            nc.vector.tensor_copy(rows[:], cst("rows")[0:8, :]).then_inc(const_ready, 1)
            link(nc.vector.memset(stat[:, 16:32], 0.0))
            la = CONST["lam"][0]
            for k in range(2):
                link(nc.vector.tensor_tensor(square[:, k, 0:64], const[:, la + 128 * k:la + 128 * k + 64],
                                             const[:, la + 128 * k + 64:la + 128 * k + 128], ALU.mult))
                nc.vector.reduce_sum(lam[:, k:k + 1], square[:, k, 0:64], AX_X).then_inc(lam_sum, 1)
            dve.wait_ge(lam_exp, 1)
            link(nc.vector.tensor_tensor(lam[:, 4:5], lam[:, 3:4], lam[:, 2:3], ALU.subtract))
            link(nc.vector.tensor_scalar(lam[:, 5:6], lam[:, 4:5], -LAMBDA_INIT, None, ALU.add))
            link(nc.vector.tensor_scalar(lam[:, 6:7], cst("norm_g"), 1.0 - LAMBDA_INIT, None, ALU.mult))

            def ffn_in(n):
                clear_sums(FFN_LN[n])

                def pair(j, p):
                    g = FC * n + j
                    dve.wait_ge(silu_done, g + 1)
                    dve.wait_ge(w_used, 2 * j + (FFN_AT[n] + 2))
                    dve.wait_ge(h_ready, g)
                    nc.vector.scalar_tensor_tensor(out=h_f[:], in0=silu_g[:, p, :], scalar=0.5,
                                                   in1=bank[2 * p + 1][:], op0=ALU.mult,
                                                   op1=ALU.mult).then_inc(h_full, 1)
                    dve.wait_ge(h_full, g + 1)
                    hj = h_hi[:, bass.ds(j, 1), :].rearrange("p a t -> p (a t)")
                    nc.vector.tensor_copy(hj, h_f[:]).then_inc(h_hi_ready, 1)
                    dve.wait_ge(h_hi_ready, g + 1)
                    nc.vector.tensor_tensor(h_lo[:, bass.ds(j, 1), :].rearrange("p a t -> p (a t)"), h_f[:],
                                            hj.bitcast(F32), ALU.subtract).then_inc(h_ready, 1)

                for p in range(2):
                    pair(p, p)
                with dve.Fori(1, FC // 2) as i:
                    for p in range(2):
                        pair(2 * i + p, p)

            def await_sums(ln):
                if ln:
                    dve.wait_ge(ln_stats.squares, 2 * ln)
                dve.wait_ge(x_ready, NORM_X_AT[ln])
                dve.wait_ge(sumsq_full, UP_AT[ln])

            def clear_sums(ln):
                await_sums(ln)
                nc.vector.memset(acc_sum[:], 0.0).then_inc(z_full, 1)
                nc.vector.memset(acc_sq[:], 0.0).then_inc(z_full, 1)
                dve.wait_ge(z_full, Z_AT[ln])

            def starts_sums(ln, j):
                return CLEARS[ln] == 0 and j == 0

            def z_write(ln, oc, b, tokens=slice(0, T)):
                scale = 1.0 if ln == ODD_LN else ALPHA
                zo = z[:, bass.ds(oc, 1), tokens].rearrange("p a t -> p (a t)")
                nc.vector.scalar_tensor_tensor(out=zo, in0=zo, scalar=scale, in1=bank[b][:, tokens], op0=ALU.mult,
                                               op1=ALU.add).then_inc(z_full, 1)

            def z_sum(ln, j, oc, tokens=slice(0, T)):
                zo = z[:, bass.ds(oc, 1), tokens].rearrange("p a t -> p (a t)")
                dve.wait_ge(z_full, j + (Z_AT[ln] + 1))
                if starts_sums(ln, j):
                    nc.vector.tensor_copy(acc_sum[:, tokens], zo).then_inc(sum_full, 1)
                else:
                    nc.vector.tensor_tensor(acc_sum[:, tokens], acc_sum[:, tokens], zo, ALU.add).then_inc(sum_full, 1)

            def z_update(ln, j, oc, b, tokens=slice(0, T)):
                z_write(ln, oc, b, tokens)
                z_sum(ln, j, oc, tokens)

            def square_sum(ln, j, slot, tokens=slice(0, T)):
                dve.wait_ge(square_full, j + (UP_AT[ln] + 1))
                if starts_sums(ln, j):
                    nc.vector.tensor_copy(acc_sq[:, tokens], square[:, slot, tokens]).then_inc(sumsq_full, 1)
                else:
                    nc.vector.tensor_tensor(acc_sq[:, tokens], acc_sq[:, tokens], square[:, slot, tokens],
                                            ALU.add).then_inc(sumsq_full, 1)

            def ffn_out(n):
                ln = FFN_LN[n]

                def chunk(oc, q):
                    dve.wait_ge(w_used, OUT_UNITS * oc + (FFN_AT[n] + 2 * FC + OUT_UNITS))
                    z_update(ln, oc, oc, 4 + q)
                    square_sum(ln, oc, q)

                with dve.Fori(0, DC // 2 - 1) as i:
                    for q in range(2):
                        chunk(2 * i + q, q)
                chunk(DC - 2, 0)

            def hi_lo(values, parts, done, blocks):
                lo = slice(blocks.start + TB, blocks.stop + TB)
                link(nc.vector.tensor_copy(parts[:, blocks].bitcast(F32R), values[:, blocks]))
                nc.vector.tensor_tensor(parts[:, lo], values[:, blocks], parts[:, blocks], ALU.subtract).then_inc(done, 1)

            def stats_in(b, blocks):
                return bank[b][:, 2 * blocks.start:2 * blocks.stop:2]

            def mean_of(st, n, b, blocks=slice(0, TB)):
                dve.wait_ge(st.sums, n)
                link(nc.vector.tensor_copy(mean[:, blocks], stats_in(b, blocks)))
                hi_lo(mean, parts_mean, st.mean_parts, blocks)
                link(nc.vector.tensor_tensor(mean2[:, blocks], mean[:, blocks], mean[:, blocks], ALU.mult))

            def inverse_variance(st, n, b, blocks=slice(0, TB)):
                dve.wait_ge(st.squares, n)
                m = mean2[:, blocks]
                link(nc.vector.scalar_tensor_tensor(out=m, in0=stats_in(b, blocks), scalar=EPS, in1=m,
                                                    op0=ALU.add, op1=ALU.subtract))
                link(nc.vector.tensor_scalar(m, m, EPS, None, ALU.max))
                nc.vector.reciprocal(inv_var[:, blocks], m).then_inc(st.inv_var, 1)

            def split_rstd(st, n, blocks=slice(0, TB)):
                dve.wait_ge(st.inv_var, n)
                dve.wait_ge(st.rstd, n)
                hi_lo(rstd, parts_rstd, st.rstd_parts, blocks)

            def layer_norm(ln):
                split, n_split, end = SPLIT_AT[ln], SPLIT[ln], END_SLOT[ln]
                held = LAST_UNIT[ln] - HELD[ln]
                after_ffn = ln not in (EVEN_LN, ODD_LN)
                tokens = slice(0, T)
                for j in range(split if after_ffn else 0, DC):
                    if j >= split:
                        dve.wait_ge(half_full, HALF_AT[ln] + j - split + 1)
                        b = A_BANKS[ln][j - split]
                    elif ln == EVEN_LN:
                        dve.wait_ge(w_used, EVEN_AT + 24 + j + 1)
                        b = (0, 1, 4, 5)[j % 4]
                    else:
                        dve.wait_ge(*((w_used, ODD_AT + 60 + j // 2 + 1) if j % 2 else (o_out_half, 4 * 3 + j // 2 + 1)))
                        b = OUT_BANKS[j]
                    z_write(ln, j, b, HALVES[0] if j >= split else tokens)
                    if j and not after_ffn:
                        dve.wait_ge(sumsq_full, UP_AT[ln] + j - 1)
                        square_sum(ln, j - 1, (j - 1) % 2, HALVES[0] if j - 1 >= split else tokens)
                    z_sum(ln, j, j, HALVES[0] if j >= split else tokens)
                dve.wait_ge(sumsq_full, UP_AT[ln] + DC - 1)
                square_sum(ln, DC - 1, (DC - 1) % 2, HALVES[0])

                def b_full(k):
                    if ln != ODD_LN:
                        dve.wait_ge(w_used, LAST_UNIT[ln] - n_split + k + 1)
                    elif k % 2 == 0:
                        dve.wait_ge(half_full, HALF_AT[ln] + n_split + k // 2 + 1)
                    else:
                        dve.wait_ge(w_used, held + k // 2 + 1)

                def slot(k):
                    if k - 1 in B_SLOTS[ln]:
                        j = B_SLOTS[ln].index(k - 1)
                        square_sum(ln, DC + j, (DC + j) % 2, HALVES[1])
                    if k in B_SLOTS[ln]:
                        j = B_SLOTS[ln].index(k)
                        b_full(j)
                        z_update(ln, DC + j, split + j, 4 - n_split + j, HALVES[1])
                    if k == end + 1:
                        mean_of(ln_stats, 2 * ln + 2, NORM_BANKS[1][0], slice(2, 4))
                    if k == end + 2:
                        inverse_variance(ln_stats, 2 * ln + 2, NORM_BANKS[1][1], slice(2, 4))
                    if k == end + 3:
                        split_rstd(ln_stats, 2 * ln + 2, slice(2, 4))

                def centre(a, c):
                    tokens = HALVES[a]
                    if c == 0:
                        dve.wait_ge(ln_stats.mean_full, 2 * ln + a + 1)
                    nc.vector.tensor_tensor(z[:, c, tokens], z[:, c, tokens], bank[NORM_BANKS[a][0]][:, tokens],
                                            ALU.subtract).then_inc(centred, 1)

                def scale(a, c):
                    tokens = HALVES[a]
                    if c == 0:
                        dve.wait_ge(ln_stats.rstd_full, 2 * ln + a + 1)
                    dve.wait_ge(centred, DC * (2 * ln + a) + c + 1)
                    nc.vector.tensor_tensor(z[:, c, tokens], z[:, c, tokens], bank[NORM_BANKS[a][1]][:, tokens],
                                            ALU.mult).then_inc(scaled, 1)

                def low(a, c):
                    if ln != LAST_LN:
                        tokens = HALVES[a]
                        dve.wait_ge(affine_done, DC * (2 * ln + a) + c + 1)
                        nc.vector.tensor_tensor(x_lo[:, c, tokens], z[:, c, tokens],
                                                x_hi[:, c, tokens].bitcast(F32), ALU.subtract).then_inc(x_ready, 1)

                mean_of(ln_stats, 2 * ln + 1, NORM_BANKS[0][0], slice(0, 2))
                inverse_variance(ln_stats, 2 * ln + 1, NORM_BANKS[0][1], slice(0, 2))
                slot(0)
                split_rstd(ln_stats, 2 * ln + 1, slice(0, 2))
                slot(1)
                lead = 2 if ln == LAST_LN else 1
                for a in range(2):
                    for c in range(lead):
                        centre(a, c)
                    for c in range(DC):
                        if a == 0 and c:
                            slot(c + 1)
                        scale(a, c)
                        if c + lead < DC:
                            centre(a, c + lead)
                        if c >= 2:
                            low(a, c - 2)
                    low(a, DC - 2)
                    low(a, DC - 1)
                    if a == 0:
                        slot(DC + 1)

            def even():
                dve.wait_ge(rope_e_loaded, 16)

                def unrotated(t):
                    dve.wait_ge(raw_hi, t + 1)
                    nc.vector.tensor_tensor(qr_lo[:, t % 2, :], bank[t][:], qr_hi[:, t % 2, :].bitcast(F32),
                                            ALU.subtract).then_inc(raw_lo, 1)
                    nc.vector.tensor_tensor(qr_cos[:, t % 2, :], bank[t][:], rope_e[:, 2 * (t % 2), :],
                                            ALU.mult).then_inc(raw_lo, 1)

                def rotated(t):
                    hi, lo = (q_hi, q_lo) if t % 2 == 0 else (k_hi, k_lo)
                    dve.wait_ge(swap_full, t + 1)
                    dve.wait_ge(rot_ready, t)
                    link(nc.vector.tensor_tensor(qr_sin[:], bank[t][:], rope_e[:, 2 * (t % 2) + 1, :], ALU.mult))
                    dve.wait_ge(raw_lo, 2 * t + 2)
                    link(nc.vector.tensor_tensor(qr_sin[:], qr_sin[:], qr_cos[:, t % 2, :], ALU.add))
                    link(nc.vector.tensor_copy(hi[:, t // 2, :], qr_sin[:]))
                    nc.vector.tensor_tensor(lo[:, t // 2, :], qr_sin[:], hi[:, t // 2, :].bitcast(F32),
                                            ALU.subtract).then_inc(rot_ready, 1)

                unrotated(0)
                unrotated(1)
                for t in range(6):
                    rotated(t)
                    unrotated(t + 2)
                rotated(6)
                rotated(7)
                link(nc.vector.memset(u_sb[:, 0:2], 0.0))
                for t in range(TB):
                    dve.wait_ge(e_v_hi, t + 1)
                    nc.vector.tensor_tensor(v_lo[:, t, :], bank[t][:], v_hi[:, t, :].bitcast(F32),
                                            ALU.subtract).then_inc(e_v_ready, 1)
                cw = CONST["conv_w"][0]

                def conv_w(k, i):
                    return const[:, cw + 4 * k + i:cw + 4 * k + i + 1]

                def conv_product(i):
                    dve.wait_ge(cc_copied, i + 1)
                    dve.wait_ge(w_used, EVEN_AT + 12 + 3 * i + 2)
                    nc.vector.tensor_tensor(u_sb[:, 2:T + 2], cc_sb[:], bank[CONV_BANKS[min(i, 1)][1]][:],
                                            ALU.mult).then_inc(u_full, 1)

                def conv_taps(i):
                    dve.wait_ge(u_full, i + 1)
                    dve.wait_ge(conv_ready, i)
                    link(nc.vector.tensor_scalar(y_sb[:], u_sb[:, 2:T + 2], conv_w(2, i), None, ALU.mult))
                    for k in (1, 0):
                        link(nc.vector.scalar_tensor_tensor(out=y_sb[:], in0=u_sb[:, k:T + k], scalar=conv_w(k, i),
                                                            in1=y_sb[:], op0=ALU.mult, op1=ALU.add))

                def conv_gate(i):
                    dve.wait_ge(w_used, EVEN_AT + 12 + 3 * i + 3)
                    dve.wait_ge(score_full, 8 * i + 8)
                    link(nc.vector.tensor_tensor(y_sb[:], y_sb[:], bank[2][:], ALU.mult))
                    link(nc.vector.tensor_copy(q_hi[:, i, :], y_sb[:]))
                    nc.vector.tensor_tensor(q_lo[:, i, :], y_sb[:], q_hi[:, i, :].bitcast(F32),
                                            ALU.subtract).then_inc(conv_ready, 1)

                def score(i, s):
                    dve.wait_ge(score_full, 8 * i + s + 1)
                    if 8 * i + s >= 2:
                        dve.wait_ge(exp_done, 8 * i + s - 1)
                        dve.wait_ge(bias_ready, 8 * i + s - 1)
                    nc.vector.reduce_max(e_max[:, s % 2:s % 2 + 1], bank[4 + s % 2][:, 0:SPAN[s % TB]], AX_X,
                                         negate=True).then_inc(bias_ready, 1)

                def mix(h, q):
                    if q == 0:
                        dve.wait_ge(exp_done, 8 * h + 8)
                        dve.wait_ge(mixed, TB * h)
                        link(nc.vector.reciprocal(e_rec[:], e_sum[:, h % 2, :]))
                        link(nc.vector.tensor_scalar(e_rec[:, 4:8], e_rec[:, 4:8], lam[:, 5:6], None, ALU.mult))
                        if h:
                            dve.wait_ge(at_full, 3 * h)
                    a, n = SPAN_AT[q], SPAN[q]
                    link(nc.vector.tensor_scalar(prob[:, 1, a:a + n], prob[:, 1, a:a + n], e_rec[:, 4 + q:5 + q], None,
                                                 ALU.mult))
                    nc.vector.scalar_tensor_tensor(out=a_sb[:, a:a + n], in0=prob[:, 0, a:a + n],
                                                   scalar=e_rec[:, q:q + 1], in1=prob[:, 1, a:a + n],
                                                   op0=ALU.mult, op1=ALU.add).then_inc(mixed, 1)

                for i in range(6):
                    for s in range(8 if i < 5 else 5):
                        if i < 4:
                            score(i, s)
                        if 1 <= i <= 4 and s < 4:
                            mix(i - 1, s)
                        if 1 <= i <= 3 and s == 0:
                            conv_gate(i - 1)
                        if i < 4 and s == 7:
                            conv_product(i)
                            if i < 3:
                                conv_taps(i)
                        if 1 <= i <= 4 and 4 <= s <= 6:
                            g = s - 4
                            a, n = REST_AT[g], REST[g] if g < 2 else TRI - REST_AT[2]
                            dve.wait_ge(at_hi_ready, 3 * (i - 1) + g + 1)
                            nc.vector.tensor_tensor(at_lo[:, a:a + n], bank[6][:, 0:n], at_hi[:, a:a + n].bitcast(F32),
                                                    ALU.subtract).then_inc(at_ready, 1)
                        if i == 4 and s == 6:
                            conv_taps(3)
                            conv_gate(3)
                        if i >= 2 and s == RMS_SLOTS[i][0]:
                            dve.wait_ge(rms_stats.squares, i - 1)
                            link(nc.vector.tensor_scalar(mean2, bank[3][:, 0:8:2], EPS, None, ALU.add))
                            nc.vector.reciprocal(inv_var, mean2).then_inc(rms_stats.inv_var, 1)
                            split_rstd(rms_stats, i - 1)
                        if i >= 2 and s == RMS_SLOTS[i][2]:
                            h = i - 2
                            dve.wait_ge(rms_stats.rstd_full, h + 1)
                            dve.wait_ge(ao_copied, h + 1)
                            link(nc.vector.tensor_tensor(ao_sb[:], ao_sb[:], bank[3][:], ALU.mult))
                            link(nc.vector.tensor_scalar(k_hi[:, h, :], ao_sb[:], lam[:, 6:7], None, ALU.mult))
                            nc.vector.scalar_tensor_tensor(out=k_lo[:, h, :], in0=ao_sb[:], scalar=lam[:, 6:7],
                                                           in1=k_hi[:, h, :].bitcast(F32), op0=ALU.mult,
                                                           op1=ALU.subtract).then_inc(attn_ready, 1)
                await_sums(EVEN_LN)

            def odd():
                dve.wait_ge(table_o_loaded, 32)
                dve.wait_ge(x_ready, NORM_X_AT[ODD_LN])
                for c in range(DC):
                    nc.vector.tensor_scalar(z[:, c, :], z[:, c, :], ALPHA, None, ALU.mult).then_inc(z_scaled, 1)
                rg = CONST["ret_g"][0]

                def head(h):
                    first = isinstance(h, int)
                    u0 = ODD_AT if first else 16 * h + (ODD_AT - 4)
                    cos, sin = rope_o[:, 0, :], rope_o[:, 1, :]
                    for b0, hi, lo in ((0, rq_hi, rq_lo), (2, rk_hi, rk_lo)):
                        dve.wait_ge(w_used, u0 + (b0 + 2))
                        for k, op in ((0, ALU.subtract), (1, ALU.add)):
                            dve.wait_ge(o_rot_ready, 4 * h + (b0 + k))
                            link(nc.vector.tensor_tensor(r_t[:, 0, :], bank[b0 + k][:], cos, ALU.mult))
                            link(nc.vector.tensor_tensor(r_t[:, 1, :], bank[b0 + 1 - k][:], sin, ALU.mult))
                            link(nc.vector.tensor_tensor(r_t[:, 0, :], r_t[:, 0, :], r_t[:, 1, :], op))
                            link(nc.vector.tensor_copy(hi[:, k, :], r_t[:, 0, :]))
                            nc.vector.tensor_tensor(lo[:, k, :], r_t[:, 0, :], hi[:, k, :].bitcast(F32),
                                                    ALU.subtract).then_inc(o_rot_ready, 1)
                    if not first:
                        for oc in range(DC):
                            if oc % 2 == 0:
                                dve.wait_ge(o_out_half, 4 * h + (oc // 2 - 3))
                            else:
                                dve.wait_ge(w_used, u0 + (4 + oc // 2 + 1))
                            dve.wait_ge(z_scaled, oc + 1)
                            nc.vector.tensor_tensor(z[:, oc, :], z[:, oc, :], bank[OUT_BANKS[oc % 4]][:],
                                                    ALU.add).then_inc(z_full, 1)

                    def value_parts():
                        for t in range(TB):
                            dve.wait_ge(o_v_hi, TB * h + t + 1)
                            nc.vector.tensor_tensor(rv_lo[:, t, :], bank[4 + t][:], rv_hi[:, t, :].bitcast(F32),
                                                    ALU.subtract).then_inc(o_v_ready, 1)

                    if first:
                        value_parts()
                    for k in range(TB):
                        n, a = REST[k], REST_AT[k]
                        dve.wait_ge(ret_full, TB * h + k + 1)
                        dve.wait_ge(m_ready, TB * h + k)
                        link(nc.vector.tensor_tensor(m_f[:, 0:n], bank[k][:, 0:n],
                                                     decay[:, bass.ds(h, 1), 0:n].rearrange("p a t -> p (a t)"),
                                                     ALU.mult))
                        link(nc.vector.tensor_copy(m_hi[:, a:a + n], m_f[:, 0:n]))
                        nc.vector.tensor_tensor(m_lo[:, a:a + n], m_f[:, 0:n], m_hi[:, a:a + n].bitcast(F32),
                                                ALU.subtract).then_inc(m_ready, 1)
                    if not first:
                        value_parts()
                    for c in range(1, 4):
                        dve.wait_ge(y_copied, 4 * h + c + 1)
                        dve.wait_ge(gn_sum, 3 * h + (c - 1))
                        nc.vector.tensor_tensor(acc_sum[:], y_f[:, 0, :] if c == 1 else acc_sum[:], y_f[:, c, :],
                                                ALU.add).then_inc(gn_sum, 1)
                        dve.wait_ge(y_squared, 4 * h + c + 1)
                        dve.wait_ge(gn_sumsq, 3 * h + (c - 1))
                        nc.vector.tensor_tensor(acc_sq[:], square[:, 0, :] if c == 1 else acc_sq[:],
                                                square[:, c % 2, :], ALU.add).then_inc(gn_sumsq, 1)
                    mean_of(gn_stats, h + 1, 3)
                    inverse_variance(gn_stats, h + 1, 2)
                    split_rstd(gn_stats, h + 1)
                    dve.wait_ge(gn_stats.mean_full, h + 1)
                    def centre_y(c):
                        nc.vector.tensor_tensor(y_f[:, c, :], y_f[:, c, :], bank[3][:],
                                                ALU.subtract).then_inc(y_centred, 1)

                    def low_y(c):
                        dve.wait_ge(y_hi_ready, 4 * h + c + 1)
                        nc.vector.tensor_tensor(y_lo[:, c, :], y_f[:, c, :], y_hi[:, c, :].bitcast(F32),
                                                ALU.subtract).then_inc(y_ready, 1)

                    centre_y(0)
                    dve.wait_ge(gn_stats.rstd_full, h + 1)
                    for c in range(4):
                        dve.wait_ge(y_centred, 4 * h + c + 1)
                        nc.vector.tensor_tensor(y_f[:, c, :], y_f[:, c, :], bank[2][:], ALU.mult).then_inc(y_scaled, 1)
                        if c < 3:
                            centre_y(c + 1)
                        dve.wait_ge(y_scaled, 4 * h + c + 1)
                        dve.wait_ge(sg_done, 4 * h + c + 1)
                        nc.vector.scalar_tensor_tensor(out=y_f[:, c, :], in0=y_f[:, c, :],
                                                       scalar=const[:, bass.ds(4 * h + (rg + c), 1)],
                                                       in1=sg[:, c, :], op0=ALU.mult,
                                                       op1=ALU.mult).then_inc(y_gated, 1)
                        if c:
                            low_y(c - 1)
                    low_y(3)

                before = chain.n
                head(0)
                loop(1, HEADS, chain.n - before, head)
                await_sums(ODD_LN)

            ffn_in(0)
            ffn_out(0)
            layer_norm(0)
            even()
            layer_norm(1)
            ffn_in(1)
            ffn_out(1)
            layer_norm(2)
            ffn_in(2)
            ffn_out(2)
            layer_norm(3)
            odd()
            layer_norm(4)
            ffn_in(3)
            ffn_out(3)
            layer_norm(5)

        @block.tensor
        def _(pe):
            def mm3(o, a, b, start, stop):
                nc.tensor.matmul(o, a[0], b[0], start=start, stop=False)
                nc.tensor.matmul(o, a[0], b[1], start=False, stop=False)
                return nc.tensor.matmul(o, a[1], b[0], start=False, stop=stop)

            def w(slot, blk):
                c = slice(blk * P, (blk + 1) * P)
                return w_hi[:, slot, c], w_lo[:, slot, c]

            def x(c):
                return x_hi[:, c, :], x_lo[:, c, :]

            def part(hi, lo, *at):
                return hi[:, *at], lo[:, *at]

            def unit(u):
                pe.wait_ge(w_ready, u + 1)

            def norm_stage(ln, a, stage):
                st, n, last = ln_stats, 2 * ln + a + 1, UP_AT[ln] + (DC, UPDATES[ln])[a]
                b_mean, b_rstd = NORM_BANKS[a]
                blocks = HALF_BLOCKS[a]
                if stage == 0:
                    pe.wait_ge(sum_full, last)
                    token_means(bank[b_mean], acc_sum, cst("mean_d"), blocks).then_inc(st.sums, 1)
                elif stage == 1:
                    pe.wait_ge(sumsq_full, last)
                    token_means(bank[b_rstd], acc_sq, cst("mean_d"), blocks).then_inc(st.squares, 1)
                elif stage == 2:
                    turn_parts(parts_mean, st.mean_parts, n, st.mean_turned, bank[b_mean])
                elif stage == 3:
                    spread(st.mean_row, n, row_mean, st.mean_full, bank[b_mean], blocks)
                elif stage == 4:
                    turn_parts(parts_rstd, st.rstd_parts, n, st.rstd_turned, bank[b_rstd])
                else:
                    spread(st.rstd_row, n, row_rstd, st.rstd_full, bank[b_rstd], blocks)

            STAGE_AT = {ln: (6, 7, 8, 10, 12, 14) if ln == ODD_LN else (3, 4, 5, 7, 9, 11) for ln in range(6)}

            def b_block(ln, m):
                if m in STAGE_AT[ln]:
                    norm_stage(ln, 0, STAGE_AT[ln].index(m))

            LAG = ((0, 0, 2, 4), (0, 1, 1, 2))

            def first_four(u0, ln):
                x_at = NORM_X_AT[ln]
                free = 4 - SPLIT[ln]
                for a, tokens in enumerate(HALVES):
                    def chunks(step):
                        pairs = [(s, step - LAG[a][s]) for s in range(RING)]
                        return [(s, c) for s, c in pairs if 0 <= c < DC]

                    for step in range(DC + LAG[a][-1] + 1):
                        for stage, at in enumerate((-2, -1, 0, 2, 2, 4)):
                            if a == 0 and step == END_SLOT[ln] + at:
                                norm_stage(ln, 1, stage)
                        if step < DC:
                            pe.wait_ge(x_hi_ready, x_at + DC * a + step + 1)
                        for s, c in chunks(step):
                            if a == 0 and c == 0:
                                unit(u0 + s)
                                if s >= free:
                                    pe.wait_ge(z_full, Z_AT[ln] + DC + s - free + 1)
                            hi, lo = w(s, c)
                            nc.tensor.matmul(bank[s][:, tokens], hi, x_hi[:, c, tokens], start=c == 0, stop=False)
                            nc.tensor.matmul(bank[s][:, tokens], lo, x_hi[:, c, tokens], start=False, stop=False)
                        if 1 <= step <= DC:
                            pe.wait_ge(x_ready, x_at + DC * a + step)
                        for s, c in chunks(step - 1):
                            last = nc.tensor.matmul(bank[s][:, tokens], w(s, c)[0], x_lo[:, c, tokens],
                                                    start=False, stop=c == DC - 1)
                            if a == 1 and c == DC - 1:
                                last.then_inc(w_used, 1)

            def project(u, slot, o, between=None):
                pe.wait_ge(w_hi_ready, u + 1)
                for c in range(DC):
                    if between:
                        between(c)
                    hi = w(slot, c)[0]
                    nc.tensor.matmul(o, hi, x_hi[:, c, :], start=c == 0, stop=False)
                    nc.tensor.matmul(o, hi, x_lo[:, c, :], start=False, stop=False)
                if between:
                    between(DC)
                unit(u)
                for c in range(DC):
                    last = nc.tensor.matmul(o, w(slot, c)[1], x_hi[:, c, :], start=False, stop=c == DC - 1)
                last.then_inc(w_used, 1)

            def project_v(u0, o, each=None):
                for k in range(RING):
                    pe.wait_ge(w_hi_ready, u0 + k + 1)
                    for half in range(2):
                        c = 2 * k + half
                        n = slice(half * T, (half + 1) * T)
                        for t in range(TB):
                            if c == 0 and each:
                                each(t)
                            hi, lo = part(x_hi, x_lo, c, slice(t * P, (t + 1) * P))
                            nc.tensor.matmul(o[t][:], hi, w_hi[:, k, n], start=c == 0, stop=False)
                            nc.tensor.matmul(o[t][:], lo, w_hi[:, k, n], start=False, stop=False)
                    yield 2 * k
                    unit(u0 + k)
                    for half in range(2):
                        c = 2 * k + half
                        for t in range(TB):
                            last = nc.tensor.matmul(o[t][:], x_hi[:, c, t * P:(t + 1) * P],
                                                    w_lo[:, k, half * T:(half + 1) * T], start=False,
                                                    stop=c == DC - 1)
                    last.then_inc(w_used, 1)
                    yield 2 * k + 1

            def ffn_in(n):
                b = FFN_AT[n]
                if n == 0:
                    for s in range(2):
                        pe.wait_ge(w_hi_ready, s + 1)
                        for c in range(DC + 1):
                            if c < DC:
                                pe.wait_ge(x_hi_ready, c + 1)
                                nc.tensor.matmul(bank[s][:], w(s, c)[0], x_hi[:, c, :], start=c == 0, stop=False)
                            if c:
                                pe.wait_ge(x_ready, c)
                                nc.tensor.matmul(bank[s][:], w(s, c - 1)[0], x_lo[:, c - 1, :], start=False, stop=False)
                        unit(s)
                        for c in range(DC):
                            last = nc.tensor.matmul(bank[s][:], w(s, c)[1], x_hi[:, c, :], start=False, stop=c == DC - 1)
                        last.then_inc(w_used, 1)
                    for s in range(2, RING):
                        project(s, s, bank[s][:])
                else:
                    first_four(b, FFN_LN[n] - 1)
                with pe.Fori(1, FC // 2) as i:
                    for s in range(4):
                        if s % 2 == 0:
                            pe.wait_ge(h_full, 2 * i + (FC * n + s // 2 - 1))
                        project(4 * i + (b + s), s, bank[s][:])

            def ffn_out(n):
                b, ln = FFN_AT[n] + 2 * FC, FFN_LN[n]
                for oc in range(DC - 1):
                    pe.wait_ge(z_full, Z_AT[ln] + oc - 1)
                    for kc in range(FC):
                        r = OUT_UNITS * oc + kc // UB
                        if kc % UB == 0:
                            unit(b + r)
                        if oc == 0:
                            pe.wait_ge(h_ready, FC * n + kc + 1)
                        last = mm3(bank[4 + oc % 2][:], w(r % RING, kc % UB), part(h_hi, h_lo, kc), kc == 0, kc == FC - 1)
                        if kc % UB == UB - 1 or kc == FC - 1:
                            last.then_inc(w_used, 1)
                pe.wait_ge(z_full, Z_AT[ln] + DC - 2)
                for a, o in enumerate((bank[5], bank[3])):
                    for kc in range(FC):
                        r = OUT_UNITS * (DC - 1) + kc // UB
                        if a == 0 and kc % UB == 0:
                            unit(b + r)
                        if a == 1:
                            b_block(ln, kc)
                        last = mm3(o[:, HALVES[a]], w(r % RING, kc % UB), part(h_hi, h_lo, kc, HALVES[a]),
                                   kc == 0, kc == FC - 1)
                        if a == 1 and (kc % UB == UB - 1 or kc == FC - 1):
                            last.then_inc(w_used, 1)
                    if a == 0:
                        last.then_inc(half_full, 1)

            def token_means(o, src, one, blocks=range(TB)):
                for k in blocks:
                    last = nc.tensor.matmul(o[:, 2 * k:2 * k + 2], src[:, k * P:(k + 1) * P], one,
                                            start=True, stop=True)
                return last

            def turn_parts(parts, done, n, turned, o):
                pe.wait_ge(done, n)
                nc.tensor.transpose(o[0:8, 0:P], parts, ident).then_inc(turned, 1)

            def spread(row_done, n, row, full, o, blocks=range(TB)):
                pe.wait_ge(row_done, n)
                for k in blocks:
                    last = nc.tensor.matmul(o[:, k * P:(k + 1) * P], rows[0:8, k * P:(k + 1) * P], row[0:8, :],
                                            start=True, stop=True)
                last.then_inc(full, 1)

            def rstd_turn(st, n, b):
                turn_parts(parts_rstd, st.rstd_parts, n, st.rstd_turned, bank[b])

            def rstd_spread(st, n, b):
                spread(st.rstd_row, n, row_rstd, st.rstd_full, bank[b])

            def even():
                b = EVEN_AT

                def swap_halves(t):
                    pe.wait_ge(raw_lo, 2 * t + 2)
                    nc.tensor.matmul(bank[t][:], swap[:], qr_hi[:, t % 2, :], start=True, stop=False)
                    nc.tensor.matmul(bank[t][:], swap[:], qr_lo[:, t % 2, :], start=False,
                                     stop=True).then_inc(swap_full, 1)

                pe.wait_ge(const_ready, 4)
                first_four(b, FFN_LN[0])
                for t in range(4):
                    project(b + 4 + t, t, bank[4 + t][:], between=lambda c: c == DC // 2 and swap_halves(t))
                for point in project_v(b + 8, bank[0:4], lambda t: pe.wait_ge(rot_ready, t + 1)):
                    if point in (1, 2, 3, 5):
                        swap_halves((1, 2, 3, 5).index(point) + 4)

                def conv_part(i, m):
                    f, c = m // DC, m % DC
                    if c == 0:
                        unit(b + 12 + 3 * i + f)
                        if i == 0:
                            pe.wait_ge(*((rot_ready, 7), (rot_ready, 8), (e_v_ready, TB))[f])
                        else:
                            pe.wait_ge((cc_copied, u_full, conv_ready)[f], i)
                    last = mm3(bank[CONV_BANKS[min(i, 1)][f]][:], w((3 * i + f) % RING, c), x(c), c == 0, c == DC - 1)
                    if c == DC - 1:
                        last.then_inc(w_used, 1)

                def score(i, s):
                    j, q = s // TB, s % TB
                    if 8 * i + s < 2:
                        pe.wait_ge(rot_ready, 8)
                    else:
                        pe.wait_ge(exp_done, 8 * i + s - 1)
                    r = slice(64 * j, 64 * j + 64)
                    qs, ks = slice(q * P, (q + 1) * P), slice(0, SPAN[q])
                    o = bank[4 + s % 2]
                    mm3(o[:, ks], (q_hi[r, i, qs], q_lo[r, i, qs]), (k_hi[r, i, ks], k_lo[r, i, ks]), True, False)
                    nc.tensor.matmul(o[:, SPAN[q] - P:SPAN[q]], ident_r[:], mask[:], start=False,
                                     stop=True).then_inc(score_full, 1)

                def turn(h, g):
                    pe.wait_ge(mixed, TB * (h + 1))
                    if 3 * h + g:
                        pe.wait_ge(at_ready, 3 * h + g)
                    if h:
                        pe.wait_ge(pv_full, h)
                    for kb in ((0,), (1,), (2, 3))[g]:
                        for q in range(kb, TB):
                            c = REST_AT[kb] - REST_AT[g] + (q - kb) * P
                            last = nc.tensor.transpose(bank[6][:, c:c + P],
                                                       a_sb[:, SPAN_AT[q] + kb * P:SPAN_AT[q] + kb * P + P], ident)
                    last.then_inc(at_full, 1)

                def values(h):
                    pe.wait_ge(at_ready, 3 * h + 3)
                    if h == 0:
                        pe.wait_ge(e_v_ready, TB)
                    else:
                        pe.wait_ge(ao_squared, h)
                    for kb in range(TB):
                        last = mm3(bank[7][:, kb * P:T], part(v_hi, v_lo, kb, slice(h * P, (h + 1) * P)),
                                   part(at_hi, at_lo, slice(REST_AT[kb], REST_AT[kb] + REST[kb])),
                                   kb == 0, kb == TB - 1)
                    last.then_inc(pv_full, 1)

                O = (0, 1, 4, 5)

                def out_part(oc, blk):
                    if blk == 0:
                        unit(b + 24 + oc)
                        pe.wait_ge(*((cc_copied, 4), (u_full, 4), (exp_done, 31), (exp_done, 32))[oc])
                    if blk < 4:
                        pe.wait_ge(conv_ready, blk + 1)
                        src = part(q_hi, q_lo, blk)
                    else:
                        pe.wait_ge(attn_ready, blk - 3)
                        src = part(k_hi, k_lo, blk - 4)
                    last = mm3(bank[O[oc % 4]][:], w(oc % RING, blk), src, blk == 0, blk == UB - 1)
                    if blk == UB - 1:
                        last.then_inc(w_used, 1)

                for i in range(6):
                    for s in range(8 if i < 5 else 5):
                        if i < 4:
                            for m in range(3 * s, 3 * s + 3):
                                conv_part(i, m)
                            score(i, s)
                        elif i == 4:
                            for m in range(12 * s // 8, 12 * (s + 1) // 8):
                                out_part(m // 3, m % 3)
                        else:
                            for m in range(16 * s // 5, 16 * (s + 1) // 5):
                                out_part(*((m // 3, 4 + m % 3) if m < 12 else (m - 12, 3)))
                        if 1 <= i <= 4 and 4 <= s <= 6:
                            turn(i - 1, s - 4)
                        if 1 <= i <= 4 and s == 7:
                            values(i - 1)
                        if i >= 2 and s == RMS_SLOTS[i][0]:
                            pe.wait_ge(ao_squared, i - 1)
                            token_means(bank[3], square[:, 0, :], cst("mean_rms")).then_inc(rms_stats.squares, 1)
                        if i >= 2 and s == RMS_SLOTS[i][1]:
                            rstd_turn(rms_stats, i - 1, 3)
                        if i >= 2 and s == RMS_SLOTS[i][2]:
                            rstd_spread(rms_stats, i - 1, 3)
                for oc in range(4):
                    out_part(oc, 7)
                def source(blk, tokens=slice(0, T)):
                    return part(q_hi, q_lo, blk, tokens) if blk < 4 else part(k_hi, k_lo, blk - 4, tokens)

                for oc in (4, 5):
                    pe.wait_ge(z_full, Z_AT[EVEN_LN] + oc - 3)
                    pe.wait_ge(w_hi_ready, b + 24 + oc + 1)
                    for blk in range(UB):
                        for k, src in enumerate(source(blk)):
                            nc.tensor.matmul(bank[O[oc % 4]][:], w(oc % RING, blk)[0], src,
                                             start=blk + k == 0, stop=False)
                    unit(b + 24 + oc)
                    for blk in range(UB):
                        last = nc.tensor.matmul(bank[O[oc % 4]][:], w(oc % RING, blk)[1], source(blk)[0],
                                                start=False, stop=blk == UB - 1)
                    last.then_inc(w_used, 1)
                for a, tokens in enumerate(HALVES):
                    for k in range(2):
                        if a == 0:
                            unit(b + 24 + 6 + k)
                            pe.wait_ge(z_full, Z_AT[EVEN_LN] + 3 + k)
                        o = bank[(A_BANKS[EVEN_LN], (2, 3))[a][k]]
                        for blk in range(UB):
                            if a == 1:
                                b_block(EVEN_LN, UB * k + blk)
                            last = mm3(o[:, tokens], w(2 + k, blk), source(blk, tokens), blk == 0, blk == UB - 1)
                        last.then_inc((half_full, w_used)[a], 1)

            def odd():
                b = ODD_AT

                def share(wu, o, c, last_c):
                    last = mm3(bank[OUT_BANKS[(2 * wu + o) % 4]][:], w(wu, 4 * o + c), part(y_hi, y_lo, c),
                               c == 0, c == last_c)
                    if c == last_c:
                        last.then_inc(w_used if o else o_out_half, 1)

                def out_of_head(u0, z_free, units):
                    for wu in units:
                        unit(u0 + wu)
                        for o in range(2):
                            oc = 2 * wu + o
                            if oc >= 4:
                                pe.wait_ge(z_full, z_free + (oc - 3))
                            for c in range(4):
                                share(wu, o, c, 3)

                def head(h, u0):
                    first = isinstance(h, int)
                    if first:
                        first_four(u0, FFN_LN[2])
                        v0 = u0 + 4
                    else:
                        for s, (free, n) in enumerate(((y_squared, 4), (sg_done, 4), (y_ready, 4), (y_ready, 4))):
                            pe.wait_ge(free, n * h)
                            project(u0 + s, s, bank[s][:])
                        z_at = Z_AT[ODD_LN] - 24
                        out_of_head(u0 + 4, 8 * h + (z_at - 8), range(4))
                        v0 = u0 + 8
                    if first:
                        for _ in project_v(v0, bank[4:8]):
                            pass
                    for kb in range(TB):
                        pe.wait_ge(o_rot_ready, 4 * h + 4)
                        for c in range(2):
                            last = mm3(bank[kb][:, 0:REST[kb]], part(rk_hi, rk_lo, c, slice(kb * P, (kb + 1) * P)),
                                       part(rq_hi, rq_lo, c, slice(kb * P, T)), c == 0, c == 1)
                        last.then_inc(ret_full, 1)
                    if not first:
                        pe.wait_ge(z_full, 8 * h + z_at)
                        for _ in project_v(v0, bank[4:8]):
                            pass
                    g0 = v0 + 4
                    gate_banks = (4, 1) if first else (1, 4)
                    if first:
                        pe.wait_ge(o_v_ready, 1)
                    else:
                        pe.wait_ge(m_ready, 4 * h + 2)
                    project(g0, 0, bank[gate_banks[0]][:])
                    pe.wait_ge(o_v_ready, 4 * h + 4)
                    pe.wait_ge(m_ready, 4 * h + 4)
                    for c, yb in enumerate((5, 6, 7, 0)):
                        for kb in range(TB):
                            last = mm3(bank[yb][:, kb * P:T], part(rv_hi, rv_lo, kb, slice(c * P, (c + 1) * P)),
                                       part(m_hi, m_lo, slice(REST_AT[kb], REST_AT[kb] + REST[kb])),
                                       kb == 0, kb == TB - 1)
                        last.then_inc(y_full, 1)
                    project(g0 + 1, 1, bank[gate_banks[1]][:])
                    pe.wait_ge(gn_sum, 3 * h + 3)
                    token_means(bank[3], acc_sum, cst("mean_dv")).then_inc(gn_stats.sums, 1)
                    pe.wait_ge(gn_sumsq, 3 * h + 3)
                    token_means(bank[2], acc_sq, cst("mean_dv")).then_inc(gn_stats.squares, 1)
                    pe.wait_ge(sg_done, 4 * h + 1)

                    def norm_stages(c):
                        if c == 1:
                            turn_parts(parts_mean, gn_stats.mean_parts, h + 1, gn_stats.mean_turned, bank[3])
                        if c == 3:
                            spread(gn_stats.mean_row, h + 1, row_mean, gn_stats.mean_full, bank[3])
                        if c == 6:
                            rstd_turn(gn_stats, h + 1, 2)
                        if c == DC:
                            rstd_spread(gn_stats, h + 1, 2)

                    project(g0 + 2, 2, bank[gate_banks[0]][:], between=norm_stages)
                    pe.wait_ge(sg_done, 4 * h + 2)
                    project(g0 + 3, 3, bank[gate_banks[1]][:])

                head(0, b)
                with pe.Fori(1, HEADS) as h:
                    head(h, 16 * h + (b - 4))
                pe.wait_ge(y_squared, 4 * HEADS)
                pe.wait_ge(sg_done, 4 * HEADS)
                for wu in range(2):
                    unit(b + 60 + wu)
                for c in range(2):
                    pe.wait_ge(y_ready, 4 * (HEADS - 1) + c + 1)
                    for wu in range(2):
                        for o in range(2):
                            share(wu, o, c, 3)
                for wu in range(2):
                    for o in range(2):
                        for c in (2, 3):
                            pe.wait_ge(y_ready, 4 * (HEADS - 1) + c + 1)
                            share(wu, o, c, 3)
                for a, tokens in enumerate(HALVES):
                    for k in range(4):
                        wu, o = 2 + k // 2, k % 2
                        if a == 0:
                            if o == 0:
                                unit(b + 60 + wu)
                            if k < 3:
                                pe.wait_ge(z_full, Z_AT[ODD_LN] + k + 2)
                        for c in range(4):
                            if a == 1:
                                b_block(ODD_LN, 4 * k + c)
                            last = mm3(bank[A_BANKS[ODD_LN][k] if a == 0 else k][:, tokens], w(wu, 4 * o + c),
                                       part(y_hi, y_lo, c, tokens), c == 0, c == 3)
                        last.then_inc(w_used if a == 1 and o else half_full, 1)

            ffn_in(0)
            ffn_out(0)
            even()
            ffn_in(1)
            ffn_out(1)
            ffn_in(2)
            ffn_out(2)
            odd()
            ffn_in(3)
            ffn_out(3)
            for stage in range(6):
                norm_stage(LAST_LN, 1, stage)


def _weight_stream(ffn_w_in, ffn_w_out, even_w_in, even_w_out, odd_w_in, odd_w_out):
    out = np.zeros((UNITS, P, UB, P), np.float32)
    at = [0]

    def put(blocks):
        out[at[0], :, :len(blocks)] = blocks.transpose(1, 0, 2)
        at[0] += 1

    def columns(wt, c):
        put(wt[:, c:c + P].reshape(DC, P, P))

    def values(wt, c):
        for k in range(RING):
            put(wt[2 * k * P:(2 * k + 2) * P, c:c + T].reshape(2, P, 4, P).transpose(0, 2, 1, 3).reshape(8, P, P))

    def ffn(w_in, w_out):
        for j in range(FC):
            columns(w_in, j * P)
            columns(w_in, FF + j * P)
        for oc in range(DC):
            rows = w_out[:, oc * P:(oc + 1) * P].reshape(FC, P, P)
            for k in range(OUT_UNITS):
                put(rows[UB * k:UB * (k + 1)])

    def even(w_in, w_out):
        for t in range(4):
            columns(w_in, t * P)
            columns(w_in, 512 + t * P)
        values(w_in, 1024)
        for i in range(4):
            for f in (2048, 2560, 1536):
                columns(w_in, f + i * P)
        for oc in range(DC):
            rows = w_out[:, oc * P:(oc + 1) * P].reshape(DC, P, P)
            put(np.concatenate([rows[4:], rows[:4]]))

    def odd(w_in, w_out):
        def share(h):
            rows = w_out[h * T:(h + 1) * T].reshape(4, P, DC, P)
            for wu in range(4):
                put(rows[:, :, 2 * wu:2 * wu + 2].transpose(2, 0, 1, 3).reshape(8, P, P))

        for h in range(HEADS):
            for c in (0, P, D, D + P):
                columns(w_in, c + 256 * h)
            if h:
                share(h - 1)
            values(w_in, 2 * D + T * h)
            for c in range(4):
                columns(w_in, 4 * D + T * h + c * P)
        share(HEADS - 1)

    ffn(ffn_w_in[0, 0], ffn_w_out[0, 0])
    even(even_w_in[0], even_w_out[0])
    ffn(ffn_w_in[0, 1], ffn_w_out[0, 1])
    ffn(ffn_w_in[1, 0], ffn_w_out[1, 0])
    odd(odd_w_in[0], odd_w_out[0])
    ffn(ffn_w_in[1, 1], ffn_w_out[1, 1])
    return out.reshape(UNITS, P, UB * P)


def _rope(half, theta, n_rot):
    inv = np.exp(np.float32(-math.log(theta)) * np.arange(half, dtype=np.float32) * np.float32(2.0 / n_rot))
    ang = inv[:, None].astype(np.float32) * np.arange(T, dtype=np.float32)[None, :]
    return np.cos(ang).astype(np.float32), np.sin(ang).astype(np.float32)


def _tables():
    c, s = _rope(8, 500000.0, 16)
    even = np.zeros((P, 4, T), np.float32)
    even[:, 2] = 1.0
    swap = np.zeros((P, P), np.float32)
    for head in (0, 64):
        even[head:head + 8, 2], even[head + 8:head + 16, 2] = c, c
        even[head:head + 8, 3], even[head + 8:head + 16, 3] = -s, s
        for m in range(8):
            swap[head + m, head + 8 + m] = swap[head + 8 + m, head + m] = 1.0
    even[:, 0:2] = even[:, 2:4] * np.float32(ATTN_SCALE)
    rows = np.zeros((P, TB, P), np.float32)
    for b in range(TB):
        rows[[b, b + 4], b] = 1.0
    c, s = _rope(128, 10000.0, 256)
    odd = np.stack([c, s], 1)
    rel = np.arange(T)[None, :] - np.arange(P)[:, None]
    decay = np.zeros((P, HEADS, T), np.float32)
    for h in range(HEADS):
        decay[:, h] = np.where(rel >= 0, np.exp(np.log1p(-2.0 ** (-5 - h)) * np.maximum(rel, 0)), 0.0) * KEY_SCALE
    mask = np.where(np.arange(P)[None, :] <= np.arange(P)[:, None], 0.0, MASKED).astype(np.float32)
    return even, odd, decay, swap, mask, rows.reshape(P, T)


def kernel(x, ln_g, ln_b, ffn_w_in, ffn_w_out, even_w_in, even_w_out, diff_lambda, diff_norm_g, conv_w,
           odd_w_in, odd_w_out, ret_norm_g):
    import concourse.bacc as bacc
    from concourse.bass_utils import run_bass_kernel_spmd

    even, odd, decay, swap, mask, rows = _tables()
    packed = {
        "ident": np.eye(P), "mean_d": np.full((P, 2), 1.0 / D), "mean_dv": np.full((P, 2), 1.0 / T),
        "mean_rms": np.full((P, 2), 1.0 / P), "swap": swap, "mask": mask, "rows": rows,
        "ln_g": np.asarray(ln_g).reshape(6 * DC, P).T, "ln_b": np.asarray(ln_b).reshape(6 * DC, P).T,
        "conv_w": np.asarray(conv_w).reshape(12, P).T, "norm_g": np.asarray(diff_norm_g).reshape(P, 1),
        "ret_g": np.asarray(ret_norm_g).reshape(16, P).T,
        "lam": np.broadcast_to(np.asarray(diff_lambda).reshape(1, 256), (P, 256)),
    }
    const = np.concatenate([np.asarray(packed[name], np.float32) for name in CONST], 1)
    arrays = {
        "x_t": np.ascontiguousarray(np.asarray(x)[0].T.reshape(DC, P, T)),
        "stream": _weight_stream(*(np.asarray(a) for a in (ffn_w_in, ffn_w_out, even_w_in, even_w_out,
                                                           odd_w_in, odd_w_out))),
        "const": np.ascontiguousarray(const), "rope_even": even, "rope_odd": odd, "decay": decay,
    }
    nc = bacc.Bacc("TRN2", target_bir_lowering=False, num_devices=1)
    args = [nc.dram_tensor(f"in_{n}", a.shape, mybir.dt.from_np(a.dtype), kind="ExternalInput").ap()
            for n, a in arrays.items()]
    out = nc.dram_tensor("out_t", (DC, P, T), F32, kind="ExternalOutput").ap()
    trunk(nc, *args, out)
    r = run_bass_kernel_spmd(nc, [{f"in_{n}": a for n, a in arrays.items()}], core_ids=[0])
    got = np.asarray(r.results[0]["out_t"])
    return np.ascontiguousarray(got.reshape(D, T).T).reshape(1, T, D)
```
